# Optimizing a Trainium2 kernel written in Bass

```python
import math
import jax, jax.numpy as jnp
from jax import lax
import numpy as np

D_MODEL = 1024
BATCH = 1
SEQ = 512
DEPTH = 1

HEAD_DIM = 64
N_BRANCHES = 4
BRANCH_WIDTH = 256

RWKV_HEADS = 4
RWKV_WIDTH = RWKV_HEADS * HEAD_DIM
RWKV_DECAY_RANK = 64
RWKV_ICL_RANK = 64
RWKV_GATE_RANK = 128
RWKV_DECAY_SCALE = 0.606531
RWKV_LN_EPS = 64e-5
RWKV_COLS = 3 * RWKV_WIDTH + RWKV_DECAY_RANK + RWKV_ICL_RANK + RWKV_GATE_RANK

DIL_PATTERNS = ((128, 1), (512, 4), (2048, 16))
DIL_GROUPS = 3
DIL_HEADS_PER_GROUP = 4
DIL_HEADS = DIL_GROUPS * DIL_HEADS_PER_GROUP
DIL_QKV = DIL_HEADS * HEAD_DIM
DIL_COLS = 3 * DIL_QKV

DIFF_HEADS = 4
DIFF_QK_DIM = 32
DIFF_V_DIM = 2 * DIFF_QK_DIM
DIFF_Q_COLS = DIFF_HEADS * 2 * DIFF_QK_DIM
DIFF_V_COLS = DIFF_HEADS * DIFF_V_DIM
DIFF_COLS = 2 * DIFF_Q_COLS + DIFF_V_COLS
DIFF_QBLOCK = 128
DIFF_SUBLN_EPS = 1e-5

CONV_CHANNELS = 256
CONV_WIDTH = 31
CONV_COLS = 2 * CONV_CHANNELS
CONV_LN_EPS = 1e-5

GATE_COLS = N_BRANCHES * D_MODEL
IN_COLS = RWKV_COLS + DIL_COLS + DIFF_COLS + CONV_COLS + GATE_COLS

D_FF = ((8 * D_MODEL + 3 * 256 - 1) // (3 * 256)) * 256

NORM_EPS = 1e-6
NEG_INF = -1e30


def _split(t, sizes):
    out, start = [], 0
    for n in sizes:
        out.append(t[..., start:start + n])
        start += n
    return out

def rms_norm(x, gain, eps=NORM_EPS):
    xf = x.astype(jnp.float32)
    y = xf * lax.rsqrt(jnp.mean(xf * xf, axis=-1, keepdims=True) + eps)
    return (y * gain.astype(jnp.float32)).astype(x.dtype)

def layer_norm_f32(x, gain, bias, eps):
    xf = x.astype(jnp.float32)
    mu = jnp.mean(xf, axis=-1, keepdims=True)
    var = jnp.mean(jnp.square(xf - mu), axis=-1, keepdims=True)
    return (xf - mu) * lax.rsqrt(var + eps) * gain.astype(jnp.float32) + bias.astype(jnp.float32)

def alibi_slopes(n):
    return jnp.asarray(2.0 ** (-8.0 * np.arange(1, n + 1) / n), dtype=jnp.float32)

def rwkv7_time_mix(p, mu, w0, w_up, a0, a_up, g_up, k_k, k_a, r_k, ln_g, ln_b):
    B, S, _ = p.shape
    H, N = RWKV_HEADS, HEAD_DIM
    f32 = jnp.float32
    p_prev = jnp.pad(p[:, :-1], ((0, 0), (1, 0), (0, 0)))
    p = p + (p_prev - p) * mu
    r, k, v, zw, za, zg = _split(p, (RWKV_WIDTH, RWKV_WIDTH, RWKV_WIDTH, RWKV_DECAY_RANK, RWKV_ICL_RANK, RWKV_GATE_RANK))
    log_w = -RWKV_DECAY_SCALE * jax.nn.sigmoid((w0 + jnp.tanh(zw) @ w_up).astype(f32))
    a = jax.nn.sigmoid((a0 + za @ a_up).astype(f32))
    g = (jax.nn.sigmoid(zg) @ g_up).astype(f32)
    heads = lambda t: t.astype(f32).reshape(B, S, H, N)
    r, k, v, log_w, a = heads(r), heads(k), heads(v), heads(log_w), heads(a)
    kk = k * k_k.astype(f32).reshape(H, N)
    kk = kk / jnp.maximum(jnp.sqrt(jnp.sum(kk * kk, axis=-1, keepdims=True)), 1e-12)
    k = k * (1.0 + (a - 1.0) * k_a.astype(f32).reshape(H, N))
    w = jnp.exp(log_w)

    def step(state, inp):
        r_t, w_t, k_t, v_t, kk_t, a_t = inp
        sa = jnp.einsum('bhvk,bhk->bhv', state, -kk_t)
        state = (state * w_t[:, :, None, :]
                 + sa[..., None] * (kk_t * a_t)[:, :, None, :]
                 + v_t[..., None] * k_t[:, :, None, :])
        return state, jnp.einsum('bhvk,bhk->bhv', state, r_t)

    xs = tuple(t.transpose(1, 0, 2, 3) for t in (r, w, k, v, kk, a))
    _, o = lax.scan(step, jnp.zeros((B, H, N, N), f32), xs)
    o = o.transpose(1, 0, 2, 3)
    o = layer_norm_f32(o, ln_g.reshape(H, N), ln_b.reshape(H, N), RWKV_LN_EPS)
    o = o + jnp.sum(r * k * r_k.astype(f32), axis=-1, keepdims=True) * v
    return (o.reshape(B, S, H * N) * g).astype(p.dtype)

def _dilated_group(q, k, v, window, dilation, slopes):
    B, S, H, Dh = q.shape
    n = window // dilation
    L = S // dilation
    nb = -(-L // n)
    Lp = nb * n

    def to_sub(t):
        t = t.reshape(B, L, dilation, H, Dh).transpose(0, 2, 1, 3, 4)
        return jnp.pad(t, ((0, 0), (0, 0), (0, Lp - L), (0, 0), (0, 0)))

    def band(t):
        t = jnp.pad(t, ((0, 0), (0, 0), (n, 0), (0, 0), (0, 0))).reshape(B, dilation, nb + 1, n, H, Dh)
        return jnp.concatenate([t[:, :, :-1], t[:, :, 1:]], axis=3)

    qb = to_sub(q).reshape(B, dilation, nb, n, H, Dh)
    kb, vb = band(to_sub(k)), band(to_sub(v))
    s = jnp.einsum('brcqhd,brckhd->brchqk', qb, kb, preferred_element_type=jnp.float32) * (Dh ** -0.5)
    kj = jnp.arange(2 * n)
    rel = n + jnp.arange(n)[:, None] - kj[None, :]
    front_pad = (jnp.arange(nb)[:, None, None] == 0) & (kj[None, None, :] < n)
    valid = ((rel >= 0) & (rel <= n))[None] & ~front_pad
    bias = -slopes[:, None, None] * (dilation * rel).astype(jnp.float32)[None]
    s = jnp.where(valid[None, None, :, None], s + bias[None, None, None], NEG_INF)
    lse = jax.nn.logsumexp(s, axis=-1)
    pr = jnp.exp(s - lse[..., None])
    o = jnp.einsum('brchqk,brckhd->brcqhd', pr, vb.astype(jnp.float32))
    o = o.reshape(B, dilation, Lp, H, Dh)[:, :, :L].transpose(0, 2, 1, 3, 4).reshape(B, S, H, Dh)
    lse = lse.transpose(0, 1, 2, 4, 3).reshape(B, dilation, Lp, H)[:, :, :L].transpose(0, 2, 1, 3).reshape(B, S, H)
    return o, lse

def dilated_attention(q, k, v, slopes):
    outs, lses = [], []
    for gi, (window, dilation) in enumerate(DIL_PATTERNS):
        o, lse = _dilated_group(q[:, :, gi], k[:, :, gi], v[:, :, gi], window, dilation, slopes[gi])
        outs.append(o)
        lses.append(lse)
    wts = jax.nn.softmax(jnp.stack(lses, axis=0), axis=0)
    return jnp.sum(wts[..., None] * jnp.stack(outs, axis=0), axis=0)

def diff_attention(q, k, v, lam, slopes, subln_g, lambda_init):
    B, S, H, _, dq = q.shape
    nq = S // DIFF_QBLOCK
    qb = q.reshape(B, nq, DIFF_QBLOCK, H, 2, dq).transpose(1, 0, 2, 3, 4, 5)
    kpos = jnp.arange(S)
    vf = v.astype(jnp.float32)

    def block(args):
        c, q_blk = args
        s = jnp.einsum('bqhmd,bkhmd->bhmqk', q_blk, k, preferred_element_type=jnp.float32) * (dq ** -0.5)
        rel = (c * DIFF_QBLOCK + jnp.arange(DIFF_QBLOCK))[:, None] - kpos[None, :]
        s = s - slopes[:, None, None, None] * rel.astype(jnp.float32)
        s = jnp.where(rel >= 0, s, NEG_INF)
        pr = jax.nn.softmax(s, axis=-1)
        att = pr[:, :, 0] - lam * pr[:, :, 1]
        return jnp.einsum('bhqk,bkhd->bqhd', att, vf)

    o = lax.map(block, (jnp.arange(nq), qb))
    o = o.transpose(1, 0, 2, 3, 4).reshape(B, S, H, -1)
    o = o * lax.rsqrt(jnp.mean(o * o, axis=-1, keepdims=True) + DIFF_SUBLN_EPS) * subln_g.astype(jnp.float32)
    return (o * (1.0 - lambda_init)).reshape(B, S, -1).astype(q.dtype)

def conformer_conv(p, dw_w, dw_b, ln_g, ln_b):
    a, b = _split(p, (CONV_CHANNELS, CONV_CHANNELS))
    u = a * jax.nn.sigmoid(b)
    y = lax.conv_general_dilated(u, dw_w, window_strides=(1,), padding=((CONV_WIDTH - 1, 0),),
                                 dimension_numbers=('NWC', 'WIO', 'NWC'),
                                 feature_group_count=CONV_CHANNELS) + dw_b
    y = layer_norm_f32(y, ln_g, ln_b, CONV_LN_EPS)
    return jax.nn.silu(y).astype(p.dtype)

def first_inputs(seed: int = 0) -> dict:
    key = jax.random.key(seed)
    ks = iter(jax.random.split(key, 40))
    L, D = DEPTH, D_MODEL
    nrm = lambda shape, scale: scale * jax.random.normal(next(ks), shape, jnp.float32)
    gain = lambda shape: 1.0 + nrm(shape, 0.02)
    return {
        'x': nrm((BATCH, SEQ, D), 1.0),
        'norm_mix_pre': gain((L, D)),
        'norm_mix_post': gain((L, D)),
        'norm_ffn_pre': gain((L, D)),
        'norm_ffn_post': gain((L, D)),
        'w_in': nrm((L, D, IN_COLS), D ** -0.5),
        'gate_bias': nrm((L, GATE_COLS), 0.01),
        'rwkv_mu': jax.random.uniform(next(ks), (L, RWKV_COLS), jnp.float32),
        'rwkv_w0': nrm((L, RWKV_WIDTH), 1.0),
        'rwkv_w_up': nrm((L, RWKV_DECAY_RANK, RWKV_WIDTH), 0.5 * RWKV_DECAY_RANK ** -0.5),
        'rwkv_a0': nrm((L, RWKV_WIDTH), 0.1),
        'rwkv_a_up': nrm((L, RWKV_ICL_RANK, RWKV_WIDTH), 0.5 * RWKV_ICL_RANK ** -0.5),
        'rwkv_g_up': nrm((L, RWKV_GATE_RANK, RWKV_WIDTH), RWKV_GATE_RANK ** -0.5),
        'rwkv_k_k': 0.85 + nrm((L, RWKV_WIDTH), 0.02),
        'rwkv_k_a': gain((L, RWKV_WIDTH)),
        'rwkv_r_k': nrm((L, RWKV_HEADS, HEAD_DIM), 0.1),
        'rwkv_ln_g': gain((L, RWKV_WIDTH)),
        'rwkv_ln_b': nrm((L, RWKV_WIDTH), 0.01),
        'diff_lam_q1': nrm((L, DIFF_QK_DIM), 0.1),
        'diff_lam_k1': nrm((L, DIFF_QK_DIM), 0.1),
        'diff_lam_q2': nrm((L, DIFF_QK_DIM), 0.1),
        'diff_lam_k2': nrm((L, DIFF_QK_DIM), 0.1),
        'diff_subln_g': gain((L, DIFF_V_DIM)),
        'conv_dw_w': nrm((L, CONV_WIDTH, 1, CONV_CHANNELS), CONV_WIDTH ** -0.5),
        'conv_dw_b': nrm((L, CONV_CHANNELS), 0.01),
        'conv_ln_g': gain((L, CONV_CHANNELS)),
        'conv_ln_b': nrm((L, CONV_CHANNELS), 0.01),
        'w_branch': nrm((L, N_BRANCHES, BRANCH_WIDTH, D), BRANCH_WIDTH ** -0.5),
        'w_out': nrm((L, D, D), D ** -0.5),
        'ffn_w_gate': nrm((L, D, D_FF), D ** -0.5),
        'ffn_w_up': nrm((L, D, D_FF), D ** -0.5),
        'ffn_w_down': nrm((L, D_FF, D), D_FF ** -0.5),
    }

def first_block(x, norm_mix_pre, norm_mix_post, norm_ffn_pre, norm_ffn_post, w_in, gate_bias,
              rwkv_mu, rwkv_w0, rwkv_w_up, rwkv_a0, rwkv_a_up, rwkv_g_up, rwkv_k_k, rwkv_k_a,
              rwkv_r_k, rwkv_ln_g, rwkv_ln_b, diff_lam_q1, diff_lam_k1, diff_lam_q2, diff_lam_k2,
              diff_subln_g, conv_dw_w, conv_dw_b, conv_ln_g, conv_ln_b, w_branch, w_out,
              ffn_w_gate, ffn_w_up, ffn_w_down):
    B, S, D = x.shape
    dil_slopes = alibi_slopes(DIL_HEADS).reshape(DIL_GROUPS, DIL_HEADS_PER_GROUP)
    diff_slopes = alibi_slopes(DIFF_HEADS)
    for l in range(DEPTH):
        h = rms_norm(x, norm_mix_pre[l])
        proj = h @ w_in[l]
        p_rwkv, p_dil, p_diff, p_conv, p_gate = _split(proj, (RWKV_COLS, DIL_COLS, DIFF_COLS, CONV_COLS, GATE_COLS))

        y_a = rwkv7_time_mix(p_rwkv, rwkv_mu[l], rwkv_w0[l], rwkv_w_up[l], rwkv_a0[l], rwkv_a_up[l],
                             rwkv_g_up[l], rwkv_k_k[l], rwkv_k_a[l], rwkv_r_k[l], rwkv_ln_g[l], rwkv_ln_b[l])

        dq, dk, dv = _split(p_dil, (DIL_QKV, DIL_QKV, DIL_QKV))
        grp = lambda t: t.reshape(B, S, DIL_GROUPS, DIL_HEADS_PER_GROUP, HEAD_DIM)
        y_b = dilated_attention(grp(dq), grp(dk), grp(dv), dil_slopes).reshape(B, S, BRANCH_WIDTH).astype(x.dtype)

        cq, ck, cv = _split(p_diff, (DIFF_Q_COLS, DIFF_Q_COLS, DIFF_V_COLS))
        lambda_init = 0.8 - 0.6 * math.exp(-0.3 * l)
        lam = (jnp.exp(jnp.sum(diff_lam_q1[l].astype(jnp.float32) * diff_lam_k1[l].astype(jnp.float32)))
               - jnp.exp(jnp.sum(diff_lam_q2[l].astype(jnp.float32) * diff_lam_k2[l].astype(jnp.float32)))
               + lambda_init)
        y_c = diff_attention(cq.reshape(B, S, DIFF_HEADS, 2, DIFF_QK_DIM),
                             ck.reshape(B, S, DIFF_HEADS, 2, DIFF_QK_DIM),
                             cv.reshape(B, S, DIFF_HEADS, DIFF_V_DIM),
                             lam, diff_slopes, diff_subln_g[l], lambda_init)

        y_d = conformer_conv(p_conv, conv_dw_w[l], conv_dw_b[l], conv_ln_g[l], conv_ln_b[l])

        ys = jnp.stack([y_a, y_b, y_c, y_d], axis=2)
        gates = jax.nn.sigmoid(p_gate + gate_bias[l]).reshape(B, S, N_BRANCHES, D)
        merged = jnp.einsum('bsnd,bsnd->bsd', gates, jnp.einsum('bsnc,ncd->bsnd', ys, w_branch[l]))
        x = x + rms_norm(merged @ w_out[l], norm_mix_post[l])

        h = rms_norm(x, norm_ffn_pre[l])
        f = (jax.nn.silu(h @ ffn_w_gate[l]) * (h @ ffn_w_up[l])) @ ffn_w_down[l]
        x = x + rms_norm(f, norm_ffn_post[l])
    return x


_first_inputs = first_inputs


def first_inputs(seed=0):
    import zlib

    import numpy as np

    out = dict(_first_inputs(seed))
    spreads = {}
    factors = {'norm_mix_post': 3.367,
     'norm_ffn_pre': 3.626,
     'norm_ffn_post': 4.998,
     'gate_bias': 8.0,
     'rwkv_a0': 2.821,
     'rwkv_k_k': 8.0,
     'rwkv_k_a': 6.723,
     'rwkv_ln_g': 7.135,
     'rwkv_ln_b': 8.0,
     'diff_lam_k1': 3.642,
     'diff_lam_q2': 3.337,
     'diff_lam_k2': 4.829,
     'diff_subln_g': 6.277,
     'conv_dw_b': 6.35,
     'conv_ln_g': 6.15,
     'conv_ln_b': 8.0}
    for name, (base, spread) in spreads.items():
        noise = np.random.default_rng([zlib.crc32(name.encode()), seed]).standard_normal(out[name].shape)
        drawn = base * np.exp(spread * noise) if base else spread * noise
        out[name] = __import__('jax').numpy.asarray(drawn.astype(out[name].dtype))
    for name, factor in factors.items():
        out[name] = (out[name] * factor).astype(out[name].dtype)
    return out


_narrow_inputs = first_inputs


def first_inputs(seed=0):

    out = dict(_narrow_inputs(seed))
    wider = {'norm_ffn_post': 3.94,
     'rwkv_k_k': 12.0,
     'rwkv_k_a': 3.35,
     'rwkv_ln_g': 4.78,
     'rwkv_ln_b': 10.16,
     'diff_subln_g': 4.78,
     'conv_ln_g': 4.89,
     'conv_ln_b': 7.51}
    for name, times in wider.items():
        mean = out[name].mean()
        out[name] = (mean + times * (out[name] - mean)).astype(out[name].dtype)
    return out


DEPTH_2 = 2

N_META = 16
D_RNN = D_MODEL
LRU_HEADS = 16
LRU_HEAD_DIM = D_RNN // LRU_HEADS
CONV_A = 4
LRU_C = 8.0
D_CONV = D_MODEL
CONV_B = 3
N_GROUPS = 4
EXPERTS_PER_GROUP = 8
N_EXPERTS = N_GROUPS * EXPERTS_PER_GROUP
TOP_K = 2
D_EXPERT = D_MODEL // 2
BLK = 128
N_MIXERS = 2
N_A_LAYERS = (DEPTH_2 + 1) // 2
N_B_LAYERS = DEPTH_2 // 2
ALPHA = (2.0 * DEPTH_2) ** 0.25
BETA = (8.0 * DEPTH_2) ** -0.25
LN_EPS = 1e-5


def layer_norm(x, g, b):
    xf = x.astype(jnp.float32)
    mu = jnp.mean(xf, axis=-1, keepdims=True)
    var = jnp.mean(jnp.square(xf - mu), axis=-1, keepdims=True)
    y = (xf - mu) * lax.rsqrt(var + LN_EPS) * g.astype(jnp.float32) + b.astype(jnp.float32)
    return y.astype(x.dtype)

def causal_depthwise_conv(x, w):
    K, C = w.shape
    return lax.conv_general_dilated(
        x, w[:, None, :].astype(x.dtype), window_strides=(1,), padding=[(K - 1, 0)],
        dimension_numbers=("NWC", "WIO", "NWC"), feature_group_count=C)

def _linear_recurrence_combine(c1, c2):
    a1, b1 = c1
    a2, b2 = c2
    return a1 * a2, a2 * b1 + b2

def rglru_mixer(h, w_in, conv_w, conv_b, w_a, b_a, w_i, b_i, lam, w_out):
    Bsz, S, _ = h.shape
    u = h @ w_in
    y_br = jax.nn.gelu(u[..., :D_RNN])
    xc = causal_depthwise_conv(u[..., D_RNN:], conv_w) + conv_b
    xh = xc.reshape(Bsz, S, LRU_HEADS, LRU_HEAD_DIM)
    r = jax.nn.sigmoid(jnp.einsum("bshd,hde->bshe", xh, w_a).reshape(Bsz, S, D_RNN) + b_a)
    gi = jax.nn.sigmoid(jnp.einsum("bshd,hde->bshe", xh, w_i).reshape(Bsz, S, D_RNN) + b_i)
    log_a = -LRU_C * r.astype(jnp.float32) * jax.nn.softplus(-lam.astype(jnp.float32))
    a = jnp.exp(log_a)
    mult = jnp.sqrt(-jnp.expm1(2.0 * log_a))
    b = mult * (gi * xc).astype(jnp.float32)
    _, hs = lax.associative_scan(_linear_recurrence_combine, (a, b), axis=1)
    return (hs.astype(h.dtype) * y_br) @ w_out

def shortconv_mixer(h, w_in, conv_w, w_out):
    u = h @ w_in
    bg = u[..., :D_CONV]
    cg = u[..., D_CONV:2 * D_CONV]
    v = u[..., 2 * D_CONV:]
    zc = causal_depthwise_conv(cg * v, conv_w)
    return (bg * zc) @ w_out

def hierarchical_moe(h, w_group, b_group, w_expert, b_expert, w_gate, w_up, w_down):
    Bsz, S, D = h.shape
    x2 = h.reshape(Bsz * S, D)
    T = x2.shape[0]
    xf = x2.astype(jnp.float32)
    glog = xf @ w_group.astype(jnp.float32) + b_group.astype(jnp.float32)
    gprob = jax.nn.softmax(glog, axis=-1)
    g = jnp.argmax(glog, axis=-1)
    pg = jnp.take_along_axis(gprob, g[:, None], axis=1)
    elog = (xf @ w_expert.astype(jnp.float32)).reshape(T, N_GROUPS, EXPERTS_PER_GROUP) + b_expert.astype(jnp.float32)
    elog_g = jnp.take_along_axis(elog, g[:, None, None], axis=1)[:, 0]
    vals, loc = lax.top_k(elog_g, TOP_K)
    gates = pg * jax.nn.softmax(vals, axis=-1)
    eid = g[:, None] * EXPERTS_PER_GROUP + loc
    A = T * TOP_K
    eid_f = eid.reshape(-1)
    tok_f = jnp.repeat(jnp.arange(T, dtype=jnp.int32), TOP_K)
    gate_f = gates.reshape(-1)
    order = jnp.argsort(eid_f)
    eid_s = eid_f[order]
    tok_s = tok_f[order]
    gate_s = gate_f[order]
    counts = jnp.bincount(eid_f, length=N_EXPERTS)
    start = jnp.cumsum(counts) - counts
    padded = (counts + BLK - 1) // BLK * BLK
    pend = jnp.cumsum(padded)
    pstart = pend - padded
    rank = jnp.arange(A, dtype=jnp.int32) - start[eid_s]
    dest = pstart[eid_s] + rank
    n_blocks = (A + N_EXPERTS * (BLK - 1) + BLK - 1) // BLK
    P = n_blocks * BLK
    slot_tok = jnp.full((P,), T, dtype=jnp.int32).at[dest].set(tok_s)
    slot_gate = jnp.zeros((P,), jnp.float32).at[dest].set(gate_s)
    block_expert = jnp.clip(jnp.searchsorted(pend, jnp.arange(n_blocks) * BLK, side="right"), 0, N_EXPERTS - 1)
    xpad = jnp.concatenate([x2, jnp.zeros((1, D), x2.dtype)], axis=0)
    xs = xpad[slot_tok].reshape(n_blocks, BLK, D)

    def expert_block(args):
        xb, e = args
        hb = jax.nn.silu(xb @ w_gate[e]) * (xb @ w_up[e])
        return hb @ w_down[e]

    ys = lax.map(expert_block, (xs, block_expert)).reshape(P, D)
    y = jnp.zeros((T + 1, D), x2.dtype).at[slot_tok].add(ys * slot_gate[:, None].astype(ys.dtype))
    return y[:T].reshape(Bsz, S, D)

def second_inputs(seed: int = 0) -> dict:
    key = jax.random.key(seed)
    ks = jax.random.split(key, 24)

    def nrm(k, shape, scale):
        return jax.random.normal(k, shape, jnp.float32) * scale

    u = jax.random.uniform(ks[10], (N_A_LAYERS, D_RNN), jnp.float32, 0.9, 0.999)
    a0 = u ** (1.0 / LRU_C)
    lru_lambda = jnp.log(a0) - jnp.log1p(-a0)
    return {
        "x": nrm(ks[0], (BATCH, SEQ, D_MODEL), 1.0),
        "meta_tokens": nrm(ks[1], (N_META, D_MODEL), 1.0),
        "lru_w_in": nrm(ks[2], (N_A_LAYERS, D_MODEL, 2 * D_RNN), D_MODEL ** -0.5),
        "lru_conv_w": nrm(ks[3], (N_A_LAYERS, CONV_A, D_RNN), CONV_A ** -0.5),
        "lru_conv_b": nrm(ks[4], (N_A_LAYERS, D_RNN), 0.01),
        "lru_w_a": nrm(ks[5], (N_A_LAYERS, LRU_HEADS, LRU_HEAD_DIM, LRU_HEAD_DIM), LRU_HEAD_DIM ** -0.5),
        "lru_b_a": nrm(ks[6], (N_A_LAYERS, D_RNN), 0.01),
        "lru_w_i": nrm(ks[7], (N_A_LAYERS, LRU_HEADS, LRU_HEAD_DIM, LRU_HEAD_DIM), LRU_HEAD_DIM ** -0.5),
        "lru_b_i": nrm(ks[8], (N_A_LAYERS, D_RNN), 0.01),
        "lru_lambda": lru_lambda,
        "lru_w_out": nrm(ks[9], (N_A_LAYERS, D_RNN, D_MODEL), BETA * D_RNN ** -0.5),
        "sc_w_in": nrm(ks[11], (N_B_LAYERS, D_MODEL, 3 * D_CONV), D_MODEL ** -0.5),
        "sc_conv_w": nrm(ks[12], (N_B_LAYERS, CONV_B, D_CONV), CONV_B ** -0.5),
        "sc_w_out": nrm(ks[13], (N_B_LAYERS, D_CONV, D_MODEL), BETA * D_CONV ** -0.5),
        "moe_w_group": nrm(ks[14], (DEPTH_2, D_MODEL, N_GROUPS), D_MODEL ** -0.5),
        "moe_b_group": nrm(ks[15], (DEPTH_2, N_GROUPS), 0.01),
        "moe_w_expert": nrm(ks[16], (DEPTH_2, D_MODEL, N_EXPERTS), D_MODEL ** -0.5),
        "moe_b_expert": nrm(ks[17], (DEPTH_2, N_GROUPS, EXPERTS_PER_GROUP), 0.01),
        "moe_w_gate": nrm(ks[18], (DEPTH_2, N_EXPERTS, D_MODEL, D_EXPERT), D_MODEL ** -0.5),
        "moe_w_up": nrm(ks[19], (DEPTH_2, N_EXPERTS, D_MODEL, D_EXPERT), D_MODEL ** -0.5),
        "moe_w_down": nrm(ks[20], (DEPTH_2, N_EXPERTS, D_EXPERT, D_MODEL), BETA * D_EXPERT ** -0.5),
        "ln_g": 1.0 + nrm(ks[21], (DEPTH_2, 2, D_MODEL), 0.02),
        "ln_b": nrm(ks[22], (DEPTH_2, 2, D_MODEL), 0.02),
    }

def second_block(x, meta_tokens, lru_w_in, lru_conv_w, lru_conv_b, lru_w_a, lru_b_a, lru_w_i, lru_b_i,
              lru_lambda, lru_w_out, sc_w_in, sc_conv_w, sc_w_out, moe_w_group, moe_b_group,
              moe_w_expert, moe_b_expert, moe_w_gate, moe_w_up, moe_w_down, ln_g, ln_b):
    Bsz = x.shape[0]
    meta = jnp.broadcast_to(meta_tokens.astype(x.dtype)[None], (Bsz, N_META, D_MODEL))
    h = jnp.concatenate([meta, x], axis=1)
    for i in range(DEPTH_2):
        j = i // N_MIXERS
        if i % N_MIXERS == 0:
            mixed = rglru_mixer(h, lru_w_in[j], lru_conv_w[j], lru_conv_b[j], lru_w_a[j], lru_b_a[j],
                                lru_w_i[j], lru_b_i[j], lru_lambda[j], lru_w_out[j])
        else:
            mixed = shortconv_mixer(h, sc_w_in[j], sc_conv_w[j], sc_w_out[j])
        h = layer_norm(ALPHA * h + mixed, ln_g[i, 0], ln_b[i, 0])
        ffn = hierarchical_moe(h, moe_w_group[i], moe_b_group[i], moe_w_expert[i], moe_b_expert[i],
                               moe_w_gate[i], moe_w_up[i], moe_w_down[i])
        h = layer_norm(ALPHA * h + ffn, ln_g[i, 1], ln_b[i, 1])
    return h[:, N_META:]


def setup_inputs(seed=0):
    out = dict(first_inputs(seed))
    for name, value in second_inputs(seed + 1).items():
        if name != "x":
            out[name + "_2"] = value
    return out


def reference(
    x, norm_mix_pre, norm_mix_post, norm_ffn_pre, norm_ffn_post, w_in, gate_bias, rwkv_mu,
    rwkv_w0, rwkv_w_up, rwkv_a0, rwkv_a_up, rwkv_g_up, rwkv_k_k, rwkv_k_a, rwkv_r_k, rwkv_ln_g,
    rwkv_ln_b, diff_lam_q1, diff_lam_k1, diff_lam_q2, diff_lam_k2, diff_subln_g, conv_dw_w,
    conv_dw_b, conv_ln_g, conv_ln_b, w_branch, w_out, ffn_w_gate, ffn_w_up, ffn_w_down,
    meta_tokens_2, lru_w_in_2, lru_conv_w_2, lru_conv_b_2, lru_w_a_2, lru_b_a_2, lru_w_i_2,
    lru_b_i_2, lru_lambda_2, lru_w_out_2, sc_w_in_2, sc_conv_w_2, sc_w_out_2, moe_w_group_2,
    moe_b_group_2, moe_w_expert_2, moe_b_expert_2, moe_w_gate_2, moe_w_up_2, moe_w_down_2,
    ln_g_2, ln_b_2,
):
    x = first_block(
        x, norm_mix_pre, norm_mix_post, norm_ffn_pre, norm_ffn_post, w_in, gate_bias, rwkv_mu,
        rwkv_w0, rwkv_w_up, rwkv_a0, rwkv_a_up, rwkv_g_up, rwkv_k_k, rwkv_k_a, rwkv_r_k,
        rwkv_ln_g, rwkv_ln_b, diff_lam_q1, diff_lam_k1, diff_lam_q2, diff_lam_k2, diff_subln_g,
        conv_dw_w, conv_dw_b, conv_ln_g, conv_ln_b, w_branch, w_out, ffn_w_gate, ffn_w_up,
        ffn_w_down,
    )
    return second_block(
        x, meta_tokens_2, lru_w_in_2, lru_conv_w_2, lru_conv_b_2, lru_w_a_2, lru_b_a_2,
        lru_w_i_2, lru_b_i_2, lru_lambda_2, lru_w_out_2, sc_w_in_2, sc_conv_w_2, sc_w_out_2,
        moe_w_group_2, moe_b_group_2, moe_w_expert_2, moe_b_expert_2, moe_w_gate_2, moe_w_up_2,
        moe_w_down_2, ln_g_2, ln_b_2,
    )


_drawn_inputs = setup_inputs


def setup_inputs(seed=0):
    import zlib

    import numpy as np

    out = dict(_drawn_inputs(seed))
    spreads = {}
    factors = {'lru_conv_b_2': 5.144,
     'lru_b_a_2': 33.008,
     'lru_b_i_2': 34.405,
     'moe_b_group_2': 5.477,
     'moe_b_expert_2': 6.169}
    for name, (base, spread) in spreads.items():
        noise = np.random.default_rng([zlib.crc32(name.encode()), seed]).standard_normal(out[name].shape)
        drawn = base * np.exp(spread * noise) if base else spread * noise
        out[name] = __import__('jax').numpy.asarray(drawn.astype(out[name].dtype))
    for name, factor in factors.items():
        out[name] = (out[name] * factor).astype(out[name].dtype)
    return out
```

```python
import numpy as np
import concourse.bass as bass
import concourse.mybir as mybir
from concourse.alu_op_type import AluOpType as ALU
from contextlib import ExitStack

F32 = mybir.dt.float32
I32 = mybir.dt.int32
ACT = mybir.ActivationFunctionType
AX = mybir.AxisListType.X
MUL, ADD, SUB, MAX, MIN = ALU.mult, ALU.add, ALU.subtract, ALU.max, ALU.min
ISEQ, ISGE, ISGT, ISLT = ALU.is_equal, ALU.is_ge, ALU.is_gt, ALU.is_lt

T = 512
D = 1024
NEXP = 32
FF = 2816
CAP = 64
NOVF = 16


class Queue:

    def __init__(self, sem):
        self.sem, self.n, self.items, self.seen = sem, 0, [], {}

    def wait(self, *toks):
        for t in toks:
            if t is None:
                continue
            if isinstance(t, list):
                self.wait(*t)
                continue
            sem, val = t
            if self.seen.get(id(sem), 0) >= val:
                continue
            self.seen[id(sem)] = val
            self.items.append(("wait", sem, val))

    def op(self, fn, *toks):
        self.wait(*toks)
        self.n += 1
        self.items.append(("op", fn, self.sem, 1))
        return self.sem, self.n

    def quiet(self, fn, *toks):
        self.wait(*toks)
        self.items.append(("op", fn, None, 0))

    def dma(self, fn, sem, *toks):
        self.wait(*toks)
        self.items.append(("op", fn, sem, 16))

    def last(self):
        return (self.sem, self.n) if self.n else None

    def emit(self, eng, items=None):
        for it in self.items if items is None else items:
            if it[0] == "wait":
                eng.wait_ge(it[1], it[2])
            elif it[0] == "late":
                for sem, val in it[1]():
                    eng.wait_ge(sem, val)
            elif it[0] == "tok":
                eng.wait_ge(*it[1])
            elif it[0] in ("read", "count"):
                it[1]["v"] = eng.value_load(it[2], min_val=0, max_val=NEXP - 1)
            elif it[0] == "when":
                with eng.If(it[1](eng)):
                    self.emit(eng, it[2])
            else:
                ins = it[1](eng)
                if it[2] is not None:
                    ins.then_inc(it[2], it[3])


class Slots:

    def __init__(self, items):
        self.items, self.free, self.i = items, [None] * len(items), 0

    def take(self):
        k = self.i % len(self.items)
        self.i += 1
        return k, self.items[k], self.free[k]


class DmaSem:

    def __init__(self, sem):
        self.sem, self.n = sem, 0

    def add(self):
        self.n += 16
        return self.sem, self.n
SLOT = 4096
NBIG = 53200


def alibi(n):
    return [float(np.float32(2.0 ** (-8.0 * k / n))) for k in range(1, n + 1)]


def shape_tables():
    q = np.arange(128)[:, None]
    c = np.arange(128)[None, :]
    parts = [("ident", np.eye(128)), ("ones", np.ones((128, 128))), ("zero", np.zeros((128, 128))),
             ("headones", (q // 64) == (c // 64)), ("mean256", np.full((128, 128), 1.0 / 256))]
    for b in range(7):
        w = 1 << b
        parts.append((f"lev{b}", ((q >> (b + 1)) == (c >> (b + 1))) & ((q & w) != 0) & ((c & w) == 0)))
    parts.append(("strict", q < c))
    parts.append(("incl", q <= c))
    parts.append(("headsel", np.concatenate([q < 64, q >= 64], 1)))
    parts.append(("neghalf", np.full((128, 16), -0.5)))
    parts.append(("poshalf", np.full((128, 2), 0.5)))
    parts.append(("eps", np.full((128, 2), 1e-5)))
    parts.append(("eid", np.broadcast_to(np.arange(32), (128, 32))))
    parts.append(("gid", np.broadcast_to(np.arange(8), (128, 8))))
    parts.append(("tok", q + 128 * np.arange(8)[None, :]))
    e = np.arange(32)[None, :]
    parts.append(("hbase", np.broadcast_to((e % 2) * 64 * 32 + e // 2, (128, 32))))
    parts.append(("first16", np.broadcast_to(q < 16, (128, 32))))
    c5 = np.arange(512)[None, :]
    rel = 384 + q - c5
    far = 3e32
    parts.append(("rdf", np.where(rel >= 0, rel, far)))
    parts.append(("rd1", np.where((rel >= 0) & (rel % 4 == 0), rel, far)))
    parts.append(("rd2", np.where((rel >= 0) & (rel % 16 == 0), rel, far)))
    c2 = np.arange(256)[None, :]
    rel = 128 + q - c2
    parts.append(("rd0", np.where((rel >= 0) & (rel <= 128), rel, far)))
    at, cols = {}, 0
    for name, a in parts:
        at[name] = (cols, a.shape[1])
        cols += a.shape[1]
    table = np.concatenate([np.asarray(a, np.float32) for _, a in parts], 1)
    return np.ascontiguousarray(table), at


VECS = [("norm_mix_pre", 8), ("norm_ffn_pre", 8), ("gate_bias", 32), ("rwkv_mu", 8), ("rwkv_w0", 2), ("rwkv_a0", 2),
        ("rwkv_k_k", 2), ("rwkv_k_a", 2), ("rwkv_r_k", 2), ("conv_dw_w", 62), ("conv_dw_b", 2), ("conv_ln_g", 2),
        ("conv_ln_b", 2), ("lru_conv_w_2", 32), ("lru_conv_b_2", 8), ("lru_b_a_2", 8), ("lru_b_i_2", 8),
        ("lru_lambda_2", 8), ("sc_conv_w_2", 24)]
ROWS = [("rwkv_ln_g", 256), ("rwkv_ln_b", 256), ("diff_subln_g", 64), ("diff_lam_q1", 32), ("diff_lam_k1", 32),
        ("diff_lam_q2", 32), ("diff_lam_k2", 32), ("moe_b_group_2", 8), ("moe_b_expert_2", 64)]


def places(spec):
    at, n = {}, 0
    for name, w in spec:
        at[name] = (n, w)
        n += w
    return at, n


VAT, NVEC = places(VECS)
RAT, NROW = places(ROWS)


class Program:
    def __init__(self, nc, ctx, A, out):
        self.nc, self.ctx, self.A, self.out = nc, ctx, A, out
        self.big = ctx.enter_context(nc.sbuf_tensor("big", [128, NBIG], F32))
        self.ps = [ctx.enter_context(nc.psum_tensor(f"ps{k}", [128, 512], F32)) for k in range(8)]
        self.nsem = 0
        self.pe, self.ac, self.dv, self.po, self.sp = (Queue(self.sem(n)) for n in ("pe", "act", "dve", "pool", "sp"))

    def sem(self, name):
        self.nsem += 1
        return self.ctx.enter_context(self.nc.semaphore(f"{name}_{self.nsem}"))

    def tt(self, out, a, b, op, *w):
        return self.dv.op(lambda e: e.tensor_tensor(out, a, b, op), *w)

    def ptt(self, out, a, b, op, *w):
        return self.po.op(lambda e: e.tensor_tensor(out, a, b, op), *w)

    def ts(self, out, a, s1, s2, op0, op1, *w):
        if s2 is None:
            return self.dv.op(lambda e: e.tensor_scalar(out, a, s1, None, op0), *w)
        return self.dv.op(lambda e: e.tensor_scalar(out, a, s1, s2, op0, op1), *w)

    def stt(self, out, a, s, b, op0, op1, *w):
        return self.dv.op(lambda e: e.scalar_tensor_tensor(out, a, s, b, op0, op1), *w)

    def cp(self, out, a, *w):
        return self.dv.op(lambda e: e.tensor_copy(out, a), *w)

    def red(self, out, a, op, *w):
        return self.dv.op(lambda e: e.tensor_reduce(out, a, AX, op), *w)

    def recip(self, out, a, *w):
        return self.dv.op(lambda e: e.reciprocal(out, a), *w)

    def act(self, out, a, func, *w, bias=0.0, scale=1.0, accum=None):
        if accum is not None:
            return self.ac.op(lambda e: e.activation(out, a, func, bias=bias, scale=scale, accum_out=accum), *w)
        return self.ac.op(lambda e: e.activation(out, a, func, bias=bias, scale=scale), *w)

    def acp(self, out, a, *w, scale=1.0):
        return self.ac.op(lambda e: e.activation(out, a, ACT.Copy, scale=scale), *w)

    def mm(self, group, *w):
        self.pe.wait(*w)
        for k, (o, l, r, s, t) in enumerate(group):
            f = (lambda o, l, r, s, t: lambda e: e.matmul(o, l, r, start=s, stop=t, skip_group_check=True))(o, l, r, s, t)
            if k == len(group) - 1:
                return self.pe.op(f)
            self.pe.quiet(f)

    def tr(self, group, *w):
        self.pe.wait(*w)
        for k, (o, i) in enumerate(group):
            f = (lambda o, i, d: lambda e: e.transpose(o, i, d))(o, i, self.ident[0:i.shape[0], 0:i.shape[0]])
            if k == len(group) - 1:
                return self.pe.op(f)
            self.pe.quiet(f)

    def rstd(self, dst, src, scale, eps, *w):
        a = self.ts(dst, src, scale, eps, MUL, ADD, *w)
        n = dst.shape[1]
        return self.ptt(dst, dst, self.cst("neghalf")[:, 0:n], ALU.pow, a)

    def load(self, q, dst, src, *w):
        s = DmaSem(self.sem("ld"))
        t = s.add()
        q.dma(lambda e: e.dma_start(dst, src), s.sem, *w)
        return t

    def cst(self, name):
        o, n = self.cat[name]
        return self.cst_sb[:, o:o + n]

    def vec(self, name, k=0, n=1):
        o, _ = VAT[name]
        return self.vec_sb[:, o + k:o + k + n]

    def row(self, name):
        o, n = RAT[name]
        return self.row_sb[:, o:o + n]

    def region(self, lo, hi):
        return Region(self.big, lo, hi)

    def row_load(self, dst, src, *w):
        return self.load(self.ac, dst, src.partition_broadcast(128), *w)

class Region:
    def __init__(self, big, lo, hi):
        self.big, self.o, self.hi = big, lo, hi

    def take(self, n):
        assert self.o + n <= self.hi, (self.o, n, self.hi)
        a = self.big[:, self.o:self.o + n]
        self.o += n
        return a


class Slot:
    def __init__(self, ap, sem):
        self.ap, self.sem, self.n, self.prev, self.gate = ap, sem, 0, None, []


class Job:
    def __init__(self, slot, prev):
        self.slot, self.prev, self.release = slot, prev, []
        slot.n += 16
        self.tok = (slot.sem, slot.n)

    def before(self):
        return self.slot.gate if self.prev is None else self.prev.release


class Loads:

    def __init__(self, P):
        self.P, self.jobs, self.at, self.turn = P, [], 0, {}

    def plan(self, group, dst, src):
        k = self.turn.get(id(group), 0)
        self.turn[id(group)] = k + 1
        slot = group[k % len(group)]
        job = Job(slot, slot.prev)
        slot.prev = job
        job.ap = dst(slot.ap)
        self.jobs.append(job)
        ap = job.ap
        self.P.sp.items.append(("late", lambda: _flat(job.before())))
        self.P.sp.dma(lambda e: e.dma_start(ap, src), slot.sem)

    def take(self):
        self.at += 1
        return self.jobs[self.at - 1]


def _flat(toks):
    out = []
    for t in toks:
        if isinstance(t, list):
            out += _flat(t)
        elif t is not None:
            out.append(t)
    return out


def rounds(*tasks):
    live = list(tasks)
    while live:
        for t in list(live):
            for _ in range(t[1]):
                try:
                    next(t[0])
                except StopIteration:
                    live.remove(t)
                    break


def three(ap, a):
    return ap.rearrange("p (a b) -> p a b", a=a)


def plan_block1(P):
    A, L = P.A, P.loads
    two = P.ring[0:2]
    w_in = A["w_in"][0].rearrange("(c p) n -> p c n", p=128)
    wb = A["w_branch"][0]

    def cols(c0, n=512):
        L.plan(two, lambda s: three(s[:, 0:8 * n], 8), w_in[:, :, c0:c0 + n])

    def branch(n):
        L.plan(P.wbr_slots, lambda s: three(s, 2), wb[n].rearrange("(c p) n -> p c n", p=128))

    for c0 in (512, 0, 4096, 3072, 3584):
        cols(c0)
    for n in (3, 2):
        branch(n)
        cols(4608 + 1024 * n)
        cols(4608 + 1024 * n + 512)
    for c0 in (1024, 1536, 2048, 2560):
        cols(c0)
    for n in (0, 1):
        branch(n)
        cols(4608 + 1024 * n)
        cols(4608 + 1024 * n + 512)
    wo = A["w_out"][0].rearrange("(c p) n -> p c n", p=128)
    for h in range(2):
        L.plan(two, lambda s: three(s, 8), wo[:, :, 512 * h:512 * h + 512])
    for f0 in range(0, FF, 512):
        n = min(512, FF - f0)
        for name in ("ffn_w_gate", "ffn_w_up"):
            w = A[name][0].rearrange("(c p) n -> p c n", p=128)
            L.plan(P.ring, lambda s, n=n: three(s[:, 0:8 * n], 8), w[:, :, f0:f0 + n])
    for f0 in range(0, FF, 512):
        n = min(512, FF - f0)
        L.plan(P.ring, lambda s, n=n: three(s[:, 0:n * 8], n // 128),
               A["ffn_w_down"][0, f0:f0 + n, :].rearrange("(c p) n -> p c n", p=128))


def halves(P, bank, job, m, rhs, n, *w):
    lhs = job.ap[:, :, 128 * m:128 * m + 128]
    P.mm([(bank[:, 0:n], lhs[:, k, :], rhs[:, k, :], k == 0, False) for k in range(4)], job.tok, *w)
    yield None
    yield P.mm([(bank[:, 0:n], lhs[:, k, :], rhs[:, k, :], False, k == 7) for k in range(4, 8)])


def norm_transpose(P, x, hT, gain, tmp, banks, toks, n=512, col0=0):
    ss, rs = P.small.take(4), P.small.take(4)
    w = []
    for t in range(4):
        w.append(P.act(P.junk, x[:, t, :], ACT.Square, toks[t], P.junk_free, accum=ss[:, t:t + 1]))
        P.junk_free = w[-1]
    r = P.rstd(rs, ss, 1.0 / D, 1e-6, w)
    hs = [P.ts(tmp[:, t, :], x[:, t, :], rs[:, t:t + 1], None, MUL, None, r) for t in range(4)]
    out = []
    for c in range(8):
        k, bank, free = banks.take()
        p = P.tr([(bank[:, 128 * t:128 * t + 128], tmp[:, t, 128 * c:128 * c + 128]) for t in range(4)], hs, free)
        g = gain[:, c:c + 1]
        if c % 2:
            e = P.act(hT[:, c, :], bank[:, :], ACT.Copy, p, scale=g)
        else:
            e = P.ts(hT[:, c, :], bank[:, :], g, None, MUL, None, p)
        banks.free[k] = e
        out.append(e)
    return out


def block1_mixers(P):
    A = P.A
    R = P.region(2 * SLOT, P.top)
    P.wbr_slots = [Slot(R.take(2048), P.sem("wbr"))]
    plan_block1(P)
    hT = three(R.take(4096), 8)
    mT = three(R.take(4096), 8)
    yT = {n: three(R.take(1024), 2) for n in (0, 2, 3)}
    th_buf = Slots([R.take(512) for _ in range(2)])
    br_buf = Slots([R.take(512) for _ in range(2)])
    P.v2 = three(R.take(1024), 4)
    wua, gup = R.take(256), R.take(256)
    tw = P.load(P.ac, wua[0:64, :], A["rwkv_w_up"][0])
    tw2 = P.load(P.ac, wua[64:128, :], A["rwkv_a_up"][0])
    tg = P.load(P.ac, gup, A["rwkv_g_up"][0])
    mark = R.o
    P.junk = P.big[:, mark:mark + 1024]

    xs = three(mT.rearrange("p a b -> p (a b)"), 4)
    ld = P.xtoks(xs)
    hT_t = norm_transpose(P, xs, hT, P.vec("norm_mix_pre", 0, 8), xs, Slots(P.ps[0:8]), ld)

    dense = Slots(P.ps[0:2])
    rw = Slots(P.ps[2:4])
    misc = Slots([P.ps[4], P.ps[7]])
    sc = Slots([P.ps[5], P.ps[6]])
    for s in (dense, rw, misc, sc):
        s.free = [hT_t] * 2

    pT = R.take(8 * 513).rearrange("p (a b) -> p a b", a=8)
    zt = P.dv.op(lambda e: e.memset(pT[:, :, 0:1], 0.0), hT_t)
    lw, L, av, kk = (three(R.take(1024), 2) for _ in range(4))
    et = three(R.take(1024), 2)
    tmps = Slots([R.take(512) for _ in range(2)])
    Bt, Kt, Vt = (R.take(256) for _ in range(3))
    X, W, Tm, TT, Ym = (three(R.take(512), 4) for _ in range(5))
    MN, GG = (three(R.take(1024), 8) for _ in range(2))
    MT, NT, GbT, GkT = MN[:, 0:4, :], MN[:, 4:8, :], GG[:, 0:4, :], GG[:, 4:8, :]
    QT, PT, ST, S2 = (three(R.take(n), 2) for n in (256, 128, 128, 128))
    osb, osq = three(R.take(256), 4), three(R.take(256), 4)
    ysb = R.take(256)
    cvec, E1, E2 = (three(R.take(8), 2) for _ in range(3))
    bon = three(R.take(16), 4)
    hw0, ha0 = R.take(2), R.take(2)
    rstat = R.take(16)
    rwkv_end = R.o
    dqk = three(R.take(2048), 4)
    dvv = three(R.take(1024), 4)
    conv_lo = R.o
    SS = [R.take(512) for _ in range(4)]
    aT = Slots([R.take(512) for _ in range(2)])
    dO = Slots([(three(R.take(256), 4), three(R.take(256), 4)) for _ in range(1)])
    diff_hi = R.o
    dstat = R.take(64)
    lamt = R.take(8)
    conv_end = R.o
    C = P.region(conv_lo, diff_hi)
    cu = C.take(2 * 542).rearrange("p (a b) -> p a b", a=2)
    cy = yT[3]
    ctm = three(C.take(1024), 2)
    chb = R.take(4)

    done = {}

    def project():
        job = None
        order = ([("r", c) for c in (4, 5, 6, 7)] + [("r", c) for c in (0, 1, 2, 3)] + [("c", c) for c in range(4)])
        for i, (kind, c) in enumerate(order):
            if i % 4 == 0:
                job = P.loads.take()
            k, bank, free = dense.take()
            for p in halves(P, bank, job, c % 4, hT, 512, free, hT_t):
                if p is None:
                    yield
            if i % 4 == 3:
                job.release = [p]
            if kind == "r":
                dense.free[k] = done["r", c] = P.acp(pT[:, c, 1:513], bank[:, :], p)
            elif c < 2:
                done["ca", c] = P.acp(ctm[:, c, :], bank[:, :], p)
                dense.free[k] = done["ca", c]
            else:
                t = P.act(cu[:, c - 2, 30:542], bank[:, :], ACT.Tanh, p, scale=0.5)
                dense.free[k] = done["cb", c - 2] = t
            yield
        job = P.loads.take()
        P.job_v2 = job
        for m in (2, 3):
            k, bank, free = dense.take()
            for p in halves(P, bank, job, m, hT, 512, free):
                if p is None:
                    yield
            dense.free[k] = done["dq", m - 2] = P.acp(dqk[:, m - 2, :], bank[:, :], p)
            yield
        for t in range(4):
            k, bank, free = dense.take()
            p = P.mm([(bank[:, 0:256], hT[:, c, 128 * t:128 * t + 128], job.ap[:, c, 0:256], c == 0, c == 7)
                      for c in range(8)], free)
            dense.free[k] = done["v2", t] = P.acp(P.v2[:, t, :], bank[:, 0:256], p)
            yield
        job.release = [p]
        job = P.loads.take()
        for m in (0, 1):
            k, bank, free = dense.take()
            for p in halves(P, bank, job, m, hT, 512, free):
                if p is None:
                    yield
            dense.free[k] = done["dk", m] = P.acp(dqk[:, 2 + m, :], bank[:, :], p)
            yield
        for t in range(4):
            k, bank, free = dense.take()
            p = P.mm([(bank[:, 0:256], hT[:, c, 128 * t:128 * t + 128], job.ap[:, c, 256:512], c == 0, c == 7)
                      for c in range(8)], free, job.tok)
            dense.free[k] = done["dv", t] = P.acp(dvv[:, t, :], bank[:, 0:256], p)
            yield
        job.release = [p]

    state = dict(first=True, m=[None] * 8)

    def merge(n):
        wbj = P.loads.take()
        first = state["first"]
        state["first"] = False
        for half in range(2):
            job = P.loads.take()
            for d in range(4):
                dd = 4 * half + d
                k, bank, free = dense.take()
                for p in halves(P, bank, job, d, hT, 512, free):
                    if p is None:
                        yield
                kt, th, tfree = th_buf.take()
                a = P.act(th, bank[:, :], ACT.Tanh, p, tfree, P.gb_t, scale=0.5, bias=P.gb[:, 8 * n + dd:8 * n + dd + 1])
                dense.free[k] = a
                k2, bank2, free2 = dense.take()
                q = P.mm([(bank2[:, :], wbj.ap[:, c, 128 * dd:128 * dd + 128], yT[n][:, c, :], c == 0, c == 1)
                          for c in range(2)], free2, done["y", n], wbj.tok)
                if first:
                    b = P.stt(mT[:, dd, :], th, 1.0, bank2[:, :], ADD, MUL, a, q, hT_t)
                    state["m"][dd] = b
                else:
                    kb, tb, bfree = br_buf.take()
                    b = P.stt(tb, th, 1.0, bank2[:, :], ADD, MUL, a, q, bfree)
                    state["m"][dd] = P.ptt(mT[:, dd, :], mT[:, dd, :], tb, ADD, b, state["m"][dd])
                    br_buf.free[kb] = state["m"][dd]
                dense.free[k2] = b
                th_buf.free[kt] = b
                yield
            job.release = [p]
        wbj.release = [q]

    def conv():
        w = P.vec("conv_dw_w", 0, 62)
        z = P.dv.op(lambda e: e.memset(cu[:, :, 0:30], 0.0))
        h0 = P.ts(chb[:, 0:2], P.vec("conv_ln_g", 0, 2), 0.5, None, MUL, None)
        h1 = P.ts(chb[:, 2:4], P.vec("conv_ln_b", 0, 2), 0.5, None, MUL, None)
        while ("cb", 1) not in done:
            yield
        last = [None, None]
        for ch in range(2):
            last[ch] = P.stt(cu[:, ch, 30:542], cu[:, ch, 30:542], 1.0, ctm[:, ch, :], ADD, MUL, done["ca", ch], done["cb", ch])
        for j in range(31):
            for ch in range(2):
                s = w[:, 2 * j + ch:2 * j + ch + 1]
                if j == 0:
                    last[ch] = P.ts(cy[:, ch, :], cu[:, ch, 0:512], s, None, MUL, None, last[ch], z)
                else:
                    last[ch] = P.stt(cy[:, ch, :], cu[:, ch, j:j + 512], s, cy[:, ch, :], MUL, ADD, last[ch])
            if j % 2:
                yield
        for ch in range(2):
            last[ch] = P.ts(cy[:, ch, :], cy[:, ch, :], 0.5, P.vec("conv_dw_b", ch), MUL, ADD, last[ch])
        k, bank, free = misc.take()
        mean = P.cst("mean256")
        p = P.mm([(bank[:, :], mean, cy[:, ch, :], ch == 0, ch == 1) for ch in range(2)], free, last)
        last = [P.tt(cy[:, ch, :], cy[:, ch, :], bank[:, :], SUB, p) for ch in range(2)]
        misc.free[k] = last[1]
        yield
        sq = [P.act(ctm[:, ch, :], cy[:, ch, :], ACT.Square, last[ch]) for ch in range(2)]
        k, bank, free = misc.take()
        p = P.mm([(bank[:, :], mean, ctm[:, ch, :], ch == 0, ch == 1) for ch in range(2)], free, sq)
        sd = P.act(cu[:, 0, 0:512], bank[:, :], ACT.Sqrt, p, last, bias=P.cst("eps")[:, 0:1])
        misc.free[k] = sd
        yield
        r = P.recip(cu[:, 0, 0:512], cu[:, 0, 0:512], sd)
        last = [P.tt(cy[:, ch, :], cy[:, ch, :], cu[:, 0, 0:512], MUL, r, sq) for ch in range(2)]
        yield
        for ch in range(2):
            a = P.act(ctm[:, ch, :], cy[:, ch, :], ACT.Tanh, last[ch], p, h0, h1, scale=chb[:, ch:ch + 1], bias=chb[:, 2 + ch:3 + ch])
            b = P.ts(cy[:, ch, :], cy[:, ch, :], chb[:, ch:ch + 1], chb[:, 2 + ch:3 + ch], MUL, ADD, a)
            last[ch] = P.stt(cy[:, ch, :], ctm[:, ch, :], 1.0, cy[:, ch, :], ADD, MUL, a, b)
        done["y", 3] = list(last)

    slopes4 = alibi(4)
    dscale = 32 ** -0.5
    rdf = P.cst("rdf")
    one_minus = 1.0 - (0.8 - 0.6 * float(np.exp(0.0)))

    def lam():
        v = [P.row(f"diff_lam_{x}") for x in ("q1", "k1", "q2", "k2")]
        w = []
        for m in range(2):
            a = P.tt(dstat[:, 0:32], v[2 * m], v[2 * m + 1], MUL, w)
            w = [P.red(lamt[:, m:m + 1], dstat[:, 0:32], ADD, a)]
        a = P.act(lamt[:, 2:4], lamt[:, 0:2], ACT.Exp, w)
        b = P.tt(lamt[:, 4:5], lamt[:, 3:4], lamt[:, 2:3], SUB, a)
        return P.ts(lamt[:, 5:6], lamt[:, 4:5], -(1.0 - one_minus), None, ADD, None, b)

    def diff():
        while ("y", 3) not in done or ("dv", 3) not in done:
            yield
        lam_t = lam()
        free = done["y", 3]
        units = [(i, h) for i in range(4) for h in range(4)]
        st = {}
        sfree = [free] * 4
        ofree = [None]

        def front(u):
            i, h = units[u]
            n = 128 * (i + 1)
            ex = []
            for m in range(2):
                k, bank, bfree = sc.take()
                part = slice(64 * (h % 2) + 32 * m, 64 * (h % 2) + 32 * m + 32)
                p = P.mm([(bank[:, 0:n], dqk[part, h // 2, 128 * i:128 * i + 128], dqk[part, 2 + h // 2, 0:n], True, True)],
                         bfree, done["dq", h // 2], done["dk", h // 2])
                sb = 2 * (u % 2) + m
                S = SS[sb][:, 0:n]
                a = P.stt(S, rdf[:, 512 - n:512], -slopes4[h] / dscale, bank[:, 0:n], MUL, ADD, p, sfree[sb], free)
                sc.free[k] = a
                o = 16 + 8 * sb
                b = P.red(dstat[:, 32 + sb:33 + sb], S, MAX, a)
                c = P.ts(dstat[:, 36 + sb:37 + sb], dstat[:, 32 + sb:33 + sb], -dscale, None, MUL, None, b)
                e = P.act(S, S, ACT.Exp, c, bias=dstat[:, 36 + sb:37 + sb], scale=dscale, accum=dstat[:, 40 + sb:41 + sb])
                ex.append(e)
            st[u] = ex

        def back(u):
            i, h = units[u]
            n = 128 * (i + 1)
            s0 = 2 * (u % 2)
            r = P.recip(dstat[:, 44 + s0:46 + s0], dstat[:, 40 + s0:42 + s0], st[u])
            m1 = P.tt(dstat[:, 48 + s0:49 + s0], dstat[:, 45 + s0:46 + s0], lamt[:, 5:6], MUL, r, lam_t)
            a = P.ts(SS[s0][:, 0:n], SS[s0][:, 0:n], dstat[:, 44 + s0:45 + s0], None, MUL, None, r)
            b = P.stt(SS[s0][:, 0:n], SS[s0 + 1][:, 0:n], dstat[:, 48 + s0:49 + s0], SS[s0][:, 0:n], MUL, ADD, a, m1)
            sfree[s0 + 1] = b
            k, bank, bfree = misc.take()
            p = P.tr([(bank[:, 128 * c:128 * c + 128], SS[s0][:, 128 * c:128 * c + 128]) for c in range(i + 1)], b, bfree)
            sfree[s0] = p
            ka, at, afree = aT.take()
            e = P.acp(at[:, 0:n], bank[:, 0:n], p, afree)
            misc.free[k] = e
            k, bank, bfree = misc.take()
            q = P.mm([(bank[:, 0:64], at[:, 128 * c:128 * c + 128], dvv[:, c, 64 * h:64 * h + 64], c == 0, c == i)
                      for c in range(i + 1)], e, bfree, [done["dv", c] for c in range(i + 1)])
            aT.free[ka] = q
            o, osq2 = dO.items[0]
            e = P.acp(o[:, h, :], bank[:, 0:64], q, ofree[0])
            misc.free[k] = e
            st[u] = e

        def finish(i):
            o, sq = dO.items[0]
            w = [st[4 * i + h] for h in range(4)]
            a = P.tt(sq, o, o, MUL, w)
            b = P.red(dstat[:, 52:56], sq, ADD, a)
            r = P.rstd(dstat[:, 56:60], dstat[:, 52:56], 1.0 / 64, 1e-5, b)
            c = P.tt(sq, o, dstat[:, 56:60].unsqueeze(2).to_broadcast([128, 4, 64]), MUL, r)
            g = P.row("diff_subln_g").unsqueeze(1).to_broadcast([128, 4, 64])
            d = P.stt(o, sq, one_minus, g, MUL, MUL, c)
            k, bank, bfree = misc.take()
            of = o.rearrange("p a b -> p (a b)")
            p = P.tr([(bank[:, 128 * c:128 * c + 128], of[:, 128 * c:128 * c + 128]) for c in range(2)], d, bfree)
            ofree[0] = p
            e = P.acp(yT[2][:, :, 128 * i:128 * i + 128], three(bank[:, 0:256], 2), p)
            misc.free[k] = e
            done.setdefault("y2", []).append(e)

        front(0)
        yield
        for u in range(16):
            if u + 1 < 16:
                front(u + 1)
                yield
            back(u)
            yield
            if u % 4 == 3:
                finish(u // 4)
                yield
        done["y", 2] = done["y2"]

    def rwkv():
        mu = P.vec("rwkv_mu", 0, 8)
        p = {}

        def shift(c):
            k, tmp, free = tmps.take()
            a = P.tt(tmp, pT[:, c, 0:512], pT[:, c, 1:513], SUB, done["r", c], zt, free)
            p[c] = P.stt(pT[:, c, 1:513], tmp, mu[:, c:c + 1], pT[:, c, 1:513], MUL, ADD, a)
            tmps.free[k] = p[c]

        V = lambda c: pT[:, c, 1:513]
        a0 = P.ts(hw0, P.vec("rwkv_w0", 0, 2), 0.5, None, MUL, None)
        a1 = P.ts(ha0, P.vec("rwkv_a0", 0, 2), 0.5, None, MUL, None)
        for c in (6, 7):
            while ("r", c) not in done:
                yield
            shift(c)
        th = P.act(pT[0:64, 6, 1:513], pT[0:64, 6, 1:513], ACT.Tanh, p[6])
        sg = P.act(V(7), V(7), ACT.Tanh, p[7], scale=0.5)
        sg = P.ts(V(7), V(7), 0.5, 0.5, MUL, ADD, sg)
        yield
        lw_t, av_t = [], []
        for ch in range(2):
            k, bank, free = rw.take()
            q = P.mm([(bank[:, :], wua[0:64, 128 * ch:128 * ch + 128], pT[0:64, 6, 1:513], True, True)], th, free, tw)
            e = P.act(lw[:, ch, :], bank[:, :], ACT.Tanh, q, a0, scale=0.5, bias=hw0[:, ch:ch + 1])
            rw.free[k] = e
            lw_t.append(P.ts(lw[:, ch, :], lw[:, ch, :], -0.5 * 0.606531, -0.5 * 0.606531, MUL, ADD, e))
            k, bank, free = rw.take()
            q = P.mm([(bank[:, :], wua[64:128, 128 * ch:128 * ch + 128], pT[64:128, 6, 1:513], True, True)], p[6], free, tw2)
            e = P.act(av[:, ch, :], bank[:, :], ACT.Tanh, q, a1, scale=0.5, bias=ha0[:, ch:ch + 1])
            rw.free[k] = e
            av_t.append(P.ts(av[:, ch, :], av[:, ch, :], 0.5, 0.5, MUL, ADD, e))
            yield
        zero = P.cst("zero")
        sc_t = []
        for ch in range(2):
            w = []
            for t in range(4):
                s = slice(128 * t, 128 * t + 128)
                w.append(P.dv.op((lambda ch, s: lambda e: e.tensor_tensor_scan(L[:, ch, s], lw[:, ch, s], zero, 0.0, ADD, ADD))(ch, s), lw_t[ch]))
            l4 = L[:, ch, :].rearrange("p (t n) -> p t n", t=4)
            a = P.cp(cvec[:, ch, :], l4[:, :, 63], w)
            sc_t.append(P.tt(l4, l4, cvec[:, ch, :].unsqueeze(2).to_broadcast([128, 4, 128]), SUB, a))
        e1 = P.act(E1, cvec, ACT.Exp, sc_t)
        yield
        for c in (4, 5, 2, 3, 0, 1):
            while ("r", c) not in done:
                yield
            shift(c)
        yield
        kk_t, k_t, b_t = [], [], []
        for ch in range(2):
            a = P.ts(kk[:, ch, :], V(2 + ch), P.vec("rwkv_k_k", ch), None, MUL, None, p[2 + ch])
            kt, tmp, free = tmps.take()
            b = P.act(tmp, kk[:, ch, :], ACT.Square, a, free)
            k, bank, bfree = rw.take()
            q = P.mm([(bank[:, :], P.cst("headones"), tmp, True, True)], b, bfree)
            s = P.act(tmp, bank[:, :], ACT.Sqrt, q)
            rw.free[k] = s
            s = P.ts(tmp, tmp, 1e-12, None, MAX, None, s)
            s = P.recip(tmp, tmp, s)
            kk_t.append(P.tt(kk[:, ch, :], kk[:, ch, :], tmp, MUL, s))
            tmps.free[kt] = kk_t[-1]
            kt, tmp, free = tmps.take()
            a = P.ts(tmp, av[:, ch, :], -1.0, P.vec("rwkv_k_a", ch), ADD, MUL, av_t[ch], free)
            k_t.append(P.stt(V(2 + ch), tmp, 1.0, V(2 + ch), ADD, MUL, a, kk_t[ch]))
            tmps.free[kt] = k_t[ch]
            b_t.append(P.tt(av[:, ch, :], av[:, ch, :], kk[:, ch, :], MUL, kk_t[ch], k_t[ch]))
            yield
        k, bank, free = rw.take()
        for ch in range(2):
            kt, tmp, tfree = tmps.take()
            a = P.stt(tmp, V(ch), P.vec("rwkv_r_k", ch), V(2 + ch), MUL, MUL, p[ch], k_t[ch], tfree)
            q = P.mm([(bank[:, 4 * t + 2 * ch:4 * t + 2 * ch + 2], tmp[:, 128 * t:128 * t + 128], P.cst("headsel"), True, True)
                      for t in range(4)], a, free)
            tmps.free[kt] = q
        bon_t = P.acp(bon.rearrange("p a b -> p (a b)"), bank[:, 0:16], q)
        rw.free[k] = bon_t
        yield
        fin = []
        for ch in range(2):
            kt, tmp, tfree = tmps.take()
            a = P.tt(tmp, L[:, ch, :], lw[:, ch, :], SUB, sc_t[ch], tfree)
            e = P.act(tmp, tmp, ACT.Exp, a)
            fin.append(P.stt(kk[:, ch, :], kk[:, ch, :], -1.0, tmp, MUL, MUL, e, b_t[ch]))
            tmps.free[kt] = fin[-1]
            a = P.act(et[:, ch, :], L[:, ch, :], ACT.Exp, sc_t[ch], scale=-1.0)
            b = P.tt(av[:, ch, :], av[:, ch, :], et[:, ch, :], MUL, a, b_t[ch])
            c = P.tt(V(2 + ch), V(2 + ch), et[:, ch, :], MUL, a, bon_t)
            a2 = P.act(L[:, ch, :], L[:, ch, :], ACT.Exp, a, fin[-1])
            d = P.cp(E2[:, ch, :], L[:, ch, :].rearrange("p (t n) -> p t n", t=4)[:, :, 127], a2)
            f = P.tt(V(ch), V(ch), L[:, ch, :], MUL, a2, bon_t)
            fin += [b, c, d, f]
            yield
        yT_t = []
        st_t = P.dv.op(lambda e: e.memset(S2, 0.0))
        tile_free = []
        ysb_free = None
        for t in range(4):
            s = slice(128 * t, 128 * t + 128)
            AT = lambda h: kk[64 * (h % 2):64 * (h % 2) + 64, h // 2, s]
            BT = lambda h: av[64 * (h % 2):64 * (h % 2) + 64, h // 2, s]
            KT = lambda h: pT[64 * (h % 2):64 * (h % 2) + 64, 2 + h // 2, 1 + 128 * t:129 + 128 * t]
            RT = lambda h: pT[64 * (h % 2):64 * (h % 2) + 64, h // 2, 1 + 128 * t:129 + 128 * t]
            k, bank, free = rw.take()
            q = P.tr([(bank[:, 128 * c:128 * c + 128], kk[:, c, s]) for c in range(2)]
                     + [(bank[:, 256 + 128 * c:384 + 128 * c], av[:, c, s]) for c in range(2)], fin, free)
            x_t = P.cp(X[:, :, 0:64], three(bank[:, 0:256], 4), q, tile_free)
            b_ = P.cp(Bt, bank[:, 256:512], q, tile_free)
            rw.free[k] = b_
            yield
            k, bank, free = rw.take()
            q = P.tr([(bank[:, 128 * c:128 * c + 128], pT[:, 2 + c, 1 + 128 * t:129 + 128 * t]) for c in range(2)]
                     + [(bank[:, 256 + 128 * c:384 + 128 * c], pT[:, 4 + c, 1 + 128 * t:129 + 128 * t]) for c in range(2)], fin, p[4], p[5], free)
            k_ = P.acp(Kt, bank[:, 0:256], q, tile_free)
            v_ = P.acp(Vt, bank[:, 256:512], q, tile_free)
            rw.free[k] = v_
            yield
            got = {}
            for name, dst, l, r, mask in (("M", MN, (BT, KT), AT, "strict"), ("G", GG, (BT, KT), RT, "incl")):
                z = P.po.op((lambda dst: lambda e: e.memset(dst, 0.0))(dst), tile_free)
                m = P.cst(mask).bitcast(I32).unsqueeze(1).to_broadcast([128, 4, 128])
                got[name] = []
                for par in range(2):
                    k, bank, free = rw.take()
                    q = P.mm([(bank[:, 256 * y + 128 * g:256 * y + 128 * g + 128], l[y](2 * g + par), r(2 * g + par), True, True)
                              for y in range(2) for g in range(2)], fin, free)
                    got[name].append(P.dv.op((lambda dst, m, bank, par: lambda e: e.copy_predicated(
                        dst[:, par::2, :], m, three(bank[:, :], 4)))(dst, m, bank, par), q, z))
                    rw.free[k] = got[name][-1]
                yield
            k, bank, free = rw.take()
            q = P.mm([(bank[:, 64 * h:64 * h + 64], NT[:, h, :], Vt[:, 64 * h:64 * h + 64], True, True) for h in range(4)], got["M"], v_, free)
            x2 = P.acp(X[:, :, 64:128], three(bank[:, 0:256], 4), q)
            rw.free[k] = x2
            idb = P.ident.unsqueeze(1).to_broadcast([128, 4, 128])
            t_t = P.po.op(lambda e: e.tensor_copy(Tm, idb), tile_free)
            tt_t = P.po.op(lambda e: e.tensor_copy(TT, idb), tile_free)
            y_free = tile_free
            for b in range(7):
                k, bank, free = rw.take()
                q = P.mm([(bank[:, 128 * h:128 * h + 128], MT[:, h, :], Tm[:, h, :], True, True) for h in range(4)], got["M"], t_t, free)
                m = P.cst(f"lev{b}").unsqueeze(1).to_broadcast([128, 4, 128])
                y = P.tt(Ym, three(bank[:, :], 4), m, MUL, q, y_free)
                rw.free[k] = y
                yield
                k, bank, free = rw.take()
                q2 = P.mm([(bank[:, 128 * h:128 * h + 128], Ym[:, h, :], TT[:, h, :], True, True) for h in range(4)], y, tt_t, free)
                y_free = q2
                if b < 6:
                    k1, bank1, free1 = rw.take()
                    q1 = P.mm([(bank1[:, 128 * h:128 * h + 128], TT[:, h, :], Ym[:, h, :], True, True) for h in range(4)], free1)
                    y_free = q1
                    t_t = P.tt(Tm, Tm, three(bank1[:, :], 4), ADD, q1)
                    rw.free[k1] = t_t
                    tt_t = P.tt(TT, TT, three(bank[:, :], 4), ADD, q2, q1)
                else:
                    tt_t = P.tt(TT, TT, three(bank[:, :], 4), ADD, q2)
                rw.free[k] = tt_t
                yield
            k, bank, free = rw.take()
            q = P.mm([(bank[:, 128 * h:128 * h + 128], TT[:, h, :], X[:, h, :], True, True) for h in range(4)], tt_t, x_t, x2, free)
            w_t = P.cp(W, three(bank[:, :], 4), q)
            rw.free[k] = w_t
            yield
            k, bank, free = rw.take()
            q = P.mm([(bank[64 * (h % 2):64 * (h % 2) + 64, 128 * (h // 2):128 * (h // 2) + 128], W[:, h, 0:64], GbT[:, h, :], True, True)
                      for h in range(4)], w_t, got["G"], free)
            q = P.mm([(bank[64 * (h % 2):64 * (h % 2) + 64, 256 + 64 * (h // 2):320 + 64 * (h // 2)], W[:, h, 0:64], Bt[:, 64 * h:64 * h + 64], True, True)
                      for h in range(4)], b_)
            qt_t = P.tt(QT, three(bank[:, 0:256], 2), pT[:, 0:2, 1 + 128 * t:129 + 128 * t], ADD, q, tile_free)
            pt_t = P.cp(PT, three(bank[:, 256:384], 2), q, tile_free)
            rw.free[k] = pt_t
            yield
            if t:
                st_t = P.tt(S2, ST, E1[:, :, t:t + 1].to_broadcast([128, 2, 64]), MUL, st_t, e1, tile_free)
            ends, zs = [], []
            for par in range(2):
                hp = slice(64 * par, 64 * par + 64)
                k, bank, free = rw.take()
                g = []
                for c in range(2):
                    h = 2 * c + par
                    o = bank[hp, 64 * c:64 * c + 64]
                    g += [(o, Bt[:, 64 * h:64 * h + 64], W[:, h, 64:128], True, False),
                          (o, Kt[:, 64 * h:64 * h + 64], Vt[:, 64 * h:64 * h + 64], False, t == 0)]
                    if t:
                        g.append((o, PT[hp, c, :], S2[hp, c, :], False, True))
                zq = P.mm(g, free, k_, st_t, pt_t, qt_t, got["G"])
                g = []
                for c in range(2):
                    h = 2 * c + par
                    o = bank[:, 128 + 64 * c:192 + 64 * c]
                    g += [(o, GbT[:, h, :], W[:, h, 64:128], True, False), (o, GkT[:, h, :], Vt[:, 64 * h:64 * h + 64], False, t == 0)]
                    if t:
                        g.append((o, QT[hp, c, :], S2[hp, c, :], False, True))
                qo = P.mm(g)
                a = P.tt(ST[hp, :, :], three(bank[hp, 0:128], 2), S2[hp, :, :], ADD, qo, st_t)
                zs.append(P.tt(ST[hp, :, :], ST[hp, :, :], E2[hp, :, t:t + 1].to_broadcast([64, 2, 64]), MUL, a))
                o_t = P.cp(osb[:, par::2, :], three(bank[:, 128:256], 2), qo, ysb_free)
                ends.append(o_t)
                rw.free[k] = o_t
            st_t, o_t = zs, ends
            yield
            s1, s2_, s3 = rstat[:, 0:4], rstat[:, 4:8], rstat[:, 8:12]
            a = P.red(s1, osb, ADD, o_t)
            a = P.ts(s1, s1, 1.0 / 64, None, MUL, None, a)
            a = P.tt(osb, osb, s1.unsqueeze(2).to_broadcast([128, 4, 64]), SUB, a)
            b = P.tt(osq, osb, osb, MUL, a)
            b = P.red(s2_, osq, ADD, b)
            b = P.rstd(s3, s2_, 1.0 / 64, 64e-5, b)
            a = P.tt(osb, osb, s3.unsqueeze(2).to_broadcast([128, 4, 64]), MUL, b)
            of = osb.rearrange("p a b -> p (a b)")
            a = P.tt(of, of, P.row("rwkv_ln_g"), MUL, a)
            a = P.tt(of, of, P.row("rwkv_ln_b"), ADD, a)
            b = P.tt(osq, three(Vt, 4), bon[:, t, :].unsqueeze(2).to_broadcast([128, 4, 64]), MUL, bon_t, v_, a)
            a = P.tt(osb, osb, osq, ADD, a, b)
            k, bank, free = rw.take()
            q = P.mm([(bank[:, 0:256], pT[:, 7, 1 + 128 * t:129 + 128 * t], gup, True, True)], sg, tg, free)
            a = P.tt(ysb, of, bank[:, 0:256], MUL, a, q, ysb_free)
            rw.free[k] = a
            yield
            k, bank, free = rw.take()
            q = P.tr([(bank[:, 128 * c:128 * c + 128], ysb[:, 128 * c:128 * c + 128]) for c in range(2)], a, free)
            ysb_free = q
            e = P.acp(yT[0][:, :, s], three(bank[:, 0:256], 2), q)
            rw.free[k] = e
            yT_t.append(e)
            tile_free = [q, a, e, st_t]
            yield
        done["y", 0] = yT_t

    def stream():
        yield from project()
        while ("y", 3) not in done:
            yield
        yield from merge(3)
        while ("y", 2) not in done:
            yield
        yield from merge(2)

    rounds((stream(), 1), (rwkv(), 1), (conv(), 1), (diff(), 1))
    part = [q.last() for q in (P.pe, P.ac, P.dv, P.po)]

    R2 = P.region(mark, P.top)
    qk = three(R2.take(6144), 12)
    vv = three(R2.take(2048), 4)
    rd = R2.take(P.ntab - P.ncst)
    yT[1] = three(R2.take(1024), 2)
    S3 = [R2.take(1280) for _ in range(2)]
    P3 = Slots([R2.take(512) for _ in range(6)])
    ob = R2.take(256)
    dst = R2.take(16)
    rd_t = P.load(P.ac, rd, A["tables"][:, P.ncst:P.ntab], part)

    def rdt(name):
        o, n = P.cat[name]
        return rd[:, o - P.ncst:o - P.ncst + n]

    def project2():
        first = True
        for s in range(3):
            job = P.loads.take()
            for m in range(4):
                k, bank, free = dense.take()
                for p in halves(P, bank, job, m, hT, 512, free):
                    if p is None:
                        yield
                c = 4 * s + m
                dense.free[k] = done["qk", c] = P.acp(qk[:, c, :], bank[:, :], p, part if first else None)
                first = False
                yield
            job.release = [p]
        job = P.loads.take()
        for t in range(4):
            k, bank, free = dense.take()
            p = P.mm([(bank[:, :], hT[:, c, 128 * t:128 * t + 128], job.ap[:, c, :], c == 0, c == 7) for c in range(8)], free, job.tok)
            dense.free[k] = done["vv", t] = P.acp(vv[:, t, :], bank[:, :], p)
            yield
        job.release = [p]

    slopes12 = alibi(12)
    scores = Slots(P.ps[2:5])
    turned = Slots(P.ps[5:7])
    outp = Slots(P.ps[7:8])
    for s in (scores, turned, outp):
        s.free = [part] * len(s.items)

    def dil():
        while ("vv", 3) not in done:
            yield
        units = [(i, j) for i in range(4) for j in range(4)]
        st = {}
        sfree = [part, part]
        ofree = [None]

        def blocks(i):
            return [(0, b) for b in range(max(0, i - 1), i + 1)] + [(1, b) for b in range(i + 1)] + [(2, b) for b in range(i + 1)]

        def front(u):
            i, j = units[u]
            S = S3[u % 2]
            col = 0
            w = []
            for g in range(3):
                b0 = max(0, i - 1) if g == 0 else 0
                n = 128 * (i + 1 - b0)
                hd = 4 * g + j
                part_ = slice(64 * (j % 2), 64 * (j % 2) + 64)
                k, bank, free = scores.take()
                p = P.mm([(bank[:, 0:n], qk[part_, hd // 2, 128 * i:128 * i + 128], qk[part_, 6 + hd // 2, 128 * b0:128 * i + 128], True, True)],
                         free, done["qk", hd // 2], done["qk", 6 + hd // 2])
                tab = rdt(f"rd{g}")
                a = P.stt(S[:, col:col + n], tab[:, tab.shape[1] - n:], -slopes12[hd] * 8.0, bank[:, 0:n], MUL, ADD, p, sfree[u % 2], rd_t)
                scores.free[k] = a
                w.append(a)
                col += n
            o = 4 * (u % 2)
            b = P.red(dst[:, o:o + 1], S[:, 0:col], MAX, w)
            c = P.ts(dst[:, o + 1:o + 2], dst[:, o:o + 1], -0.125, None, MUL, None, b)
            st[u] = P.act(S[:, 0:col], S[:, 0:col], ACT.Exp, c, bias=dst[:, o + 1:o + 2], scale=0.125, accum=dst[:, o + 2:o + 3])

        def back(u):
            i, j = units[u]
            S = S3[u % 2]
            o = 4 * (u % 2)
            r = P.recip(dst[:, o + 3:o + 4], dst[:, o + 2:o + 3], st[u])
            bl = blocks(i)
            ko, bo, ofr = outp.take()
            pv = []
            for c0 in range(0, len(bl), 4):
                n = min(4, len(bl) - c0)
                k, bank, free = turned.take()
                p = P.tr([(bank[:, 128 * c:128 * c + 128], S[:, 128 * (c0 + c):128 * (c0 + c) + 128]) for c in range(n)], st[u], free)
                kp, buf, pfree = P3.take()
                e = P.acp(buf[:, 0:128 * n], bank[:, 0:128 * n], p, pfree)
                turned.free[k] = e
                pv.append((c0, n, kp, buf, e))
            sfree[u % 2] = p
            for c0, n, kp, buf, e in pv:
                g = []
                for c in range(n):
                    grp, b = bl[c0 + c]
                    v0 = 256 * grp + 64 * j
                    V = vv[:, b, v0:v0 + 64] if grp < 2 else P.v2[:, b, v0 - 512:v0 - 448]
                    g.append((bo[:, 0:64], buf[:, 128 * c:128 * c + 128], V, c0 + c == 0, c0 + c == len(bl) - 1))
                q = P.mm(g, e, ofr, [done["vv", b] for b in range(4)])
                P3.free[kp] = q
            e = P.ts(ob[:, 64 * j:64 * j + 64], bo[:, 0:64], dst[:, o + 3:o + 4], None, MUL, None, q, r, ofree[0])
            outp.free[ko] = e
            st[u] = e

        def finish(i):
            k, bank, free = turned.take()
            p = P.tr([(bank[:, 128 * c:128 * c + 128], ob[:, 128 * c:128 * c + 128]) for c in range(2)],
                     [st[4 * i + j] for j in range(4)], free)
            ofree[0] = p
            e = P.acp(yT[1][:, :, 128 * i:128 * i + 128], three(bank[:, 0:256], 2), p)
            turned.free[k] = e
            done.setdefault("y1", []).append(e)

        front(0)
        yield
        for u in range(16):
            if u + 1 < 16:
                front(u + 1)
                yield
            back(u)
            yield
            if u % 4 == 3:
                finish(u // 4)
                yield
        done["y", 1] = done["y1"]

    def stream2():
        yield from project2()
        yield from merge(0)
        while ("y", 1) not in done:
            yield
        yield from merge(1)

    rounds((stream2(), 1), (dil(), 2))
    return mT, state["m"]


def add_norm(P, o, x, gain, out, *w):
    ss, rs = P.small.take(4), P.small.take(4)
    sq = []
    for t in range(4):
        sq.append(P.act(P.junk, o[:, t, :], ACT.Square, w[0][t], P.junk_free, accum=ss[:, t:t + 1]))
        P.junk_free = sq[-1]
    toks = []
    for t in range(4):
        r = P.rstd(rs[:, t:t + 1], ss[:, t:t + 1], 1.0 / D, 1e-6, sq[t])
        a = P.stt(o[:, t, :], o[:, t, :], rs[:, t:t + 1], gain, MUL, MUL, r, *w[1:])
        toks.append(P.tt(out[:, t, :], o[:, t, :], x[:, t, :], ADD, a))
    return toks


def block1_out(P, mT, m_t):
    A = P.A
    R = P.region(6 * SLOT, P.top)
    x1 = three(R.take(4096), 4)
    hT = three(R.take(4096), 8)
    aT = R.take(22 * 512).rearrange("p (a b) -> p a b", a=22)
    gain = R.take(1024)
    P.junk = R.take(1024)
    xr = three(aT.rearrange("p a b -> p (a b)")[:, 0:4096], 4)
    sg = Slots([R.take(512) for _ in range(2)])
    before = [q.last() for q in (P.pe, P.ac, P.dv, P.po)]
    ld = [P.load(P.ac, xr[:, t, :], A["x"][0, 128 * t:128 * t + 128, :], before if t == 0 else None) for t in range(4)]
    gt = P.row_load(gain, A["norm_mix_post"][0], before)
    banks = Slots(P.ps)
    banks.free = [before] * 8
    ev = {}
    for h in range(2):
        job = P.loads.take()
        for t in range(4):
            k, bank, free = banks.take()
            p = P.mm([(bank[:, :], mT[:, c, 128 * t:128 * t + 128], job.ap[:, c, :], c == 0, c == 7) for c in range(8)],
                     free, job.tok, m_t)
            banks.free[k] = ev[t, h] = P.acp(x1[:, t, 512 * h:512 * h + 512], bank[:, :], p, before, scale=0.5)
        job.release = [p]
    P.ring_gate += [p]
    x1_t = add_norm(P, x1, xr, gain, x1, [[ev[t, 0], ev[t, 1]] for t in range(4)], gt, ld)
    xn = three(aT.rearrange("p a b -> p (a b)")[:, 4096:8192], 4)
    h_t = norm_transpose(P, x1, hT, P.vec("norm_ffn_pre", 0, 8), xn, banks, x1_t)
    g2 = P.row_load(gain, A["norm_ffn_post"][0], x1_t)
    f = 0
    a_t = []
    for f0 in range(0, FF, 512):
        n = min(512, FF - f0)
        jg, ju = P.loads.take(), P.loads.take()
        for m in range(n // 128):
            k, bank, free = banks.take()
            p = P.mm([(bank[:, :], jg.ap[:, c, 128 * m:128 * m + 128], hT[:, c, :], c == 0, c == 7) for c in range(8)], free, jg.tok, h_t)
            ks, s, sfree = sg.take()
            a = P.act(s, bank[:, :], ACT.Silu, p, sfree)
            banks.free[k] = a
            k, bank, free = banks.take()
            q = P.mm([(bank[:, :], ju.ap[:, c, 128 * m:128 * m + 128], hT[:, c, :], c == 0, c == 7) for c in range(8)], free, ju.tok)
            b = P.tt(aT[:, f, :], s, bank[:, :], MUL, a, q)
            banks.free[k] = sg.free[ks] = b
            a_t.append(b)
            f += 1
        jg.release, ju.release = [p], [q]
    f = 0
    for f0 in range(0, FF, 512):
        n = min(512, FF - f0)
        job = P.loads.take()
        for t in range(4):
            for h in range(2):
                b = 2 * t + h
                p = P.mm([(P.ps[b][:, :], aT[:, f + c, 128 * t:128 * t + 128], job.ap[:, c, 512 * h:512 * h + 512], f + c == 0, f + c == 21)
                          for c in range(n // 128)], banks.free[b] if f == 0 else None, job.tok, a_t)
                if f0 + n == FF:
                    banks.free[b] = ev[t, h] = P.acp(hT.rearrange("p a b -> p (a b)")[:, 1024 * t + 512 * h:1024 * t + 512 * h + 512], P.ps[b][:, :], p, h_t)
        job.release = [p]
        f += n // 128
    o = three(hT.rearrange("p a b -> p (a b)"), 4)
    x2_t = add_norm(P, o, x1, gain, x1, [[ev[t, 0], ev[t, 1]] for t in range(4)], g2)
    return x1, x2_t


def setup(P):
    R = P.region(0, NBIG)
    n = P.cat["rd1"][0]
    P.ncst, P.ntab = n, P.table_cols
    top = NBIG - n - NVEC - NROW - 400 - 32
    P.top = top
    S = P.region(top, NBIG)
    P.cst_sb, P.vec_sb, P.row_sb = S.take(n), S.take(NVEC), S.take(NROW)
    P.gb = S.take(32)
    P.small = P.region(S.o, S.o + 400)
    P.junk_free = None
    P.ident = P.cst("ident")
    P.ring_gate = []
    P.ring = [Slot(P.big[:, SLOT * k:SLOT * k + SLOT], P.sem("ring")) for k in range(6)]
    for s in P.ring[2:]:
        s.gate = P.ring_gate
    P.loads = Loads(P)
    P.sp_sections = []

    def xtoks(xs):
        toks = [P.load(P.ac, xs[:, t, :], P.A["x"][0, 128 * t:128 * t + 128, :]) for t in range(4)]
        c = P.load(P.ac, P.cst_sb, P.A["tables"][:, 0:n])
        v = P.load(P.ac, P.vec_sb, P.A["vecs"])
        r = P.load(P.ac, P.row_sb, P.A["rows"].partition_broadcast(128))
        for q in (P.pe, P.ac, P.dv, P.po):
            q.wait(c, v, r)
        P.gb_t = P.ts(P.gb, P.vec("gate_bias", 0, 32), 0.5, None, MUL, None)
        return toks
    P.xtoks = xtoks


def program(nc, A, out, cat, table_cols):
    with ExitStack() as ctx:
        P = Program(nc, ctx, A, out)
        P.cat, P.table_cols = cat, table_cols
        setup(P)
        mT, m_t = block1_mixers(P)
        x2, x2_t = block1_out(P, mT, m_t)
        block2(P, x2, x2_t)
        for at, sec in reversed(list(zip(P.sp_at, P.sp_sections))):
            P.sp.items[at:at] = sec
        block = ctx.enter_context(nc.Block())

        @block.sync
        def _(e):
            P.sp.emit(e)

        @block.tensor
        def _(e):
            P.pe.emit(e)

        @block.scalar
        def _(e):
            P.ac.emit(e)

        @block.vector
        def _(e):
            P.dv.emit(e)

        @block.gpsimd
        def _(e):
            P.po.emit(e)


ALPHA = 4.0 ** 0.25
NTAB = 32


def plan_block2(P):
    A, L = P.A, P.loads
    ring = P.ring

    def cols(w, c0):
        L.plan(ring, lambda s: three(s, 8), w.rearrange("(c p) n -> p c n", p=128)[:, :, c0:c0 + 512])

    def experts(l):
        while P.loads.turn[id(ring)] % 6:
            P.loads.turn[id(ring)] += 1
        for e in range(NEXP):
            cols(A["moe_w_gate_2"][l, e], 0)
            cols(A["moe_w_up_2"][l, e], 0)
            L.plan(ring, lambda s: three(s, 4), A["moe_w_down_2"][l, e].rearrange("(c p) n -> p c n", p=128))

    for s in range(2):
        cols(A["lru_w_in_2"][0], 1024 + 512 * s)
        cols(A["lru_w_in_2"][0], 512 * s)
    for h in range(2):
        cols(A["lru_w_out_2"][0], 512 * h)
    experts(0)
    P.sp_at = [len(P.sp.items)]
    for s in range(2):
        for g in (1, 2, 0):
            cols(A["sc_w_in_2"][0], 1024 * g + 512 * s)
    for h in range(2):
        cols(A["sc_w_out_2"][0], 512 * h)
    experts(1)
    P.sp_at.append(len(P.sp.items))


def layer_norm(P, x, n, g, b, toks, gb_t):
    st = P.lnst.take()[1]
    st6, mv, rs = st[:, 0:12], st[:, 12:14], st[:, 14:15]
    w = [P.dv.op((lambda h: lambda e: e.bn_stats(st6[0:n, 6 * h:6 * h + 6], x[:, 512 * h:512 * h + 512]))(h), toks) for h in range(2)]
    a = P.dv.op(lambda e: e.bn_aggr(mv[0:n, :], st6[0:n, :]), w)
    r = P.ts(rs[0:n, :], mv[0:n, 1:2], 1.0, 1e-5, MUL, ADD, a)
    r = P.ptt(rs[0:n, :], rs[0:n, :], P.cst("neghalf")[0:n, 0:1], ALU.pow, r)
    a = P.ts(x, x, mv[0:n, 0:1], rs[0:n, 0:1], SUB, MUL, r)
    a = P.tt(x, x, g[0:n, :], MUL, a, gb_t)
    return P.tt(x, x, b[0:n, :], ADD, a)


def block2(P, x2, x2_t):
    A, nc = P.A, P.nc
    plan_block2(P)
    R = P.region(6 * SLOT + 4096, P.top)
    meta = R.take(1024)
    base = R.o
    before = [q.last() for q in (P.pe, P.ac, P.dv, P.po)]
    banks = Slots(P.ps)
    banks.free = [before] * 8
    stat = R.take(96)
    P.lnst = Slots([stat[:, 16 * k:16 * k + 16] for k in range(5)])
    hD = nc.dram_tensor("rows_h", (T + 17, D), F32, kind="Internal").ap()
    yD = nc.dram_tensor("rows_y", (64 * (NEXP + NOVF), D), F32, kind="Internal").ap()
    tab = [nc.dram_tensor(f"slot_{l}", (128 * NTAB, 1), I32, kind="Internal").ap() for l in range(2)]
    inner = R.o
    zr = P.load(P.ac, yD[64 * NEXP:64 * (NEXP + NOVF), :].rearrange("(p r) (k c) -> p (r k) c", p=128, c=128),
                P.cst("zero").unsqueeze(1).to_broadcast([128, 64, 128]))

    hT = R.take(8 * 528).rearrange("p (a b) -> p a b", a=8)
    z = R.take(8 * 528).rearrange("p (a b) -> p a b", a=8)
    gw = [three(R.take(1024), 8) for _ in range(2)]
    sp4 = R.take(8)
    hb = R.take(16)
    tmp8 = [R.take(8) for _ in range(5)]
    ux = Slots([R.take(532) for _ in range(2)])
    tb = Slots([[R.take(528) for _ in range(6)] for _ in range(2)])
    mt = P.load(P.ac, meta[0:16, :], A["meta_tokens_2"], before)
    gt = [P.load(P.ac, gw[i], A["lru_gates"][i], before) for i in range(2)]
    lam = P.vec("lru_lambda_2", 0, 8)
    u, d, e_, m, f = tmp8
    a = P.ts(u, lam, -1.0, None, MUL, None, before)
    a = P.tt(m, lam, u, MAX, a)
    a = P.act(e_, m, ACT.Exp, a, scale=-1.0)
    b = P.ts(d, e_, 1.0, None, ADD, None, a)
    c = P.act(f, d, ACT.Ln, b)
    b = P.ts(d, d, -1.0, None, ADD, None, c)
    c2 = P.ts(m, d, 0.0, None, ISEQ, None, b)
    c3 = P.tt(d, d, m, ADD, c2)
    c3 = P.recip(d, d, c3)
    c3 = P.tt(f, f, e_, MUL, c3)
    c3 = P.tt(f, f, d, MUL, c3)
    c2 = P.tt(m, m, e_, MUL, c3)
    c3 = P.tt(f, f, m, ADD, c2)
    c3 = P.stt(sp4, u, 0.0, f, MAX, ADD, c3)
    sp_t = P.ts(sp4, sp4, -2.0, None, MUL, None, c3)
    h0 = P.ts(hb[:, 0:8], P.vec("lru_b_a_2", 0, 8), 0.5, None, MUL, None, before)
    h1 = P.ts(hb[:, 8:16], P.vec("lru_b_i_2", 0, 8), 0.5, None, MUL, None)

    def turn(hT, off, w, n_meta, meta_at):
        out = []
        for c in range(8):
            k, bank, free = banks.take()
            p = P.tr([(bank[:, 128 * t:128 * t + 128], x2[:, t, 128 * c:128 * c + 128]) for t in range(4)], w, free)
            f = P.acp if c % 2 else P.cp
            out.append(f(hT[:, c, off:off + 512], bank[:, :], p))
            banks.free[k] = out[-1]
        if n_meta:
            k, bank, free = banks.take()
            p = P.tr([(bank[:, 16 * c:16 * c + 16], meta[0:16, 128 * c:128 * c + 128]) for c in range(8)], w, free)
            out.append(P.cp(hT[:, :, meta_at:meta_at + n_meta], three(bank[:, 0:128], 8)[:, :, 16 - n_meta:16], p))
            banks.free[k] = out[-1]
        return out

    h_t = turn(hT, 16, [x2_t, mt], 16, 0)
    zp = [P.dv.op((lambda x: lambda e: e.memset(x[:, 0:3], 0.0))(x)) for x in ux.items]
    N2 = 264

    def wide(job, m, rhs, w):
        got = []
        for hf in range(2):
            k, bank, free = banks.take()
            p = P.mm([(bank[:, 0:N2], job[:, c, 128 * m:128 * m + 128], rhs[:, c, N2 * hf:N2 * hf + N2], c == 0, c == 7) for c in range(8)], free, w)
            got.append((k, bank, p))
        return got

    z_t = []
    for s in range(2):
        jx, jy = P.loads.take(), P.loads.take()
        for mm_ in range(4):
            c = 4 * s + mm_
            ku, u_, ufree = ux.take()
            kt, (xc, th, q, it, hs, ge), tfree = tb.take()
            ev = []
            for hf, (k, bank, p) in enumerate(wide(jx.ap, mm_, hT, [jx.tok, h_t])):
                ev.append(P.acp(u_[:, 3 + N2 * hf:3 + N2 * hf + N2], bank[:, 0:N2], p, ufree))
                banks.free[k] = ev[-1]
                px = p
            w4 = P.vec("lru_conv_w_2", 0, 32)
            a = P.ts(xc, u_[:, 0:528], w4[:, c:c + 1], P.vec("lru_conv_b_2", c), MUL, ADD, ev, zp, tfree)
            for j in range(1, 4):
                a = P.stt(xc, u_[:, j:j + 528], w4[:, 8 * j + c:8 * j + c + 1], xc, MUL, ADD, a)
            ux.free[ku] = a
            ys = []
            for hf, (k, bank, p) in enumerate(wide(jy.ap, mm_, hT, [jy.tok])):
                ys.append(P.act(ge[:, N2 * hf:N2 * hf + N2], bank[:, 0:N2], ACT.Gelu_apprx_tanh, p, tfree))
                banks.free[k] = ys[-1]
                py = p
            rt, gt2 = [], []
            for g, dst, lst in ((0, th, rt), (1, it, gt2)):
                for hf in range(2):
                    k, bank, free = banks.take()
                    p = P.mm([(bank[:, 0:N2], gw[g][:, c, :], xc[:, N2 * hf:N2 * hf + N2], True, True)], a, free, gt[g])
                    lst.append(P.act(dst[:, N2 * hf:N2 * hf + N2], bank[:, 0:N2], ACT.Tanh, p, h0, h1, tfree, scale=0.5, bias=hb[:, 8 * g + c:8 * g + c + 1]))
                    banks.free[k] = lst[-1]
            t = P.act(th, th, ACT.Tanh, rt, sp_t, scale=sp4[:, c:c + 1], bias=sp4[:, c:c + 1])
            b = P.ts(q, th, -1.0, 1.0, MUL, ADD, t, tfree)
            b = P.recip(q, q, b)
            sq = P.act(hs, th, ACT.Sqrt, t, tfree, scale=-1.0)
            x = P.stt(it, it, 1.0, xc, ADD, MUL, gt2)
            x = P.tt(it, it, q, MUL, x, b)
            x = P.tt(it, it, hs, MUL, x, sq)
            y = P.stt(th, th, 1.0, q, ADD, MUL, b, sq)
            v = P.dv.op((lambda hs, th, it: lambda e: e.tensor_tensor_scan(hs, th, it, 0.0, MUL, ADD))(hs, th, it), x, y)
            v = P.tt(z[:, c, :], hs, ge, MUL, v, ys)
            tb.free[kt] = v
            z_t.append(v)
        jx.release, jy.release = [px], [py]
    tiles = [(x2[:, t, :], 128, 16 + 128 * t) for t in range(4)] + [(meta[0:16, :], 16, 0)]

    def residual(z, z_t, tiles):
        w = {}
        for h in range(2):
            job = P.loads.take()
            for x, n, c0 in tiles:
                k, bank, free = banks.take()
                p = P.mm([(bank[0:n, :], z[:, c, c0:c0 + n], job.ap[:, c, :], c == 0, c == 7) for c in range(8)], free, z_t, job.tok)
                xs = x[:, 512 * h:512 * h + 512]
                e = P.stt(xs, xs, ALPHA, bank[0:n, :], MUL, ADD, p)
                banks.free[k] = e
                w.setdefault(c0, []).append(e)
            job.release = [p]
        return [w[c0] for _, _, c0 in tiles]

    w = residual(z, z_t, tiles)
    R = P.region(inner, P.top)
    g, b = R.take(1024), R.take(1024)
    lt = [P.row_load(g, A["ln_g_2"][0, 0], w), P.row_load(b, A["ln_b_2"][0, 0], w)]
    w = [layer_norm(P, x, n, g, b, w[i], lt) for i, (x, n, _) in enumerate(tiles)]
    w = moe(P, 0, x2, meta, tiles, w, banks, inner, hD, yD, tab[0], zr)

    R = P.region(inner, P.top)
    hT = R.take(8 * 514).rearrange("p (a b) -> p a b", a=8)
    z = three(R.take(4096), 8)
    cg = Slots([R.take(514) for _ in range(2)])
    zz = Slots([R.take(514) for _ in range(2)])
    zc = Slots([R.take(512) for _ in range(2)])
    h_t = turn(hT, 2, w, 2, 0)
    w3 = P.vec("sc_conv_w_2", 0, 24)
    z_t = []
    N2 = 257
    for s in range(2):
        jc, jv, jb = P.loads.take(), P.loads.take(), P.loads.take()
        for mm_ in range(4):
            c = 4 * s + mm_
            kc, cgb, cfree = cg.take()
            kz, zzb, zfree = zz.take()
            ko, zcb, ofree = zc.take()
            parts = []
            for job in (jc, jv):
                for hf in range(2):
                    k, bank, free = banks.take()
                    p = P.mm([(bank[:, 0:N2], job.ap[:, i, 128 * mm_:128 * mm_ + 128], hT[:, i, N2 * hf:N2 * hf + N2], i == 0, i == 7)
                              for i in range(8)], free, h_t, job.tok)
                    parts.append((k, bank, p))
                job.release = [p]
            zt = []
            for hf in range(2):
                k, bank, p = parts[hf]
                a = P.acp(cgb[:, N2 * hf:N2 * hf + N2], bank[:, 0:N2], p, cfree)
                banks.free[k] = a
                k, bank, p = parts[2 + hf]
                zt.append(P.tt(zzb[:, N2 * hf:N2 * hf + N2], cgb[:, N2 * hf:N2 * hf + N2], bank[:, 0:N2], MUL, a, p, zfree))
                banks.free[k] = zt[-1]
            cg.free[kc] = zt
            a = P.ts(zcb, zzb[:, 0:512], w3[:, c:c + 1], None, MUL, None, zt, ofree)
            for j in (1, 2):
                a = P.stt(zcb, zzb[:, j:j + 512], w3[:, 8 * j + c:8 * j + c + 1], zcb, MUL, ADD, a)
            zz.free[kz] = a
            k, bank, free = banks.take()
            p = P.mm([(bank[:, :], jb.ap[:, i, 128 * mm_:128 * mm_ + 128], hT[:, i, 2:514], i == 0, i == 7) for i in range(8)], free, jb.tok)
            v = P.tt(z[:, c, :], zcb, bank[:, :], MUL, a, p)
            jb.release = [p]
            banks.free[k] = zc.free[ko] = v
            z_t.append(v)
    tiles = [(x2[:, t, :], 128, 128 * t) for t in range(4)]
    w = residual(z, z_t, tiles)
    R = P.region(inner, P.top)
    g, b = R.take(1024), R.take(1024)
    lt = [P.row_load(g, A["ln_g_2"][1, 0], w), P.row_load(b, A["ln_b_2"][1, 0], w)]
    w = [layer_norm(P, x, n, g, b, w[i], lt) for i, (x, n, _) in enumerate(tiles)]
    w = moe(P, 1, x2, meta, tiles, w, banks, inner, hD, yD, tab[1], zr)
    s = DmaSem(P.sem("out"))
    for t in range(4):
        s.add()
        P.ac.dma((lambda t: lambda e: e.dma_start(P.out[0, 128 * t:128 * t + 128, :], x2[:, t, :]))(t), s.sem, w[t])
    P.ac.wait((s.sem, s.n))


def moe(P, l, x2, meta, tiles, toks, banks, inner, hD, yD, tab, zr):
    A, nc = P.A, P.nc
    nt = len(tiles)
    R = P.region(inner, P.top)
    idx = R.take(NTAB).bitcast(I32)
    ovi = R.take(32).bitcast(I32)
    posi = [R.take(8).bitcast(I32) for _ in range(4)]
    tki = R.take(8).bitcast(I32)
    gates = [R.take(8) for _ in range(2)]
    xg = Slots([R.take(1024) for _ in range(2)])
    xT = Slots([three(R.take(1024), 8) for _ in range(2)])
    hs = Slots([[R.take(256) for _ in range(3)] for _ in range(2)])
    yb = Slots([R.take(512) for _ in range(2)])
    tail = R.o
    ow = R.take(3 * SLOT)
    Rt = P.region(tail, tail + 3 * SLOT)
    hT = Rt.take(8 * 528).rearrange("p (a b) -> p a b", a=8)
    rw = three(Rt.take(288), 8)
    zrow = Rt.take(1024)
    sm = [Rt.take(8) for _ in range(26)]
    lg = three(Rt.take(nt * 36), nt)
    wide = [three(Rt.take(nt * 32), nt) for _ in range(6)]
    e32 = [Rt.take(32) for _ in range(6)]
    ov = Rt.take(512)
    ovx = Rt.take(32)
    fill = Rt.take(NTAB).bitcast(I32)
    before = [toks] + [q.last() for q in (P.pe, P.ac, P.dv, P.po)]
    npad = T + 16

    hsem = DmaSem(P.sem("rows"))
    zt = P.dv.op(lambda e: e.memset(zrow[0:1, :], 0.0), before)
    ft = P.dv.op(lambda e: e.memset(fill, npad), before)
    for i, (x, n, _) in enumerate(tiles):
        hw = hsem.add()
        P.ac.dma((lambda i, x, n: lambda e: e.dma_start(hD[128 * i:128 * i + n, :], x))(i, x, n), hsem.sem, toks[i])
    hw = hsem.add()
    P.ac.dma(lambda e: e.dma_start(hD[npad:npad + 1, :], zrow[0:1, :]), hsem.sem, zt)
    fsem = DmaSem(P.sem("fill"))
    fw = fsem.add()
    P.ac.dma(lambda e: e.dma_start(tab.rearrange("(p c) o -> p (c o)", p=128), fill), fsem.sem, ft)
    rt = P.load(P.ac, rw, A["router"][l].rearrange("(c p) n -> p c n", p=128), before)

    h_t = []
    for c in range(8):
        k, bank, free = banks.take()
        p = P.tr([(bank[:, 128 * t:128 * t + 128], x2[:, t, 128 * c:128 * c + 128]) for t in range(4)], before, free)
        h_t.append((P.acp if c % 2 else P.cp)(hT[:, c, 0:512], bank[:, :], p, before))
        banks.free[k] = h_t[-1]
    if nt == 5:
        k, bank, free = banks.take()
        p = P.tr([(bank[:, 16 * c:16 * c + 16], meta[0:16, 128 * c:128 * c + 128]) for c in range(8)], free)
        h_t.append(P.cp(hT[:, :, 512:528], three(bank[:, 0:128], 8), p, before))
        banks.free[k] = h_t[-1]
    k, bank, free = banks.take()
    for t in range(nt):
        n = tiles[t][1]
        p = P.mm([(bank[0:n, 36 * t:36 * t + 36], hT[:, c, 128 * t:128 * t + n], rw[:, c, :], c == 0, c == 7) for c in range(8)], h_t, rt, free)
    zl = P.dv.op(lambda e: e.memset(lg, 0.0), before)
    o, _ = RAT["moe_b_group_2"]
    bg = P.row_sb[:, o + 4 * l:o + 4 * l + 4]
    o, _ = RAT["moe_b_expert_2"]
    be = P.row_sb[:, o + 32 * l:o + 32 * l + 32]
    a = []
    for n, t0, t1 in ((128, 0, 4), (16, 4, 5))[0:1 if nt == 4 else 2]:
        src = three(bank[0:n, 36 * t0:36 * t1], t1 - t0)
        for b_, c0, c1 in ((bg, 0, 4), (be, 4, 36)):
            a.append(P.tt(lg[0:n, t0:t1, c0:c1], src[:, :, c0:c1], b_[0:n, :].unsqueeze(1).to_broadcast([n, t1 - t0, c1 - c0]), ADD, p, zl))
    banks.free[k] = a[-1]
    k4 = lambda x: x[:, 0:nt]
    gl, el = lg[:, :, 0:4], lg[:, :, 4:36]
    S = [k4(x) for x in sm]
    W4 = [x[:, :, 0:4] for x in wide]

    def bc(x, n):
        return x.unsqueeze(2).to_broadcast([128, nt, n])

    gid = P.cst("gid")[:, 0:4].unsqueeze(1).to_broadcast([128, nt, 4])
    eid = P.cst("eid").unsqueeze(1).to_broadcast([128, nt, 32])

    def first_max(v, val, n, ids, tmp, idx_out, hot, w):
        a = P.red(val, v, MAX, w)
        a = P.tt(tmp, v, bc(val, n), ISEQ, a)
        a = P.ts(tmp, tmp, -100.0, 100.0, MUL, ADD, a)
        a = P.tt(tmp, tmp, ids, ADD, a)
        a = P.red(idx_out, tmp, MIN, a)
        return P.tt(hot, ids, bc(idx_out, n), ISEQ, a)

    a = first_max(gl, S[0], 4, gid, W4[0], S[1], W4[1], a)
    b = P.tt(W4[2], gl, bc(S[0], 4), SUB, a)
    b = P.act(W4[2], W4[2], ACT.Exp, b)
    b = P.red(S[2], W4[2], ADD, b)
    pg_t = P.recip(S[2], S[2], b)
    b = P.ts(W4[1], W4[1], 1.0, 1e30, SUB, MUL, a)
    elm, oh1, oh2, cb, t1, t2 = wide[3], wide[4], wide[5], wide[0], wide[1], wide[2]
    a = P.tt(elm.rearrange("p t (g e) -> p t g e", g=4), el.rearrange("p t (g e) -> p t g e", g=4),
             W4[1].unsqueeze(3).to_broadcast([128, nt, 4, 8]), ADD, b)
    a = first_max(elm, S[3], 32, eid, t2, S[4], oh1, a)
    a = P.stt(elm, oh1, -2e30, elm, MUL, ADD, a)
    a = first_max(elm, S[5], 32, eid, t2, S[6], oh2, a)
    b = P.tt(S[7], S[5], S[3], SUB, a)
    b = P.act(S[7], S[7], ACT.Exp, b)
    c = P.ts(S[8], S[7], 1.0, None, ADD, None, b)
    c = P.recip(S[8], S[8], c)
    c = P.tt(gates[0][:, 0:nt], S[8], S[2], MUL, c, pg_t)
    g_t = P.tt(gates[1][:, 0:nt], gates[0][:, 0:nt], S[7], MUL, c)
    M = elm
    m = P.tt(M, oh1, oh2, ADD, a)
    if nt == 5:
        m = [m, P.tt(M[:, 4, :], M[:, 4, :], P.cst("first16"), MUL, m)]
    k, bank, free = banks.take()
    strict, ones = P.cst("strict"), P.cst("ones")
    for t in range(nt):
        p = P.mm([(bank[:, 32 * t:32 * t + 32], strict, M[:, t, :], True, t == 0)]
                 + [(bank[:, 32 * t:32 * t + 32], ones, M[:, s, :], False, s == t - 1) for s in range(t)], m, free)
    p = P.mm([(bank[:, 256:288], ones, M[:, s, :], s == 0, s == nt - 1) for s in range(nt)])
    cnt, nb, inc, exc = e32[0:4]
    cb_t = P.cp(cb, three(bank[:, 0:32 * nt], nt), p, a)
    cn_t = P.cp(cnt, bank[:, 256:288], p)
    banks.free[k] = cn_t
    a = P.ts(nb, cnt, 64.0, None, ISGT, None, cn_t)
    for q in range(2, 9):
        a = P.stt(nb, cnt, 64.0 * q, nb, ISGT, ADD, a)
    b = P.dv.op(lambda e: e.tensor_tensor_scan(inc, nb, P.cst("zero")[:, 0:32], 0.0, ADD, ADD), a)
    c = P.tt(exc, inc, nb, SUB, b)
    o3 = three(ov, 16)
    d = P.tt(o3, inc.unsqueeze(1).to_broadcast([128, 16, 32]), P.cst("eid")[:, 0:16].unsqueeze(2).to_broadcast([128, 16, 32]), ALU.is_le, b)
    d = P.red(ovx[:, 0:16], o3, ADD, d)
    d = P.ts(ovx[:, 0:16], ovx[:, 0:16], 31.0, None, MIN, None, d)
    d = P.cp(ovi[:, 0:16], ovx[:, 0:16], d)
    ov_t = P.cp(ovi[:, 16:17], inc[:, 31:32], d)
    excb = exc.unsqueeze(1).to_broadcast([128, nt, 32])
    hb_ = P.cst("hbase").unsqueeze(1).to_broadcast([128, nt, 32])
    tok = []
    scat = []
    tk_t = P.cp(tki[:, 0:nt], P.cst("tok")[:, 0:nt], before)
    for j, (oh, ei) in enumerate(((oh1, S[4]), (oh2, S[6]))):
        rank, ob, hbv, blk, pos, first, ad = (S[9 + 8 * j + q] for q in range(7))
        a = P.tt(t1, oh, cb, MUL, cb_t, tok)
        a = P.red(rank, t1, ADD, a)
        b = P.tt(t2, oh, excb, MUL, c, tok)
        b = P.red(ob, t2, ADD, b)
        x = P.tt(t1, oh, hb_, MUL, a)
        x = P.red(hbv, t1, ADD, x)
        a = P.ts(blk, rank, 64.0, None, ISGE, None, a)
        for q in range(2, 9):
            a = P.stt(blk, rank, 64.0 * q, blk, ISGE, ADD, a)
        y = P.stt(pos, blk, -64.0, rank, MUL, ADD, a)
        fst = P.ts(first, blk, 0.0, None, ISEQ, None, a)
        o_ = P.stt(ob, ob, -1.0, blk, ADD, ADD, b, a)
        q1 = P.ts(ad, ob, 16.0, None, ADD, None, o_)
        q1 = P.tt(hbv, hbv, ad, SUB, q1, x)
        q1 = P.tt(hbv, hbv, first, MUL, q1, fst)
        q1 = P.tt(hbv, hbv, ad, ADD, q1)
        q1 = P.stt(hbv, pos, float(NTAB), hbv, MUL, ADD, q1, y)
        q1 = P.cp(posi[j][:, 0:nt], hbv, q1)
        q2 = P.ts(ad, ob, 32.0, None, ADD, None, q1)
        q2 = P.tt(rank, ei, ad, SUB, q2, y)
        q2 = P.tt(rank, rank, first, MUL, q2)
        q2 = P.tt(rank, rank, ad, ADD, q2)
        q2 = P.stt(rank, rank, 64.0, pos, MUL, ADD, q2)
        q2 = P.cp(posi[2 + j][:, 0:nt], rank, q2)
        tok = [q1, q2]
        for t, (_, n, _) in enumerate(tiles):
            scat.append((j, t, n))
    ssem = DmaSem(P.sem("scatter"))
    P.po.wait(fw, tok, tk_t)
    for j, t, n in scat:
        sw = ssem.add()
        P.po.dma((lambda j, t, n: lambda e: e.indirect_dma_start(
            out=tab, out_offset=bass.IndirectOffsetOnAxis(ap=posi[j][0:n, t:t + 1], axis=0),
            in_=tki[0:n, t:t + 1], in_offset=None, bounds_check=128 * NTAB - 1, oob_is_err=False))(j, t, n), ssem.sem)
    it = P.load(P.po, idx, tab.rearrange("(p c) o -> p (c o)", p=128), sw)
    routed = [it, hw]
    P.po.wait(hw)

    gsem = [P.sem("gather") for _ in range(2)]
    ysem = [P.sem("ystore") for _ in range(2)]

    def gather(q, buf, n, col, sem, *w):
        q.dma(lambda e: e.indirect_dma_start(out=buf[0:n, :], out_offset=None, in_=hD,
                                             in_offset=bass.IndirectOffsetOnAxis(ap=idx[0:n, col:col + 1], axis=0),
                                             bounds_check=T + 16, oob_is_err=False), sem, *w)

    def turn(xb, xt, n, w, wx):
        out = []
        for g in range(2):
            k, bank, free = banks.take()
            p = P.tr([(bank[:, n * c:n * c + n], xb[0:n, 512 * g + 128 * c:512 * g + 128 * c + 128]) for c in range(4)], w, free)
            dst, src = xt[:, 4 * g:4 * g + 4, 0:n], three(bank[:, 0:4 * n], 4)
            out.append(P.acp(dst, src, p, wx) if g else P.cp(dst, src, p, wx))
            banks.free[k] = out[-1]
        return out

    def up(gu, xt, x0, w):
        k, bank, free = banks.take()
        grp = []
        for c in range(8):
            for hf in range(2):
                grp.append((bank[64 * hf:64 * hf + 64, :], xt[:, c, x0:x0 + 64], gu[:, :, 512 * c + 256 * hf:512 * c + 256 * hf + 256], c == 0, c == 7))
        p = P.mm(grp, free, w)
        kh, (s, h, ht), hfree = hs.take()
        a = P.act(s, bank[:, 0:256], ACT.Silu, p, hfree)
        b = P.tt(h, s, bank[:, 256:512], MUL, a)
        banks.free[k] = b
        return p, kh, h, ht, b

    def down(kh, h, ht, b, dw, w):
        k, bank, free = banks.take()
        p = P.tr([(bank[:, 128 * j:128 * j + 128], h[:, 128 * j:128 * j + 128]) for j in range(2)], b, free)
        e = P.cp(ht, bank[:, 0:256], p)
        banks.free[k] = e
        k, bank, free = banks.take()
        grp = []
        for c in range(4):
            lhs = ht[:, 128 * (c % 2) + 64 * (c // 2):128 * (c % 2) + 64 * (c // 2) + 64]
            for hf in range(2):
                grp.append((bank[64 * hf:64 * hf + 64, :], lhs, dw[:, c, 512 * hf:512 * hf + 512], c == 0, c == 3))
        q = P.mm(grp, e, free, w)
        hs.free[kh] = q
        ky, y, yfree = yb.take()
        a = P.acp(y, bank[:, :], q, yfree)
        banks.free[k] = a
        return q, a, ky, y

    ycount = [0, 0]
    ylast = {}

    def store(e, a, ky, y):
        for hf in range(2):
            P.ac.dma((lambda hf: lambda en: en.dma_start(yD[64 * e:64 * e + 64, 512 * hf:512 * hf + 512], y[64 * hf:64 * hf + 64, :]))(hf), ysem[ky], a)
            ycount[ky] += 16
        yb.free[ky] = (ysem[ky], ycount[ky])

    gcount = [0, 0]
    xbuf = {}
    gath = {}

    def start_gather(c):
        k, xb, free = xg.take()
        gather(P.po, xb, 128, c, gsem[k], it, hw, free)
        gcount[k] += 16
        gath[c] = (k, xb, (gsem[k], gcount[k]))

    start_gather(0)
    start_gather(1)
    pend = None
    for c in range(16):
        k, xb, gtok = gath[c]
        kx, xt, xfree = xT.take()
        x_t = turn(xb, xt, 128, gtok, xfree)
        xg.free[k] = x_t
        if c + 2 < 16:
            start_gather(c + 2)
        for par in range(2):
            jg, ju, jd = P.loads.take(), P.loads.take(), P.loads.take()
            s0 = P.ring.index(jg.slot)
            gu = P.big[:, SLOT * s0:SLOT * s0 + 2 * SLOT].rearrange("p (s n) -> p s n", s=2)
            r = up(gu, xt, 64 * par, [x_t, jg.tok, ju.tok])
            jg.release = ju.release = [r[0]]
            if pend is not None:
                e0, jd0, r0 = pend
                q, a, ky, y = down(*r0[1:], jd0.ap, jd0.tok)
                jd0.release = [q]
                store(e0, a, ky, y)
            pend = (2 * c + par, jd, r)
        xT.free[kx] = r[0]
    e0, jd0, r0 = pend
    q, a, ky, y = down(*r0[1:], jd0.ap, jd0.tok)
    jd0.release = [q]
    store(e0, a, ky, y)
    ydone = [(ysem[k], ycount[k]) for k in range(2)]
    main_done = [x.last() for x in (P.pe, P.ac, P.dv, P.po)] + ydone + [zr]

    real = (P.pe, P.ac, P.dv, P.po)
    P.pe, P.ac, P.dv, P.po = (Queue(P.sem("ovf")) for _ in range(4))
    osp = Queue(P.sem("ovf"))
    queues = {"pe": (real[0], P.pe), "ac": (real[1], P.ac), "dv": (real[2], P.dv), "po": (real[3], P.po), "sp": (None, osp)}
    marks = {n: [0] for n in queues}
    banks_keep = banks.free
    for s in (banks, hs, yb, xT, xg):
        s.free = [None] * len(s.items)
    wsem = [P.sem("ow") for _ in range(2)]
    gs, ys = [P.sem("ogather") for _ in range(2)], P.sem("oystore")
    gu = ow[:, 0:2 * SLOT].rearrange("p (s n) -> p s n", s=2)
    dw = three(ow[:, 2 * SLOT:3 * SLOT], 4)
    gu_free = dw_free = main_done
    yn = 0
    for i in range(NOVF):
        for q in (P.pe, P.ac, P.dv, P.po, osp):
            q.wait(main_done)
        regs = {}
        osp.items.append(("read", regs, ovi[0:1, i:i + 1]))
        for s, name in enumerate(("moe_w_gate_2", "moe_w_up_2")):
            osp.dma((lambda s, w, regs: lambda e: e.dma_start(three(gu[:, s, :], 8), w[l, bass.ds(regs["v"], 1)].rearrange("o (c p) n -> p (o c) n", p=128)))(s, A[name], regs),
                    wsem[0], gu_free)
        osp.dma((lambda w, regs: lambda e: e.dma_start(dw, w[l, bass.ds(regs["v"], 1)].rearrange("o (c p) n -> p (o c) n", p=128)))(A["moe_w_down_2"], regs),
                wsem[1], dw_free)
        k, xb, free = xg.take()
        gather(P.po, xb, 64, 16 + i, gs[k], free)
        kx, xt, xfree = xT.take()
        x_t = turn(xb, xt, 64, (gs[k], 16 * (i // 2 + 1)), xfree)
        xg.free[k] = x_t
        r = up(gu, xt, 0, [x_t, (wsem[0], 32 * (i + 1))])
        xT.free[kx] = gu_free = [r[0]]
        q, a, ky, y = down(*r[1:], dw, (wsem[1], 16 * (i + 1)))
        dw_free = [q]
        for hf in range(2):
            P.ac.dma((lambda hf, i, y: lambda en: en.dma_start(yD[64 * (NEXP + i):64 * (NEXP + i) + 64, 512 * hf:512 * hf + 512], y[64 * hf:64 * hf + 64, :]))(hf, i, y), ys, a)
            yn += 16
        P.ac.wait((ys, yn))
        yb.free[ky] = (ys, yn)
        for n, (_, q) in queues.items():
            marks[n].append(len(q.items))
    P.pe, P.ac, P.dv, P.po = real
    for n, (main, q) in queues.items():
        sec = [("tok", ov_t), ("count", {}, ovi[0:1, 16:17])]
        count = sec[1][1]
        for i in range(NOVF):
            sec.append(("when", (lambda count, i: lambda e: count["v"] > i)(count, i), q.items[marks[n][i]:marks[n][i + 1]]))
        if main is None:
            P.sp_sections.append(sec)
        else:
            main.items += sec
            main.seen = {}
    done = P.act(stat_of(P), stat_of(P), ACT.Copy, main_done)
    for q in (P.pe, P.dv, P.po):
        q.wait(done)
    banks.free = [done] * 8
    for s in (hs, yb, xT, xg):
        s.free = [done] * len(s.items)

    Rt = P.region(tail, tail + 3 * SLOT)
    g, b = Rt.take(1024), Rt.take(1024)
    lt = [P.row_load(g, A["ln_g_2"][l, 1], done), P.row_load(b, A["ln_b_2"][l, 1], done)]
    yy = Slots([Rt.take(1024) for _ in range(6)])
    out = []
    for t, (x, n, _) in enumerate(tiles):
        w = None
        for j in range(2):
            k, buf, free = yy.take()
            s = P.sem("back")
            P.po.dma((lambda buf, n, j, t: lambda e: e.indirect_dma_start(
                out=buf[0:n, :], out_offset=None, in_=yD, in_offset=bass.IndirectOffsetOnAxis(ap=posi[2 + j][0:n, t:t + 1], axis=0),
                bounds_check=64 * (NEXP + NOVF) - 1, oob_is_err=False))(buf, n, j, t), s, done, free)
            if j == 0:
                w = P.ts(x, x, ALPHA, None, MUL, None, done)
            w = P.stt(x, buf[0:n, :], gates[j][0:n, t:t + 1], x, MUL, ADD, w, (s, 16), g_t)
            yy.free[k] = w
        out.append(layer_norm(P, x, n, g, b, w, lt))
    return out


def stat_of(P):
    return P.lnst.items[4][0:1, 15:16]


def columns(a, n):
    return np.ascontiguousarray(a).reshape(-1, 128).T


def laid_out(inputs):
    x = {k: np.ascontiguousarray(v) for k, v in inputs.items()}
    vecs = np.concatenate([columns(x[k], n) for k, n in VECS], 1)
    rows = np.concatenate([x[k].reshape(-1) for k, _ in ROWS])
    tables, _ = shape_tables()
    wa = np.zeros((2, 128, 8, 128), np.float32)
    for i, k in enumerate(("lru_w_a_2", "lru_w_i_2")):
        for h in range(16):
            wa[i, 64 * (h % 2):64 * (h % 2) + 64, h // 2, 64 * (h % 2):64 * (h % 2) + 64] = x[k][0, h]
    router = np.concatenate([x["moe_w_group_2"], x["moe_w_expert_2"]], 2)
    keep = ["x", "w_in", "rwkv_w_up", "rwkv_a_up", "rwkv_g_up", "w_branch", "w_out", "norm_mix_post", "norm_ffn_post",
            "ffn_w_gate", "ffn_w_up", "ffn_w_down", "meta_tokens_2", "lru_w_in_2", "lru_w_out_2", "sc_w_in_2", "sc_w_out_2",
            "moe_w_gate_2", "moe_w_up_2", "moe_w_down_2", "ln_g_2", "ln_b_2"]
    arrays = {k: x[k] for k in keep}
    arrays.update(vecs=np.ascontiguousarray(vecs), rows=np.ascontiguousarray(rows), tables=tables, lru_gates=wa,
                  router=np.ascontiguousarray(router))
    return arrays


def kernel(**inputs):
    import concourse.bacc as bacc
    from concourse.bass_utils import run_bass_kernel_spmd

    arrays = laid_out(inputs)
    _, cat = shape_tables()
    nc = bacc.Bacc("TRN2", target_bir_lowering=False, num_devices=1)
    aps = {k: nc.dram_tensor("in_" + k, a.shape, mybir.dt.from_np(a.dtype), kind="ExternalInput").ap() for k, a in arrays.items()}
    out = nc.dram_tensor("out_x", (1, T, D), F32, kind="ExternalOutput").ap()
    program(nc, aps, out, cat, arrays["tables"].shape[1])
    r = run_bass_kernel_spmd(nc, [{"in_" + k: a for k, a in arrays.items()}], core_ids=[0])
    return r.results[0]["out_x"]
```

```python
import numpy as np
import concourse.bass as bass
import concourse.mybir as mybir
from concourse.alu_op_type import AluOpType as ALU
from contextlib import ExitStack

F32 = mybir.dt.float32
I32 = mybir.dt.int32
ACT = mybir.ActivationFunctionType
AX = mybir.AxisListType.X
MUL, ADD, SUB, MAX, MIN = ALU.mult, ALU.add, ALU.subtract, ALU.max, ALU.min
ISEQ, ISGE, ISGT, ISLT = ALU.is_equal, ALU.is_ge, ALU.is_gt, ALU.is_lt

T = 512
D = 1024
NEXP = 32
FF = 2816
CAP = 64
NOVF = 16


class Queue:

    def __init__(self, sem):
        self.sem, self.n, self.items, self.seen = sem, 0, [], {}

    def wait(self, *toks):
        for t in toks:
            if t is None:
                continue
            if isinstance(t, list):
                self.wait(*t)
                continue
            sem, val = t
            if not val:
                continue
            if self.seen.get(id(sem), 0) >= val:
                continue
            self.seen[id(sem)] = val
            self.items.append(("wait", sem, val))

    def op(self, fn, *toks):
        self.wait(*toks)
        self.n += 1
        self.items.append(("op", fn, self.sem, 1))
        return self.sem, self.n

    def said(self, *toks):
        self.wait(*toks)
        self.n += 1
        self.items.append(("inc", self.sem))
        return self.sem, self.n

    def quiet(self, fn, *toks):
        self.wait(*toks)
        self.items.append(("op", fn, None, 0))

    def dma(self, fn, sem, *toks):
        self.wait(*toks)
        self.items.append(("op", fn, sem, 16))

    def open(self):
        self.at = len(self.items), self.n, dict(self.seen)

    def close(self, cond, dmas=()):
        i, n, self.seen = self.at
        body, self.items = self.items[i:], self.items[:i]
        self.items.append(("either", cond, body, [(self.sem, n)], [(self.sem, self.n - n)] + list(dmas)))

    def last(self):
        return (self.sem, self.n) if self.n else None

    def emit(self, eng, items=None):
        for it in self.items if items is None else items:
            if it[0] == "wait":
                eng.wait_ge(it[1], it[2])
            elif it[0] == "late":
                for sem, val in it[1]():
                    eng.wait_ge(sem, val)
            elif it[0] == "tok":
                eng.wait_ge(*it[1])
            elif it[0] in ("read", "count"):
                it[1]["v"] = eng.value_load(it[2], min_val=0, max_val=it[3])
            elif it[0] == "when":
                with eng.If(it[1](eng)):
                    self.emit(eng, it[2])
            elif it[0] == "inc":
                eng.sem_inc(it[1], 1)
            elif it[0] == "either":
                with eng.If(it[1](eng)):
                    self.emit(eng, it[2])
                with eng.Else():
                    for sem, val in it[3]:
                        if val:
                            eng.wait_ge(sem, val)
                    for sem, val in it[4]:
                        if val:
                            eng.sem_inc(sem, val)
            else:
                ins = it[1](eng)
                if it[2] is not None:
                    ins.then_inc(it[2], it[3])


class Slots:

    def __init__(self, items):
        self.items, self.free, self.i = items, [None] * len(items), 0

    def take(self):
        k = self.i % len(self.items)
        self.i += 1
        return k, self.items[k], self.free[k]


class DmaSem:

    def __init__(self, sem):
        self.sem, self.n = sem, 0

    def add(self):
        self.n += 16
        return self.sem, self.n
SLOT = 4096
NBIG = 53200


def alibi(n):
    return [float(np.float32(2.0 ** (-8.0 * k / n))) for k in range(1, n + 1)]


def shape_tables():
    q = np.arange(128)[:, None]
    c = np.arange(128)[None, :]
    parts = [("ident", np.eye(128)), ("ones", np.ones((128, 128))), ("zero", np.zeros((128, 128))),
             ("headones", (q // 64) == (c // 64)), ("mean256", np.full((128, 128), 1.0 / 256))]
    for b in range(7):
        w = 1 << b
        parts.append((f"lev{b}", ((q >> (b + 1)) == (c >> (b + 1))) & ((q & w) != 0) & ((c & w) == 0)))
    parts.append(("strict", q < c))
    parts.append(("incl", q <= c))
    parts.append(("headsel", np.concatenate([q < 64, q >= 64], 1)))
    parts.append(("neghalf", np.full((128, 16), -0.5)))
    parts.append(("poshalf", np.full((128, 2), 0.5)))
    parts.append(("eps", np.full((128, 2), 1e-5)))
    parts.append(("eid", np.broadcast_to(np.arange(32) - 100, (128, 32))))
    parts.append(("gid", np.broadcast_to(np.arange(8) - 100, (128, 8))))
    tok = q + 128 * np.arange(8)[None, :]
    parts.append(("tok", np.where(tok < T + 16, tok - (T + 16), 0)))
    parts.append(("iota", np.broadcast_to(c, (128, 128))))
    parts.append(("thr", np.broadcast_to(CAP * np.arange(1, 9), (128, 8))))
    parts.append(("bit", np.broadcast_to(2.0 ** (np.arange(32) % 16), (128, 32))))
    parts.append(("first16", np.broadcast_to(q < 16, (128, 32))))
    c5 = np.arange(512)[None, :]
    rel = 384 + q - c5
    far = 3e32
    parts.append(("rdf", np.where(rel >= 0, rel, far)))
    parts.append(("rd1", np.where((rel >= 0) & (rel % 4 == 0), rel, far)))
    parts.append(("rd2", np.where((rel >= 0) & (rel % 16 == 0), rel, far)))
    c2 = np.arange(256)[None, :]
    rel = 128 + q - c2
    parts.append(("rd0", np.where((rel >= 0) & (rel <= 128), rel, far)))
    at, cols = {}, 0
    for name, a in parts:
        at[name] = (cols, a.shape[1])
        cols += a.shape[1]
    table = np.concatenate([np.asarray(a, np.float32) for _, a in parts], 1)
    return np.ascontiguousarray(table), at


VECS = [("norm_mix_pre", 8), ("norm_ffn_pre", 8), ("gate_bias", 32), ("rwkv_mu", 8), ("rwkv_w0", 2), ("rwkv_a0", 2),
        ("rwkv_k_k", 2), ("rwkv_k_a", 2), ("rwkv_r_k", 2), ("conv_dw_w", 62), ("conv_dw_b", 2), ("conv_ln_g", 2),
        ("conv_ln_b", 2), ("lru_conv_w_2", 32), ("lru_conv_b_2", 8), ("lru_b_a_2", 8), ("lru_b_i_2", 8),
        ("lru_lambda_2", 8), ("sc_conv_w_2", 24)]
ROWS = [("rwkv_ln_g", 256), ("rwkv_ln_b", 256), ("diff_subln_g", 64), ("diff_lam_q1", 32), ("diff_lam_k1", 32),
        ("diff_lam_q2", 32), ("diff_lam_k2", 32), ("moe_bias", 72)]


def places(spec):
    at, n = {}, 0
    for name, w in spec:
        at[name] = (n, w)
        n += w
    return at, n


VAT, NVEC = places(VECS)
RAT, NROW = places(ROWS)


class Program:
    def __init__(self, nc, ctx, A, out):
        self.nc, self.ctx, self.A, self.out = nc, ctx, A, out
        self.big = ctx.enter_context(nc.sbuf_tensor("big", [128, NBIG], F32))
        self.ps = [ctx.enter_context(nc.psum_tensor(f"ps{k}", [128, 512], F32)) for k in range(8)]
        self.nsem = 0
        self.pe, self.ac, self.dv, self.po, self.sp = (Queue(self.sem(n)) for n in ("pe", "act", "dve", "pool", "sp"))

    def sem(self, name):
        self.nsem += 1
        return self.ctx.enter_context(self.nc.semaphore(f"{name}_{self.nsem}"))

    def tt(self, out, a, b, op, *w):
        return self.dv.op(lambda e: e.tensor_tensor(out, a, b, op), *w)

    def ptt(self, out, a, b, op, *w):
        return self.po.op(lambda e: e.tensor_tensor(out, a, b, op), *w)

    def ts(self, out, a, s1, s2, op0, op1, *w):
        if s2 is None:
            return self.dv.op(lambda e: e.tensor_scalar(out, a, s1, None, op0), *w)
        return self.dv.op(lambda e: e.tensor_scalar(out, a, s1, s2, op0, op1), *w)

    def stt(self, out, a, s, b, op0, op1, *w):
        return self.dv.op(lambda e: e.scalar_tensor_tensor(out, a, s, b, op0, op1), *w)

    def cp(self, out, a, *w):
        return self.dv.op(lambda e: e.tensor_copy(out, a), *w)

    def red(self, out, a, op, *w):
        return self.dv.op(lambda e: e.tensor_reduce(out, a, AX, op), *w)

    def recip(self, out, a, *w):
        return self.dv.op(lambda e: e.reciprocal(out, a), *w)

    def act(self, out, a, func, *w, bias=0.0, scale=1.0, accum=None):
        if accum is not None:
            return self.ac.op(lambda e: e.activation(out, a, func, bias=bias, scale=scale, accum_out=accum), *w)
        return self.ac.op(lambda e: e.activation(out, a, func, bias=bias, scale=scale), *w)

    def acp(self, out, a, *w, scale=1.0):
        return self.ac.op(lambda e: e.activation(out, a, ACT.Copy, scale=scale), *w)

    def mm(self, group, *w):
        self.pe.wait(*w)
        for k, (o, l, r, s, t) in enumerate(group):
            f = (lambda o, l, r, s, t: lambda e: e.matmul(o, l, r, start=s, stop=t, skip_group_check=True))(o, l, r, s, t)
            if k == len(group) - 1:
                return self.pe.op(f)
            self.pe.quiet(f)

    def tr(self, group, *w):
        self.pe.wait(*w)
        for k, (o, i) in enumerate(group):
            f = (lambda o, i, d: lambda e: e.transpose(o, i, d))(o, i, self.ident[0:i.shape[0], 0:i.shape[0]])
            if k == len(group) - 1:
                return self.pe.op(f)
            self.pe.quiet(f)

    def rstd(self, dst, src, scale, eps, *w):
        a = self.ts(dst, src, scale, eps, MUL, ADD, *w)
        n = dst.shape[1]
        return self.ptt(dst, dst, self.cst("neghalf")[:, 0:n], ALU.pow, a)

    def load(self, q, dst, src, *w):
        s = DmaSem(self.sem("ld"))
        t = s.add()
        q.dma(lambda e: e.dma_start(dst, src), s.sem, *w)
        return t

    def cst(self, name):
        o, n = self.cat[name]
        return self.cst_sb[:, o:o + n]

    def vec(self, name, k=0, n=1):
        o, _ = VAT[name]
        return self.vec_sb[:, o + k:o + k + n]

    def row(self, name):
        o, n = RAT[name]
        return self.row_sb[:, o:o + n]

    def region(self, lo, hi):
        return Region(self.big, lo, hi)

    def row_load(self, dst, src, *w):
        return self.load(self.ac, dst, src.partition_broadcast(128), *w)

class Region:
    def __init__(self, big, lo, hi):
        self.big, self.o, self.hi = big, lo, hi

    def take(self, n):
        assert self.o + n <= self.hi, (self.o, n, self.hi)
        a = self.big[:, self.o:self.o + n]
        self.o += n
        return a


class Slot:
    def __init__(self, ap, sem):
        self.ap, self.sem, self.n, self.prev, self.gate = ap, sem, 0, None, []


class Job:
    def __init__(self, slot, prev):
        self.slot, self.prev, self.release = slot, prev, []
        slot.n += 16
        self.tok = (slot.sem, slot.n)

    def before(self):
        return self.slot.gate if self.prev is None else self.prev.release


class Loads:

    def __init__(self, P):
        self.P, self.jobs, self.at, self.turn = P, [], 0, {}

    def plan(self, group, dst, src):
        k = self.turn.get(id(group), 0)
        self.turn[id(group)] = k + 1
        slot = group[k % len(group)]
        job = Job(slot, slot.prev)
        slot.prev = job
        job.ap = dst(slot.ap)
        self.jobs.append(job)
        ap = job.ap
        self.P.sp.items.append(("late", lambda: _flat(job.before())))
        self.P.sp.dma(lambda e: e.dma_start(ap, src), slot.sem)

    def take(self):
        self.at += 1
        return self.jobs[self.at - 1]


def _flat(toks):
    out = []
    for t in toks:
        if isinstance(t, list):
            out += _flat(t)
        elif t is not None:
            out.append(t)
    return out


def rounds(*tasks):
    live = list(tasks)
    while live:
        for t in list(live):
            for _ in range(t[1]):
                try:
                    next(t[0])
                except StopIteration:
                    live.remove(t)
                    break


def three(ap, a):
    return ap.rearrange("p (a b) -> p a b", a=a)


def plan_block1(P):
    A, L = P.A, P.loads
    two = P.ring[0:2]
    w_in = A["w_in"][0].rearrange("(c p) n -> p c n", p=128)
    wb = A["w_branch"][0]

    def cols(c0, n=512):
        L.plan(two, lambda s: three(s[:, 0:8 * n], 8), w_in[:, :, c0:c0 + n])

    def branch(n):
        L.plan(P.wbr_slots, lambda s: three(s, 2), wb[n].rearrange("(c p) n -> p c n", p=128))

    for c0 in (512, 0, 4096, 3072, 3584):
        cols(c0)
    for n in (3, 2):
        branch(n)
        cols(4608 + 1024 * n)
        cols(4608 + 1024 * n + 512)
    for c0 in (1024, 1536, 2048, 2560):
        cols(c0)
    for n in (0, 1):
        branch(n)
        cols(4608 + 1024 * n)
        cols(4608 + 1024 * n + 512)
    wo = A["w_out"][0].rearrange("(c p) n -> p c n", p=128)
    for h in range(2):
        L.plan(two, lambda s: three(s, 8), wo[:, :, 512 * h:512 * h + 512])
    for f0 in range(0, FF, 512):
        n = min(512, FF - f0)
        for name in ("ffn_w_gate", "ffn_w_up"):
            w = A[name][0].rearrange("(c p) n -> p c n", p=128)
            L.plan(P.ring, lambda s, n=n: three(s[:, 0:8 * n], 8), w[:, :, f0:f0 + n])
    for f0 in range(0, FF, 512):
        n = min(512, FF - f0)
        L.plan(P.ring, lambda s, n=n: three(s[:, 0:n * 8], n // 128),
               A["ffn_w_down"][0, f0:f0 + n, :].rearrange("(c p) n -> p c n", p=128))


def halves(P, bank, job, m, rhs, n, *w):
    lhs = job.ap[:, :, 128 * m:128 * m + 128]
    P.mm([(bank[:, 0:n], lhs[:, k, :], rhs[:, k, :], k == 0, False) for k in range(4)], job.tok, *w)
    yield None
    yield P.mm([(bank[:, 0:n], lhs[:, k, :], rhs[:, k, :], False, k == 7) for k in range(4, 8)])


def norm_transpose(P, x, hT, gain, tmp, banks, toks, n=512, col0=0):
    ss, rs = P.small.take(4), P.small.take(4)
    w = []
    for t in range(4):
        w.append(P.act(P.junk, x[:, t, :], ACT.Square, toks[t], P.junk_free, accum=ss[:, t:t + 1]))
        P.junk_free = w[-1]
    r = P.rstd(rs, ss, 1.0 / D, 1e-6, w)
    hs = [P.ts(tmp[:, t, :], x[:, t, :], rs[:, t:t + 1], None, MUL, None, r) for t in range(4)]
    out = []
    for c in range(8):
        k, bank, free = banks.take()
        p = P.tr([(bank[:, 128 * t:128 * t + 128], tmp[:, t, 128 * c:128 * c + 128]) for t in range(4)], hs, free)
        g = gain[:, c:c + 1]
        if c % 2:
            e = P.act(hT[:, c, :], bank[:, :], ACT.Copy, p, scale=g)
        else:
            e = P.ts(hT[:, c, :], bank[:, :], g, None, MUL, None, p)
        banks.free[k] = e
        out.append(e)
    return out


def block1_mixers(P):
    A = P.A
    R = P.region(2 * SLOT, P.top)
    P.wbr_slots = [Slot(R.take(2048), P.sem("wbr"))]
    plan_block1(P)
    hT = three(R.take(4096), 8)
    mT = three(R.take(4096), 8)
    yT = {n: three(R.take(1024), 2) for n in (0, 2, 3)}
    th_buf = Slots([R.take(512) for _ in range(2)])
    br_buf = Slots([R.take(512) for _ in range(2)])
    P.v2 = three(R.take(1024), 4)
    wua, gup = R.take(256), R.take(256)
    tw = P.load(P.ac, wua[0:64, :], A["rwkv_w_up"][0])
    tw2 = P.load(P.ac, wua[64:128, :], A["rwkv_a_up"][0])
    tg = P.load(P.ac, gup, A["rwkv_g_up"][0])
    mark = R.o
    P.junk = P.big[:, mark:mark + 1024]

    xs = three(mT.rearrange("p a b -> p (a b)"), 4)
    ld = P.xtoks(xs)
    hT_t = norm_transpose(P, xs, hT, P.vec("norm_mix_pre", 0, 8), xs, Slots(P.ps[0:8]), ld)

    dense = Slots(P.ps[0:2])
    rw = Slots(P.ps[2:5])
    misc = Slots([P.ps[7]])
    sc = Slots([P.ps[5], P.ps[6]])
    for s in (dense, rw, misc, sc):
        s.free = [hT_t] * len(s.items)

    pT = R.take(8 * 513).rearrange("p (a b) -> p a b", a=8)
    zt = P.dv.op(lambda e: e.memset(pT[:, :, 0:1], 0.0), hT_t)
    lw, L, av, kk = (three(R.take(1024), 2) for _ in range(4))
    et = three(R.take(1024), 2)
    tmps = Slots([R.take(512) for _ in range(2)])
    Bt, Kt, Vt = (R.take(256) for _ in range(3))
    X, W, Tm, TT, Ym = (three(R.take(512), 4) for _ in range(5))
    MN, GG = (three(R.take(1024), 8) for _ in range(2))
    GbT, GkT = GG[:, 0:4, :], GG[:, 4:8, :]
    QT, PT, ST, S2 = (three(R.take(n), 2) for n in (256, 128, 128, 128))
    osb, osq = three(R.take(256), 4), three(R.take(256), 4)
    ysb = R.take(256)
    cvec, E1, E2 = (three(R.take(8), 2) for _ in range(3))
    bon = three(R.take(16), 4)
    hw0, ha0 = R.take(2), R.take(2)
    rstat = R.take(16)
    rwkv_end = R.o
    dqk = three(R.take(2048), 4)
    dvv = three(R.take(1024), 4)
    conv_lo = R.o
    SS = [R.take(512) for _ in range(4)]
    aT = Slots([R.take(512) for _ in range(2)])
    dO = Slots([(three(R.take(256), 4), three(R.take(256), 4)) for _ in range(1)])
    diff_hi = R.o
    dstat = R.take(64)
    lamt = R.take(8)
    conv_end = R.o
    C = P.region(conv_lo, diff_hi)
    cu = C.take(2 * 542).rearrange("p (a b) -> p a b", a=2)
    cy = yT[3]
    ctm = three(C.take(1024), 2)
    chb = R.take(4)

    done = {}

    def project():
        job = None
        order = ([("r", c) for c in (4, 5, 6, 7)] + [("r", c) for c in (0, 1, 2, 3)] + [("c", c) for c in range(4)])
        for i, (kind, c) in enumerate(order):
            if i % 4 == 0:
                job = P.loads.take()
            k, bank, free = dense.take()
            for p in halves(P, bank, job, c % 4, hT, 512, free, hT_t):
                if p is None:
                    yield
            if i % 4 == 3:
                job.release = [p]
            if kind == "r":
                dense.free[k] = done["r", c] = P.acp(pT[:, c, 1:513], bank[:, :], p)
            elif c < 2:
                done["ca", c] = P.acp(ctm[:, c, :], bank[:, :], p)
                dense.free[k] = done["ca", c]
            else:
                t = P.act(cu[:, c - 2, 30:542], bank[:, :], ACT.Tanh, p, scale=0.5)
                dense.free[k] = done["cb", c - 2] = t
            yield
        job = P.loads.take()
        P.job_v2 = job
        for m in (2, 3):
            k, bank, free = dense.take()
            for p in halves(P, bank, job, m, hT, 512, free):
                if p is None:
                    yield
            dense.free[k] = done["dq", m - 2] = P.acp(dqk[:, m - 2, :], bank[:, :], p)
            yield
        for t in range(4):
            k, bank, free = dense.take()
            p = P.mm([(bank[:, 0:256], hT[:, c, 128 * t:128 * t + 128], job.ap[:, c, 0:256], c == 0, c == 7)
                      for c in range(8)], free)
            dense.free[k] = done["v2", t] = P.acp(P.v2[:, t, :], bank[:, 0:256], p)
            yield
        job.release = [p]
        job = P.loads.take()
        for m in (0, 1):
            k, bank, free = dense.take()
            for p in halves(P, bank, job, m, hT, 512, free):
                if p is None:
                    yield
            dense.free[k] = done["dk", m] = P.acp(dqk[:, 2 + m, :], bank[:, :], p)
            yield
        for t in range(4):
            k, bank, free = dense.take()
            p = P.mm([(bank[:, 0:256], hT[:, c, 128 * t:128 * t + 128], job.ap[:, c, 256:512], c == 0, c == 7)
                      for c in range(8)], free, job.tok)
            dense.free[k] = done["dv", t] = P.acp(dvv[:, t, :], bank[:, 0:256], p)
            yield
        job.release = [p]

    state = dict(first=True, m=[None] * 8)

    def merge(n):
        wbj = P.loads.take()
        first = state["first"]
        state["first"] = False
        for half in range(2):
            job = P.loads.take()
            for d in range(4):
                dd = 4 * half + d
                k, bank, free = dense.take()
                for p in halves(P, bank, job, d, hT, 512, free):
                    if p is None:
                        yield
                kt, th, tfree = th_buf.take()
                a = P.act(th, bank[:, :], ACT.Tanh, p, tfree, P.gb_t, scale=0.5, bias=P.gb[:, 8 * n + dd:8 * n + dd + 1])
                dense.free[k] = a
                k2, bank2, free2 = dense.take()
                q = P.mm([(bank2[:, :], wbj.ap[:, c, 128 * dd:128 * dd + 128], yT[n][:, c, :], c == 0, c == 1)
                          for c in range(2)], free2, done["y", n], wbj.tok)
                if first:
                    b = P.stt(mT[:, dd, :], th, 1.0, bank2[:, :], ADD, MUL, a, q, hT_t)
                    state["m"][dd] = b
                else:
                    kb, tb, bfree = br_buf.take()
                    b = P.stt(tb, th, 1.0, bank2[:, :], ADD, MUL, a, q, bfree)
                    state["m"][dd] = P.ptt(mT[:, dd, :], mT[:, dd, :], tb, ADD, b, state["m"][dd])
                    br_buf.free[kb] = state["m"][dd]
                dense.free[k2] = b
                th_buf.free[kt] = b
                yield
            job.release = [p]
        wbj.release = [q]

    def conv():
        w = P.vec("conv_dw_w", 0, 62)
        z = P.dv.op(lambda e: e.memset(cu[:, :, 0:30], 0.0))
        h0 = P.ts(chb[:, 0:2], P.vec("conv_ln_g", 0, 2), 0.5, None, MUL, None)
        h1 = P.ts(chb[:, 2:4], P.vec("conv_ln_b", 0, 2), 0.5, None, MUL, None)
        while ("cb", 1) not in done:
            yield
        last = [None, None]
        for ch in range(2):
            last[ch] = P.stt(cu[:, ch, 30:542], cu[:, ch, 30:542], 1.0, ctm[:, ch, :], ADD, MUL, done["ca", ch], done["cb", ch])
        for j in range(31):
            for ch in range(2):
                s = w[:, 2 * j + ch:2 * j + ch + 1]
                if j == 0:
                    last[ch] = P.ts(cy[:, ch, :], cu[:, ch, 0:512], s, None, MUL, None, last[ch], z)
                else:
                    last[ch] = P.stt(cy[:, ch, :], cu[:, ch, j:j + 512], s, cy[:, ch, :], MUL, ADD, last[ch])
            if j % 2:
                yield
        for ch in range(2):
            last[ch] = P.ts(cy[:, ch, :], cy[:, ch, :], 0.5, P.vec("conv_dw_b", ch), MUL, ADD, last[ch])
        k, bank, free = misc.take()
        mean = P.cst("mean256")
        p = P.mm([(bank[:, :], mean, cy[:, ch, :], ch == 0, ch == 1) for ch in range(2)], free, last)
        last = [P.tt(cy[:, ch, :], cy[:, ch, :], bank[:, :], SUB, p) for ch in range(2)]
        misc.free[k] = last[1]
        yield
        sq = [P.act(ctm[:, ch, :], cy[:, ch, :], ACT.Square, last[ch]) for ch in range(2)]
        k, bank, free = misc.take()
        p = P.mm([(bank[:, :], mean, ctm[:, ch, :], ch == 0, ch == 1) for ch in range(2)], free, sq)
        sd = P.act(cu[:, 0, 0:512], bank[:, :], ACT.Sqrt, p, last, bias=P.cst("eps")[:, 0:1])
        misc.free[k] = sd
        yield
        r = P.recip(cu[:, 0, 0:512], cu[:, 0, 0:512], sd)
        last = [P.tt(cy[:, ch, :], cy[:, ch, :], cu[:, 0, 0:512], MUL, r, sq) for ch in range(2)]
        yield
        for ch in range(2):
            a = P.act(ctm[:, ch, :], cy[:, ch, :], ACT.Tanh, last[ch], p, h0, h1, scale=chb[:, ch:ch + 1], bias=chb[:, 2 + ch:3 + ch])
            b = P.ts(cy[:, ch, :], cy[:, ch, :], chb[:, ch:ch + 1], chb[:, 2 + ch:3 + ch], MUL, ADD, a)
            last[ch] = P.stt(cy[:, ch, :], ctm[:, ch, :], 1.0, cy[:, ch, :], ADD, MUL, a, b)
        done["y", 3] = list(last)

    slopes4 = alibi(4)
    dscale = 32 ** -0.5
    rdf = P.cst("rdf")
    one_minus = 1.0 - (0.8 - 0.6 * float(np.exp(0.0)))

    def lam():
        v = [P.row(f"diff_lam_{x}") for x in ("q1", "k1", "q2", "k2")]
        w = []
        for m in range(2):
            a = P.tt(dstat[:, 0:32], v[2 * m], v[2 * m + 1], MUL, w)
            w = [P.red(lamt[:, m:m + 1], dstat[:, 0:32], ADD, a)]
        a = P.act(lamt[:, 2:4], lamt[:, 0:2], ACT.Exp, w)
        b = P.tt(lamt[:, 4:5], lamt[:, 3:4], lamt[:, 2:3], SUB, a)
        return P.ts(lamt[:, 5:6], lamt[:, 4:5], -(1.0 - one_minus), None, ADD, None, b)

    def diff():
        while ("y", 3) not in done or ("dv", 3) not in done:
            yield
        lam_t = lam()
        free = done["y", 3]
        units = [(i, h) for i in range(4) for h in range(4)]
        st = {}
        sfree = [free] * 4
        ofree = [None]

        def front(u):
            i, h = units[u]
            n = 128 * (i + 1)
            ex = []
            for m in range(2):
                k, bank, bfree = sc.take()
                part = slice(64 * (h % 2) + 32 * m, 64 * (h % 2) + 32 * m + 32)
                p = P.mm([(bank[:, 0:n], dqk[part, h // 2, 128 * i:128 * i + 128], dqk[part, 2 + h // 2, 0:n], True, True)],
                         bfree, done["dq", h // 2], done["dk", h // 2])
                sb = 2 * (u % 2) + m
                S = SS[sb][:, 0:n]
                a = P.stt(S, rdf[:, 512 - n:512], -slopes4[h] / dscale, bank[:, 0:n], MUL, ADD, p, sfree[sb], free)
                sc.free[k] = a
                o = 16 + 8 * sb
                b = P.red(dstat[:, 32 + sb:33 + sb], S, MAX, a)
                c = P.ts(dstat[:, 36 + sb:37 + sb], dstat[:, 32 + sb:33 + sb], -dscale, None, MUL, None, b)
                e = P.act(S, S, ACT.Exp, c, bias=dstat[:, 36 + sb:37 + sb], scale=dscale, accum=dstat[:, 40 + sb:41 + sb])
                ex.append(e)
            st[u] = ex

        def back(u):
            i, h = units[u]
            n = 128 * (i + 1)
            s0 = 2 * (u % 2)
            r = P.recip(dstat[:, 44 + s0:46 + s0], dstat[:, 40 + s0:42 + s0], st[u])
            m1 = P.tt(dstat[:, 48 + s0:49 + s0], dstat[:, 45 + s0:46 + s0], lamt[:, 5:6], MUL, r, lam_t)
            a = P.ts(SS[s0][:, 0:n], SS[s0][:, 0:n], dstat[:, 44 + s0:45 + s0], None, MUL, None, r)
            b = P.stt(SS[s0][:, 0:n], SS[s0 + 1][:, 0:n], dstat[:, 48 + s0:49 + s0], SS[s0][:, 0:n], MUL, ADD, a, m1)
            sfree[s0 + 1] = b
            k, bank, bfree = misc.take()
            p = P.tr([(bank[:, 128 * c:128 * c + 128], SS[s0][:, 128 * c:128 * c + 128]) for c in range(i + 1)], b, bfree)
            sfree[s0] = p
            ka, at, afree = aT.take()
            e = P.acp(at[:, 0:n], bank[:, 0:n], p, afree)
            misc.free[k] = e
            yield
            k, bank, bfree = misc.take()
            q = P.mm([(bank[:, 0:64], at[:, 128 * c:128 * c + 128], dvv[:, c, 64 * h:64 * h + 64], c == 0, c == i)
                      for c in range(i + 1)], e, bfree, [done["dv", c] for c in range(i + 1)])
            aT.free[ka] = q
            o, osq2 = dO.items[0]
            e = P.acp(o[:, h, :], bank[:, 0:64], q, ofree[0])
            misc.free[k] = e
            st[u] = e

        def finish(i):
            o, sq = dO.items[0]
            w = [st[4 * i + h] for h in range(4)]
            a = P.tt(sq, o, o, MUL, w)
            b = P.red(dstat[:, 52:56], sq, ADD, a)
            r = P.rstd(dstat[:, 56:60], dstat[:, 52:56], 1.0 / 64, 1e-5, b)
            c = P.tt(sq, o, dstat[:, 56:60].unsqueeze(2).to_broadcast([128, 4, 64]), MUL, r)
            g = P.row("diff_subln_g").unsqueeze(1).to_broadcast([128, 4, 64])
            d = P.stt(o, sq, one_minus, g, MUL, MUL, c)
            k, bank, bfree = misc.take()
            of = o.rearrange("p a b -> p (a b)")
            p = P.tr([(bank[:, 128 * c:128 * c + 128], of[:, 128 * c:128 * c + 128]) for c in range(2)], d, bfree)
            ofree[0] = p
            e = P.acp(yT[2][:, :, 128 * i:128 * i + 128], three(bank[:, 0:256], 2), p)
            misc.free[k] = e
            done.setdefault("y2", []).append(e)

        front(0)
        yield
        for u in range(16):
            if u + 1 < 16:
                front(u + 1)
                yield
            yield from back(u)
            yield
            if u % 4 == 3:
                finish(u // 4)
                yield
        done["y", 2] = done["y2"]

    def rwkv():
        mu = P.vec("rwkv_mu", 0, 8)
        p = {}

        def shift(c):
            k, tmp, free = tmps.take()
            a = P.tt(tmp, pT[:, c, 0:512], pT[:, c, 1:513], SUB, done["r", c], zt, free)
            p[c] = P.stt(pT[:, c, 1:513], tmp, mu[:, c:c + 1], pT[:, c, 1:513], MUL, ADD, a)
            tmps.free[k] = p[c]

        V = lambda c: pT[:, c, 1:513]
        a0 = P.ts(hw0, P.vec("rwkv_w0", 0, 2), 0.5, None, MUL, None)
        a1 = P.ts(ha0, P.vec("rwkv_a0", 0, 2), 0.5, None, MUL, None)
        for c in (6, 7):
            while ("r", c) not in done:
                yield
            shift(c)
        th = P.act(pT[0:64, 6, 1:513], pT[0:64, 6, 1:513], ACT.Tanh, p[6])
        sg = P.act(V(7), V(7), ACT.Tanh, p[7], scale=0.5)
        sg = P.ts(V(7), V(7), 0.5, 0.5, MUL, ADD, sg)
        yield
        lw_t, av_t = [], []
        for ch in range(2):
            k, bank, free = rw.take()
            q = P.mm([(bank[:, :], wua[0:64, 128 * ch:128 * ch + 128], pT[0:64, 6, 1:513], True, True)], th, free, tw)
            e = P.act(lw[:, ch, :], bank[:, :], ACT.Tanh, q, a0, scale=0.5, bias=hw0[:, ch:ch + 1])
            rw.free[k] = e
            lw_t.append(P.ts(lw[:, ch, :], lw[:, ch, :], -0.5 * 0.606531, -0.5 * 0.606531, MUL, ADD, e))
            k, bank, free = rw.take()
            q = P.mm([(bank[:, :], wua[64:128, 128 * ch:128 * ch + 128], pT[64:128, 6, 1:513], True, True)], p[6], free, tw2)
            e = P.act(av[:, ch, :], bank[:, :], ACT.Tanh, q, a1, scale=0.5, bias=ha0[:, ch:ch + 1])
            rw.free[k] = e
            av_t.append(P.ts(av[:, ch, :], av[:, ch, :], 0.5, 0.5, MUL, ADD, e))
            yield
        zero = P.cst("zero")
        sc_t = []
        for ch in range(2):
            w = []
            for t in range(4):
                s = slice(128 * t, 128 * t + 128)
                w.append(P.dv.op((lambda ch, s: lambda e: e.tensor_tensor_scan(L[:, ch, s], lw[:, ch, s], zero, 0.0, ADD, ADD))(ch, s), lw_t[ch]))
            l4 = L[:, ch, :].rearrange("p (t n) -> p t n", t=4)
            a = P.cp(cvec[:, ch, :], l4[:, :, 63], w)
            sc_t.append(P.tt(l4, l4, cvec[:, ch, :].unsqueeze(2).to_broadcast([128, 4, 128]), SUB, a))
        e1 = P.act(E1, cvec, ACT.Exp, sc_t)
        yield
        for c in (4, 5, 2, 3, 0, 1):
            while ("r", c) not in done:
                yield
            shift(c)
        yield
        kk_t, k_t, b_t = [], [], []
        for ch in range(2):
            a = P.ts(kk[:, ch, :], V(2 + ch), P.vec("rwkv_k_k", ch), None, MUL, None, p[2 + ch])
            kt, tmp, free = tmps.take()
            b = P.act(tmp, kk[:, ch, :], ACT.Square, a, free)
            k, bank, bfree = rw.take()
            q = P.mm([(bank[:, :], P.cst("headones"), tmp, True, True)], b, bfree)
            s = P.act(tmp, bank[:, :], ACT.Sqrt, q)
            rw.free[k] = s
            s = P.ts(tmp, tmp, 1e-12, None, MAX, None, s)
            s = P.recip(tmp, tmp, s)
            kk_t.append(P.tt(kk[:, ch, :], kk[:, ch, :], tmp, MUL, s))
            tmps.free[kt] = kk_t[-1]
            kt, tmp, free = tmps.take()
            a = P.ts(tmp, av[:, ch, :], -1.0, P.vec("rwkv_k_a", ch), ADD, MUL, av_t[ch], free)
            k_t.append(P.stt(V(2 + ch), tmp, 1.0, V(2 + ch), ADD, MUL, a, kk_t[ch]))
            tmps.free[kt] = k_t[ch]
            b_t.append(P.tt(av[:, ch, :], av[:, ch, :], kk[:, ch, :], MUL, kk_t[ch], k_t[ch]))
            yield
        k, bank, free = rw.take()
        for ch in range(2):
            kt, tmp, tfree = tmps.take()
            a = P.stt(tmp, V(ch), P.vec("rwkv_r_k", ch), V(2 + ch), MUL, MUL, p[ch], k_t[ch], tfree)
            q = P.mm([(bank[:, 4 * t + 2 * ch:4 * t + 2 * ch + 2], tmp[:, 128 * t:128 * t + 128], P.cst("headsel"), True, True)
                      for t in range(4)], a, free)
            tmps.free[kt] = q
        bon_t = P.acp(bon.rearrange("p a b -> p (a b)"), bank[:, 0:16], q)
        rw.free[k] = bon_t
        yield
        fin = []
        for ch in range(2):
            kt, tmp, tfree = tmps.take()
            a = P.tt(tmp, L[:, ch, :], lw[:, ch, :], SUB, sc_t[ch], tfree)
            e = P.act(tmp, tmp, ACT.Exp, a)
            fin.append(P.stt(kk[:, ch, :], kk[:, ch, :], -1.0, tmp, MUL, MUL, e, b_t[ch]))
            tmps.free[kt] = fin[-1]
            a = P.act(et[:, ch, :], L[:, ch, :], ACT.Exp, sc_t[ch], scale=-1.0)
            b = P.tt(av[:, ch, :], av[:, ch, :], et[:, ch, :], MUL, a, b_t[ch])
            c = P.tt(V(2 + ch), V(2 + ch), et[:, ch, :], MUL, a, bon_t)
            a2 = P.act(L[:, ch, :], L[:, ch, :], ACT.Exp, a, fin[-1])
            d = P.cp(E2[:, ch, :], L[:, ch, :].rearrange("p (t n) -> p t n", t=4)[:, :, 127], a2)
            f = P.tt(V(ch), V(ch), L[:, ch, :], MUL, a2, bon_t)
            fin += [b, c, d, f]
            yield
        done["prep"] = (fin + [p[4], p[5]], bon_t, e1, sg)

    def sets():
        l2, e2, m2 = (three(x.rearrange("p a b -> p (a b)"), 8) for x in (L, et, lw))
        yield dict(X=X, Tm=Tm, TT=TT, Ym=Ym, MN=MN, Vt=Vt)
        yield dict(X=l2[:, 0:4, :], Ym=l2[:, 4:8, :], Tm=e2[:, 0:4, :], TT=e2[:, 4:8, :], MN=m2, Vt=tmps.items[0][:, 0:256])
    tile_set = list(sets())

    def early(t):
        while "prep" not in done or (t > 1 and ("late", t - 2) not in done):
            yield
        S_ = tile_set[t % 2]
        X, Tm, TT, Ym, MN, Vt = (S_[n] for n in ("X", "Tm", "TT", "Ym", "MN", "Vt"))
        MT, NT = MN[:, 0:4, :], MN[:, 4:8, :]
        fin = done["prep"][0]
        before = done["late", t - 2] if t > 1 else fin
        s = slice(128 * t, 128 * t + 128)
        AT = lambda h: kk[64 * (h % 2):64 * (h % 2) + 64, h // 2, s]
        BT = lambda h: av[64 * (h % 2):64 * (h % 2) + 64, h // 2, s]
        KT = lambda h: pT[64 * (h % 2):64 * (h % 2) + 64, 2 + h // 2, 1 + 128 * t:129 + 128 * t]
        z = P.po.op((lambda MN: lambda e: e.memset(MN, 0.0))(MN), before)
        m = P.cst("strict").bitcast(I32).unsqueeze(1).to_broadcast([128, 4, 128])
        got = []
        for par in range(2):
            k, bank, free = rw.take()
            q = P.mm([(bank[:, 256 * y + 128 * g:256 * y + 128 * g + 128], (BT, KT)[y](2 * g + par), AT(2 * g + par), True, True)
                      for y in range(2) for g in range(2)], fin, free)
            got.append(P.dv.op((lambda MN, m, bank, par: lambda e: e.copy_predicated(
                MN[:, par::2, :], m, three(bank[:, :], 4)))(MN, m, bank, par), q, z))
            rw.free[k] = got[-1]
        yield
        idb = P.ident.unsqueeze(1).to_broadcast([128, 4, 128])
        t_t = P.po.op((lambda Tm: lambda e: e.tensor_copy(Tm, idb))(Tm), before)
        tt_t = P.po.op((lambda TT: lambda e: e.tensor_copy(TT, idb))(TT), before)
        k, bank, free = rw.take()
        q = P.tr([(bank[:, 128 * c:128 * c + 128], kk[:, c, s]) for c in range(2)]
                 + [(bank[:, 256 + 128 * c:384 + 128 * c], pT[:, 4 + c, 1 + 128 * t:129 + 128 * t]) for c in range(2)], fin, free)
        x_t = P.acp(X[:, :, 0:64], three(bank[:, 0:256], 4), q, before)
        v_ = P.acp(Vt, bank[:, 256:512], q, before)
        rw.free[k] = [x_t, v_]
        yield
        x2 = None
        y_free = before
        for b in range(7):
            k, bank, free = rw.take()
            q = P.mm([(bank[:, 128 * h:128 * h + 128], MT[:, h, :], Tm[:, h, :], True, True) for h in range(4)], got, t_t, free)
            m = P.cst(f"lev{b}").unsqueeze(1).to_broadcast([128, 4, 128])
            y = P.tt(Ym, three(bank[:, :], 4), m, MUL, q, y_free)
            rw.free[k] = y
            yield
            if b == 1:
                k, bank, free = rw.take()
                q = P.mm([(bank[:, 64 * h:64 * h + 64], NT[:, h, :], Vt[:, 64 * h:64 * h + 64], True, True) for h in range(4)], v_, free)
                x2 = P.acp(X[:, :, 64:128], three(bank[:, 0:256], 4), q, before)
                rw.free[k] = x2
            k, bank, free = rw.take()
            q2 = P.mm([(bank[:, 128 * h:128 * h + 128], Ym[:, h, :], TT[:, h, :], True, True) for h in range(4)], y, tt_t, free)
            y_free = q2
            if b < 6:
                k1, bank1, free1 = rw.take()
                q1 = P.mm([(bank1[:, 128 * h:128 * h + 128], TT[:, h, :], Ym[:, h, :], True, True) for h in range(4)], free1)
                y_free = q1
                t_t = P.tt(Tm, Tm, three(bank1[:, :], 4), ADD, q1)
                rw.free[k1] = t_t
                tt_t = P.tt(TT, TT, three(bank[:, :], 4), ADD, q2, q1)
            else:
                tt_t = P.tt(TT, TT, three(bank[:, :], 4), ADD, q2)
            rw.free[k] = tt_t
            yield
        done["early", t] = (x_t, x2, tt_t, v_)

    def late():
        while "prep" not in done:
            yield
        fin, bon_t, e1, sg = done["prep"]
        yT_t = []
        st_t = P.dv.op(lambda e: e.memset(S2, 0.0))
        tile_free = []
        ysb_free = None
        for t in range(4):
            S_ = tile_set[t % 2]
            X, TT, Vt = S_["X"], S_["TT"], S_["Vt"]
            s = slice(128 * t, 128 * t + 128)
            BT = lambda h: av[64 * (h % 2):64 * (h % 2) + 64, h // 2, s]
            KT = lambda h: pT[64 * (h % 2):64 * (h % 2) + 64, 2 + h // 2, 1 + 128 * t:129 + 128 * t]
            RT = lambda h: pT[64 * (h % 2):64 * (h % 2) + 64, h // 2, 1 + 128 * t:129 + 128 * t]
            z = P.po.op(lambda e: e.memset(GG, 0.0), tile_free)
            m = P.cst("incl").bitcast(I32).unsqueeze(1).to_broadcast([128, 4, 128])
            got = []
            for par in range(2):
                k, bank, free = rw.take()
                q = P.mm([(bank[:, 256 * y + 128 * g:256 * y + 128 * g + 128], (BT, KT)[y](2 * g + par), RT(2 * g + par), True, True)
                          for y in range(2) for g in range(2)], fin, free)
                got.append(P.dv.op((lambda m, bank, par: lambda e: e.copy_predicated(
                    GG[:, par::2, :], m, three(bank[:, :], 4)))(m, bank, par), q, z))
                rw.free[k] = got[-1]
            yield
            k, bank, free = rw.take()
            q = P.tr([(bank[:, 128 * c:128 * c + 128], av[:, c, s]) for c in range(2)]
                     + [(bank[:, 256 + 128 * c:384 + 128 * c], pT[:, 2 + c, 1 + 128 * t:129 + 128 * t]) for c in range(2)], fin, free)
            b_ = P.acp(Bt, bank[:, 0:256], q, tile_free)
            k_ = P.acp(Kt, bank[:, 256:512], q, tile_free)
            rw.free[k] = [b_, k_]
            yield
            while ("early", t) not in done:
                yield
            x_t, x2, tt_t, v_ = done["early", t]
            k, bank, free = rw.take()
            q = P.mm([(bank[:, 128 * h:128 * h + 128], TT[:, h, :], X[:, h, :], True, True) for h in range(4)], tt_t, x_t, x2, free)
            w_t = P.cp(W, three(bank[:, :], 4), q, tile_free)
            rw.free[k] = w_t
            yield
            k, bank, free = rw.take()
            q = P.mm([(bank[64 * (h % 2):64 * (h % 2) + 64, 128 * (h // 2):128 * (h // 2) + 128], W[:, h, 0:64], GbT[:, h, :], True, True)
                      for h in range(4)], w_t, got, free)
            q = P.mm([(bank[64 * (h % 2):64 * (h % 2) + 64, 256 + 64 * (h // 2):320 + 64 * (h // 2)], W[:, h, 0:64], Bt[:, 64 * h:64 * h + 64], True, True)
                      for h in range(4)], b_)
            qt_t = P.tt(QT, three(bank[:, 0:256], 2), pT[:, 0:2, 1 + 128 * t:129 + 128 * t], ADD, q, tile_free)
            pt_t = P.cp(PT, three(bank[:, 256:384], 2), q, tile_free)
            rw.free[k] = pt_t
            yield
            if t:
                st_t = P.tt(S2, ST, E1[:, :, t:t + 1].to_broadcast([128, 2, 64]), MUL, st_t, e1, tile_free)
            ends, zs = [], []
            for par in range(2):
                hp = slice(64 * par, 64 * par + 64)
                k, bank, free = rw.take()
                g = []
                for c in range(2):
                    h = 2 * c + par
                    o = bank[hp, 64 * c:64 * c + 64]
                    g += [(o, Bt[:, 64 * h:64 * h + 64], W[:, h, 64:128], True, False),
                          (o, Kt[:, 64 * h:64 * h + 64], Vt[:, 64 * h:64 * h + 64], False, t == 0)]
                    if t:
                        g.append((o, PT[hp, c, :], S2[hp, c, :], False, True))
                zq = P.mm(g, free, k_, st_t, pt_t, qt_t, got)
                g = []
                for c in range(2):
                    h = 2 * c + par
                    o = bank[:, 128 + 64 * c:192 + 64 * c]
                    g += [(o, GbT[:, h, :], W[:, h, 64:128], True, False), (o, GkT[:, h, :], Vt[:, 64 * h:64 * h + 64], False, t == 0)]
                    if t:
                        g.append((o, QT[hp, c, :], S2[hp, c, :], False, True))
                qo = P.mm(g)
                a = P.tt(ST[hp, :, :], three(bank[hp, 0:128], 2), S2[hp, :, :], ADD, qo, st_t)
                zs.append(P.tt(ST[hp, :, :], ST[hp, :, :], E2[hp, :, t:t + 1].to_broadcast([64, 2, 64]), MUL, a))
                o_t = P.cp(osb[:, par::2, :], three(bank[:, 128:256], 2), qo, ysb_free)
                ends.append(o_t)
                rw.free[k] = o_t
            st_t, o_t = zs, ends
            yield
            s1, s2_, s3 = rstat[:, 0:4], rstat[:, 4:8], rstat[:, 8:12]
            a = P.red(s1, osb, ADD, o_t)
            a = P.ts(s1, s1, 1.0 / 64, None, MUL, None, a)
            a = P.tt(osb, osb, s1.unsqueeze(2).to_broadcast([128, 4, 64]), SUB, a)
            b = P.tt(osq, osb, osb, MUL, a)
            b = P.red(s2_, osq, ADD, b)
            b = P.rstd(s3, s2_, 1.0 / 64, 64e-5, b)
            a = P.tt(osb, osb, s3.unsqueeze(2).to_broadcast([128, 4, 64]), MUL, b)
            of = osb.rearrange("p a b -> p (a b)")
            a = P.tt(of, of, P.row("rwkv_ln_g"), MUL, a)
            a = P.tt(of, of, P.row("rwkv_ln_b"), ADD, a)
            b = P.tt(osq, three(Vt, 4), bon[:, t, :].unsqueeze(2).to_broadcast([128, 4, 64]), MUL, bon_t, v_, a)
            a = P.tt(osb, osb, osq, ADD, a, b)
            k, bank, free = rw.take()
            q = P.mm([(bank[:, 0:256], pT[:, 7, 1 + 128 * t:129 + 128 * t], gup, True, True)], sg, tg, free)
            a = P.tt(ysb, of, bank[:, 0:256], MUL, a, q, ysb_free)
            rw.free[k] = a
            yield
            k, bank, free = rw.take()
            q = P.tr([(bank[:, 128 * c:128 * c + 128], ysb[:, 128 * c:128 * c + 128]) for c in range(2)], a, free)
            ysb_free = q
            e = P.acp(yT[0][:, :, s], three(bank[:, 0:256], 2), q)
            rw.free[k] = e
            yT_t.append(e)
            tile_free = [q, a, e, st_t]
            done["late", t] = tile_free
            yield
        done["y", 0] = yT_t

    def stream():
        yield from project()
        while ("y", 3) not in done:
            yield
        yield from merge(3)
        while ("y", 2) not in done:
            yield
        yield from merge(2)

    def tiles(first):
        for t in (first, first + 2):
            yield from early(t)

    df = diff()
    rounds((stream(), 1), (rwkv(), 1), (df, 1), (tiles(0), 1), (conv(), 1), (df, 1), (tiles(1), 1), (df, 1), (late(), 1))
    part = [q.last() for q in (P.pe, P.ac, P.dv, P.po)]

    R2 = P.region(mark, P.top)
    qk = three(R2.take(6144), 12)
    vv = three(R2.take(2048), 4)
    rd = R2.take(P.ntab - P.ncst)
    yT[1] = three(R2.take(1024), 2)
    S3 = [R2.take(1280) for _ in range(2)]
    P3 = Slots([R2.take(512) for _ in range(6)])
    ob = R2.take(256)
    dst = R2.take(16)
    rd_t = P.load(P.ac, rd, A["tables"][:, P.ncst:P.ntab], part)

    def rdt(name):
        o, n = P.cat[name]
        return rd[:, o - P.ncst:o - P.ncst + n]

    def project2():
        first = True
        for s in range(3):
            job = P.loads.take()
            for m in range(4):
                k, bank, free = dense.take()
                for p in halves(P, bank, job, m, hT, 512, free):
                    if p is None:
                        yield
                c = 4 * s + m
                dense.free[k] = done["qk", c] = P.acp(qk[:, c, :], bank[:, :], p, part if first else None)
                first = False
                yield
            job.release = [p]
        job = P.loads.take()
        for t in range(4):
            k, bank, free = dense.take()
            p = P.mm([(bank[:, :], hT[:, c, 128 * t:128 * t + 128], job.ap[:, c, :], c == 0, c == 7) for c in range(8)], free, job.tok)
            dense.free[k] = done["vv", t] = P.acp(vv[:, t, :], bank[:, :], p)
            yield
        job.release = [p]

    slopes12 = alibi(12)
    scores = Slots(P.ps[2:5])
    turned = Slots(P.ps[5:7])
    outp = Slots(P.ps[7:8])
    for s in (scores, turned, outp):
        s.free = [part] * len(s.items)

    def dil():
        while ("vv", 3) not in done:
            yield
        units = [(i, j) for i in range(4) for j in range(4)]
        st = {}
        sfree = [part, part]
        ofree = [None]

        def blocks(i):
            return [(0, b) for b in range(max(0, i - 1), i + 1)] + [(1, b) for b in range(i + 1)] + [(2, b) for b in range(i + 1)]

        def front(u):
            i, j = units[u]
            S = S3[u % 2]
            col = 0
            w = []
            for g in range(3):
                b0 = max(0, i - 1) if g == 0 else 0
                n = 128 * (i + 1 - b0)
                hd = 4 * g + j
                part_ = slice(64 * (j % 2), 64 * (j % 2) + 64)
                k, bank, free = scores.take()
                p = P.mm([(bank[:, 0:n], qk[part_, hd // 2, 128 * i:128 * i + 128], qk[part_, 6 + hd // 2, 128 * b0:128 * i + 128], True, True)],
                         free, done["qk", hd // 2], done["qk", 6 + hd // 2])
                tab = rdt(f"rd{g}")
                a = P.stt(S[:, col:col + n], tab[:, tab.shape[1] - n:], -slopes12[hd] * 8.0, bank[:, 0:n], MUL, ADD, p, sfree[u % 2], rd_t)
                scores.free[k] = a
                w.append(a)
                col += n
            o = 4 * (u % 2)
            b = P.red(dst[:, o:o + 1], S[:, 0:col], MAX, w)
            c = P.ts(dst[:, o + 1:o + 2], dst[:, o:o + 1], -0.125, None, MUL, None, b)
            st[u] = P.act(S[:, 0:col], S[:, 0:col], ACT.Exp, c, bias=dst[:, o + 1:o + 2], scale=0.125, accum=dst[:, o + 2:o + 3])

        def back(u):
            i, j = units[u]
            S = S3[u % 2]
            o = 4 * (u % 2)
            r = P.recip(dst[:, o + 3:o + 4], dst[:, o + 2:o + 3], st[u])
            bl = blocks(i)
            ko, bo, ofr = outp.take()
            pv = []
            for c0 in range(0, len(bl), 4):
                n = min(4, len(bl) - c0)
                k, bank, free = turned.take()
                p = P.tr([(bank[:, 128 * c:128 * c + 128], S[:, 128 * (c0 + c):128 * (c0 + c) + 128]) for c in range(n)], st[u], free)
                kp, buf, pfree = P3.take()
                e = P.acp(buf[:, 0:128 * n], bank[:, 0:128 * n], p, pfree)
                turned.free[k] = e
                pv.append((c0, n, kp, buf, e))
            sfree[u % 2] = p
            yield
            for c0, n, kp, buf, e in pv:
                g = []
                for c in range(n):
                    grp, b = bl[c0 + c]
                    v0 = 256 * grp + 64 * j
                    V = vv[:, b, v0:v0 + 64] if grp < 2 else P.v2[:, b, v0 - 512:v0 - 448]
                    g.append((bo[:, 0:64], buf[:, 128 * c:128 * c + 128], V, c0 + c == 0, c0 + c == len(bl) - 1))
                q = P.mm(g, e, ofr, [done["vv", b] for b in range(4)])
                P3.free[kp] = q
            e = P.ts(ob[:, 64 * j:64 * j + 64], bo[:, 0:64], dst[:, o + 3:o + 4], None, MUL, None, q, r, ofree[0])
            outp.free[ko] = e
            st[u] = e

        def finish(i):
            k, bank, free = turned.take()
            p = P.tr([(bank[:, 128 * c:128 * c + 128], ob[:, 128 * c:128 * c + 128]) for c in range(2)],
                     [st[4 * i + j] for j in range(4)], free)
            ofree[0] = p
            e = P.acp(yT[1][:, :, 128 * i:128 * i + 128], three(bank[:, 0:256], 2), p)
            turned.free[k] = e
            done.setdefault("y1", []).append(e)

        front(0)
        yield
        for u in range(16):
            if u + 1 < 16:
                front(u + 1)
                yield
            yield from back(u)
            yield
            if u % 4 == 3:
                finish(u // 4)
                yield
        done["y", 1] = done["y1"]

    def stream2():
        yield from project2()
        yield from merge(0)
        while ("y", 1) not in done:
            yield
        yield from merge(1)

    rounds((stream2(), 1), (dil(), 2))
    return mT, state["m"]


def add_norm(P, o, x, gain, out, *w):
    ss, rs = P.small.take(1), P.small.take(1)
    P.junk_free = P.act(P.junk, o, ACT.Square, *w, P.junk_free, accum=ss)
    r = P.rstd(rs, ss, 1.0 / D, 1e-6, P.junk_free)
    a = P.stt(o, o, rs, gain, MUL, MUL, r, *w)
    return P.tt(out, o, x, ADD, a)


def norm_tile(P, x, tmp, *w):
    ss, rs = P.small.take(1), P.small.take(1)
    P.junk_free = P.act(P.junk, x, ACT.Square, *w, P.junk_free, accum=ss)
    r = P.rstd(rs, ss, 1.0 / D, 1e-6, P.junk_free)
    return P.ts(tmp, x, rs, None, MUL, None, r)


def turn_gain(P, banks, tmp, hT, gain, cols, *w):
    out = []
    for g in range(2):
        k, bank, free = banks.take()
        p = P.tr([(bank[:, 128 * c:128 * c + 128], tmp[:, 512 * g + 128 * c:512 * g + 128 * c + 128]) for c in range(4)], *w, free)
        out.append(P.tt(hT[:, 4 * g:4 * g + 4, cols], three(bank[:, :], 4), gain[:, 4 * g:4 * g + 4].unsqueeze(2).to_broadcast([128, 4, 128]), MUL, p))
        banks.free[k] = out[-1]
    return out


def block1_out(P, mT, m_t):
    A = P.A
    R = P.region(6 * SLOT, P.top)
    x1 = three(R.take(4096), 4)
    hT = three(R.take(4096), 8)
    aT = R.take(22 * 512).rearrange("p (a b) -> p a b", a=22)
    gain = R.take(1024)
    P.junk = R.take(1024)
    xr = three(aT.rearrange("p a b -> p (a b)")[:, 0:4096], 4)
    sg = Slots([R.take(512) for _ in range(2)])
    before = [q.last() for q in (P.pe, P.ac, P.dv, P.po)]
    ld = [P.load(P.ac, xr[:, t, :], A["x"][0, 128 * t:128 * t + 128, :], before if t == 0 else None) for t in range(4)]
    gt = P.row_load(gain, A["norm_mix_post"][0], before)
    banks = Slots(P.ps)
    banks.free = [before] * 8
    P.hD = P.nc.dram_tensor("rows_h", (T + 16, D), F32, kind="Internal").ap()
    P.yD = P.nc.dram_tensor("rows_y", (64 * NBLK, D), F32, kind="Internal").ap()
    xn = three(aT.rearrange("p a b -> p (a b)")[:, 4096:8192], 4)
    jobs = [P.loads.take(), P.loads.take()]
    x1_t, h_t, late = [], [], None
    for t in range(4):
        ev = []
        for h in range(2):
            k, bank, free = banks.take()
            p = P.mm([(bank[:, :], mT[:, c, 128 * t:128 * t + 128], jobs[h].ap[:, c, :], c == 0, c == 7) for c in range(8)],
                     free, jobs[h].tok, m_t)
            jobs[h].release = [p]
            banks.free[k] = P.acp(x1[:, t, 512 * h:512 * h + 512], bank[:, :], p, before, scale=0.5)
            ev.append(banks.free[k])
        if late:
            h_t += turn_gain(P, banks, *late)
        x1_t.append(add_norm(P, x1[:, t, :], xr[:, t, :], gain, x1[:, t, :], ev, gt, ld[t]))
        n = norm_tile(P, x1[:, t, :], xn[:, t, :], x1_t[t])
        late = (xn[:, t, :], hT, P.vec("norm_ffn_pre", 0, 8), slice(128 * t, 128 * t + 128), n)
    h_t += turn_gain(P, banks, *late)
    P.ring_gate += [p]
    g2 = P.row_load(gain, A["norm_ffn_post"][0], x1_t)
    f = 0
    a_t = []
    for f0 in range(0, FF, 512):
        n = min(512, FF - f0)
        jg, ju = P.loads.take(), P.loads.take()
        for m in range(n // 128):
            k, bank, free = banks.take()
            p = P.mm([(bank[:, :], jg.ap[:, c, 128 * m:128 * m + 128], hT[:, c, :], c == 0, c == 7) for c in range(8)], free, jg.tok, h_t)
            ks, s, sfree = sg.take()
            a = P.act(s, bank[:, :], ACT.Silu, p, sfree)
            banks.free[k] = a
            k, bank, free = banks.take()
            q = P.mm([(bank[:, :], ju.ap[:, c, 128 * m:128 * m + 128], hT[:, c, :], c == 0, c == 7) for c in range(8)], free, ju.tok)
            b = P.tt(aT[:, f, :], s, bank[:, :], MUL, a, q)
            banks.free[k] = sg.free[ks] = b
            a_t.append(b)
            f += 1
            if f == 10:
                P.zr = P.load(P.ac, P.yD[64 * NEXP:64 * NBLK, :].rearrange("(p r) (k c) -> p (r k) c", p=128, c=128),
                              P.cst("zero").unsqueeze(1).to_broadcast([128, 8 * (64 * (NBLK - NEXP) // 128), 128]))
        jg.release, ju.release = [p], [q]
    o = three(hT.rearrange("p a b -> p (a b)"), 4)

    def down(t, h, job, f, n):
        b = 2 * t + h
        return P.mm([(P.ps[b][:, :], aT[:, f + c, 128 * t:128 * t + 128], job.ap[:, c, 512 * h:512 * h + 512], f + c == 0, f + c == 21)
                     for c in range(n)], banks.free[b] if f == 0 else None, job.tok, a_t)

    for f in (0, 4, 8, 12):
        job = P.loads.take()
        for t in range(4):
            for h in range(2):
                p = down(t, h, job, f, 4)
        job.release = [p]
    jobs = [P.loads.take(), P.loads.take()]
    x2_t = []
    for t in range(4):
        ev = []
        for h in range(2):
            down(t, h, jobs[0], 16, 4)
            p = down(t, h, jobs[1], 20, 2)
            banks.free[2 * t + h] = P.acp(o[:, t, 512 * h:512 * h + 512], P.ps[2 * t + h][:, :], p, h_t)
            ev.append(banks.free[2 * t + h])
        x2_t.append(add_norm(P, o[:, t, :], x1[:, t, :], gain, x1[:, t, :], ev, g2))
    jobs[0].release, jobs[1].release = [p], [p]
    return x1, x2_t


def setup(P):
    R = P.region(0, NBIG)
    n = P.cat["rd1"][0]
    P.ncst, P.ntab = n, P.table_cols
    top = NBIG - n - NVEC - NROW - 400 - 32
    P.top = top
    S = P.region(top, NBIG)
    P.cst_sb, P.vec_sb, P.row_sb = S.take(n), S.take(NVEC), S.take(NROW)
    P.gb = S.take(32)
    P.small = P.region(S.o, S.o + 400)
    P.junk_free = None
    P.ident = P.cst("ident")
    P.ring_gate = []
    P.ring = [Slot(P.big[:, SLOT * k:SLOT * k + SLOT], P.sem("ring")) for k in range(6)]
    for s in P.ring[2:]:
        s.gate = P.ring_gate
    P.loads = Loads(P)
    P.sp_sections, P.sp_ends = [], []

    def xtoks(xs):
        loads, P.sp.items = P.sp.items, []
        toks = [P.load(P.sp, xs[:, t, :], P.A["x"][0, 128 * t:128 * t + 128, :]) for t in range(4)]
        c = P.load(P.sp, P.cst_sb, P.A["tables"][:, 0:n])
        v = P.load(P.sp, P.vec_sb, P.A["vecs"])
        r = P.load(P.sp, P.row_sb, P.A["rows"].partition_broadcast(128))
        for q in (P.pe, P.dv, P.po):
            q.wait(c, v, r)
        P.sp.items += loads
        P.gb_t = P.ts(P.gb, P.vec("gate_bias", 0, 32), 0.5, None, MUL, None)
        return toks
    P.xtoks = xtoks


def program(nc, A, out, cat, table_cols):
    with ExitStack() as ctx:
        P = Program(nc, ctx, A, out)
        P.cat, P.table_cols = cat, table_cols
        setup(P)
        mT, m_t = block1_mixers(P)
        x2, x2_t = block1_out(P, mT, m_t)
        block2(P, x2, x2_t)
        put = list(zip(P.sp_at, P.sp_sections)) + [(at, [w]) for at, w in zip(P.sp_done, P.sp_ends)]
        for at, sec in sorted(put, key=lambda x: -x[0]):
            P.sp.items[at:at] = sec
        block = ctx.enter_context(nc.Block())

        @block.sync
        def _(e):
            P.sp.emit(e)

        @block.tensor
        def _(e):
            P.pe.emit(e)

        @block.scalar
        def _(e):
            P.ac.emit(e)

        @block.vector
        def _(e):
            P.dv.emit(e)

        @block.gpsimd
        def _(e):
            P.po.emit(e)


ALPHA = 4.0 ** 0.25
NTAB = 64
NBLK = 2 * NEXP + NOVF


def order(i):
    return i // 2 + 16 * (i % 2)


def plan_block2(P, then):
    A, L = P.A, P.loads
    ring = P.ring

    def cols(w, c0):
        L.plan(ring, lambda s: three(s, 8), w.rearrange("(c p) n -> p c n", p=128)[:, :, c0:c0 + 512])

    def experts(l):
        while P.loads.turn[id(ring)] % 6:
            P.loads.turn[id(ring)] += 1
        for i in range(NEXP):
            e = order(i)
            cols(A["moe_w_gate_2"][l, e], 0)
            cols(A["moe_w_up_2"][l, e], 0)
            L.plan(ring, lambda s: three(s, 4), A["moe_w_down_2"][l, e].rearrange("(c p) n -> p c n", p=128))

    for s in range(2):
        cols(A["lru_w_in_2"][0], 1024 + 512 * s)
        cols(A["lru_w_in_2"][0], 512 * s)
        if s == 0:
            then()
    for h in range(2):
        cols(A["lru_w_out_2"][0], 512 * h)
    experts(0)
    P.sp_at, P.sp_done = [len(P.sp.items)], []
    P.loads.turn[id(ring)] += 3
    for s in range(2):
        for g in (1, 2, 0):
            cols(A["sc_w_in_2"][0], 1024 * g + 512 * s)
        if s == 0:
            P.sp_done.append(len(P.sp.items))
    for h in range(2):
        cols(A["sc_w_out_2"][0], 512 * h)
    experts(1)
    P.sp_at.append(len(P.sp.items))


def layer_norm(P, x, n, g, b, toks, gb_t):
    st = P.lnst.take()[1]
    st6, mv, rs, nm = st[:, 0:12], st[:, 12:14], st[0:n, 14:15], st[0:n, 15:16]
    w = [P.dv.op((lambda h: lambda e: e.bn_stats(st6[0:n, 6 * h:6 * h + 6], x[:, 512 * h:512 * h + 512]))(h), toks) for h in range(2)]
    a = P.dv.op(lambda e: e.bn_aggr(mv[0:n, :], st6[0:n, :]), w)
    r = P.ts(rs, mv[0:n, 1:2], 1.0, 1e-5, MUL, ADD, a)
    m = P.ts(nm, mv[0:n, 0:1], -1.0, None, MUL, None, a)
    r = P.ptt(rs, rs, P.cst("neghalf")[0:n, 0:1], ALU.pow, r)
    r = P.ptt(nm, nm, rs, MUL, m, r)
    s = P.act(x, x, ACT.Identity, r, scale=rs, bias=nm)

    def rest():
        a = P.tt(x, x, g[0:n, :], MUL, s, gb_t)
        return P.ptt(x, x, b[0:n, :], ADD, a)
    return rest


def turn_tile(P, banks, hT, cols, x, n, w):
    out = []
    if n < 128:
        k, bank, free = banks.take()
        p = P.tr([(bank[:, n * c:n * c + n], x[:, 128 * c:128 * c + 128]) for c in range(8)], w, free)
        out.append(P.cp(hT[:, :, cols], three(bank[:, 0:8 * n], 8), p))
        banks.free[k] = out[-1]
        return out
    for g in range(2):
        k, bank, free = banks.take()
        p = P.tr([(bank[:, 128 * c:128 * c + 128], x[:, 512 * g + 128 * c:512 * g + 128 * c + 128]) for c in range(4)], w, free)
        out.append((P.acp if g else P.cp)(hT[:, 4 * g:4 * g + 4, cols], three(bank[:, :], 4), p))
        banks.free[k] = out[-1]
    return out


class Places:

    def __init__(self, P, lo):
        self.a, self.b, self.c, self.hi = lo, lo + 8 * 528, lo + 16 * 528, P.top


def block2(P, x2, x2_t):
    A, nc = P.A, P.nc
    R = P.region(6 * SLOT + 4096, P.top)
    meta = R.take(1024)
    before = [q.last() for q in (P.pe, P.ac, P.dv, P.po)]
    banks = Slots(P.ps)
    banks.free = [before] * 8
    stat = R.take(96)
    P.lnst = Slots([stat[:, 16 * k:16 * k + 16] for k in range(5)])
    P.last_cell = stat[0:1, 95:96]
    P.gsem, P.gcount = [P.sem("gather") for _ in range(2)], [0] * 2
    P.ysem, P.ycount = [P.sem("ystore") for _ in range(3)], [0] * 3
    P.bsem = [DmaSem(P.sem("back")) for _ in range(10)]
    rw = [three(R.take(288), 8) for _ in range(2)]
    keep = dict(idx=R.take(NTAB).bitcast(I32), ovi=R.take(32).bitcast(I32),
                pos=R.take(16).bitcast(I32), gates=R.take(16))
    at = Places(P, R.o)
    hD, yD, zr = P.hD, P.yD, P.zr
    gw = [three(P.big[:, at.c + 1024 * i:at.c + 1024 * i + 1024], 8) for i in range(2)]
    soon = []

    def small():
        soon.append(P.load(P.sp, meta[0:16, :], A["meta_tokens_2"], before))
        soon.append([P.load(P.sp, gw[i], A["lru_gates"][i], before) for i in range(2)])
        soon.append([P.load(P.sp, rw[l], A["router"][l].rearrange("(c p) n -> p c n", p=128), before) for l in range(2)])

    plan_block2(P, small)
    mt, gt, rw_t = soon

    RA, RB, R = P.region(at.a, at.b), P.region(at.b, at.c), P.region(at.c, at.hi)
    hT = RA.take(8 * 528).rearrange("p (a b) -> p a b", a=8)
    z = RB.take(8 * 528).rearrange("p (a b) -> p a b", a=8)
    R.take(2048)
    sp4 = R.take(8)
    hb = R.take(16)
    tmp8 = [R.take(8) for _ in range(5)]
    ux = Slots([R.take(532) for _ in range(2)])
    tb = Slots([[R.take(528) for _ in range(6)] for _ in range(2)])
    lam = P.vec("lru_lambda_2", 0, 8)
    u, d, e_, m, f = tmp8
    a = P.ts(u, lam, -1.0, None, MUL, None, before)
    a = P.tt(m, lam, u, MAX, a)
    a = P.act(e_, m, ACT.Exp, a, scale=-1.0)
    b = P.ts(d, e_, 1.0, None, ADD, None, a)
    c = P.act(f, d, ACT.Ln, b)
    b = P.ts(d, d, -1.0, None, ADD, None, c)
    c2 = P.ts(m, d, 0.0, None, ISEQ, None, b)
    c3 = P.tt(d, d, m, ADD, c2)
    c3 = P.recip(d, d, c3)
    c3 = P.tt(f, f, e_, MUL, c3)
    c3 = P.tt(f, f, d, MUL, c3)
    c2 = P.tt(m, m, e_, MUL, c3)
    c3 = P.tt(f, f, m, ADD, c2)
    c3 = P.stt(sp4, u, 0.0, f, MAX, ADD, c3)
    sp_t = P.ts(sp4, sp4, -2.0, None, MUL, None, c3)
    h0 = P.ts(hb[:, 0:8], P.vec("lru_b_a_2", 0, 8), 0.5, None, MUL, None, before)
    h1 = P.ts(hb[:, 8:16], P.vec("lru_b_i_2", 0, 8), 0.5, None, MUL, None)
    h_t = turn_tile(P, banks, hT, slice(0, 16), meta[0:16, :], 16, [mt, before])
    for t in range(4):
        h_t += turn_tile(P, banks, hT, slice(16 + 128 * t, 144 + 128 * t), x2[:, t, :], 128, x2_t[t])
    zp = [P.dv.op((lambda x: lambda e: e.memset(x[:, 0:3], 0.0))(x)) for x in ux.items]
    N2 = 264

    def wide(job, m, rhs, w):
        got = []
        for hf in range(2):
            k, bank, free = banks.take()
            p = P.mm([(bank[:, 0:N2], job[:, c, 128 * m:128 * m + 128], rhs[:, c, N2 * hf:N2 * hf + N2], c == 0, c == 7) for c in range(8)], free, w)
            got.append((k, bank, p))
        return got

    z_t = []
    for s in range(2):
        jx, jy = P.loads.take(), P.loads.take()
        for mm_ in range(4):
            c = 4 * s + mm_
            ku, u_, ufree = ux.take()
            kt, (xc, th, q, it, hs, ge), tfree = tb.take()
            ev = []
            for hf, (k, bank, p) in enumerate(wide(jx.ap, mm_, hT, [jx.tok, h_t])):
                ev.append(P.acp(u_[:, 3 + N2 * hf:3 + N2 * hf + N2], bank[:, 0:N2], p, ufree))
                banks.free[k] = ev[-1]
                px = p
            w4 = P.vec("lru_conv_w_2", 0, 32)
            a = P.ts(xc, u_[:, 0:528], w4[:, c:c + 1], P.vec("lru_conv_b_2", c), MUL, ADD, ev, zp, tfree)
            for j in range(1, 4):
                a = P.stt(xc, u_[:, j:j + 528], w4[:, 8 * j + c:8 * j + c + 1], xc, MUL, ADD, a)
            ux.free[ku] = a
            ys = []
            for hf, (k, bank, p) in enumerate(wide(jy.ap, mm_, hT, [jy.tok])):
                ys.append(P.act(ge[:, N2 * hf:N2 * hf + N2], bank[:, 0:N2], ACT.Gelu_apprx_tanh, p, tfree))
                banks.free[k] = ys[-1]
                py = p
            rt, gt2 = [], []
            for g, dst, lst in ((0, th, rt), (1, it, gt2)):
                for hf in range(2):
                    k, bank, free = banks.take()
                    p = P.mm([(bank[:, 0:N2], gw[g][:, c, :], xc[:, N2 * hf:N2 * hf + N2], True, True)], a, free, gt[g])
                    lst.append(P.act(dst[:, N2 * hf:N2 * hf + N2], bank[:, 0:N2], ACT.Tanh, p, h0, h1, tfree, scale=0.5, bias=hb[:, 8 * g + c:8 * g + c + 1]))
                    banks.free[k] = lst[-1]
            t = P.act(th, th, ACT.Tanh, rt, sp_t, scale=sp4[:, c:c + 1], bias=sp4[:, c:c + 1])
            b = P.ts(q, th, -1.0, 1.0, MUL, ADD, t, tfree)
            b = P.recip(q, q, b)
            sq = P.act(hs, th, ACT.Sqrt, t, tfree, scale=-1.0)
            x = P.stt(it, it, 1.0, xc, ADD, MUL, gt2)
            x = P.tt(it, it, q, MUL, x, b)
            x = P.tt(it, it, hs, MUL, x, sq)
            y = P.stt(th, th, 1.0, q, ADD, MUL, b, sq)
            v = P.dv.op((lambda hs, th, it: lambda e: e.tensor_tensor_scan(hs, th, it, 0.0, MUL, ADD))(hs, th, it), x, y)
            v = P.tt(z[:, c, :], hs, ge, MUL, v, ys)
            tb.free[kt] = v
            z_t.append(v)
        jx.release, jy.release = [px], [py]

    def residual(z, z_t, tiles, x, ready, then):
        jobs = [P.loads.take(), P.loads.take()]
        late = None
        for i, (x, n, c0) in enumerate(tiles):
            got, w = [], []
            for h in range(2):
                k, bank, free = banks.take()
                p = P.mm([(bank[0:n, :], z[:, c, c0:c0 + n], jobs[h].ap[:, c, :], c == 0, c == 7) for c in range(8)], free, z_t, jobs[h].tok)
                got.append((k, bank, p))
                jobs[h].release = [p]
            if late:
                then(*late)
            for h, (k, bank, p) in enumerate(got):
                xs = x[:, 512 * h:512 * h + 512]
                w.append(P.stt(xs, xs, ALPHA, bank[0:n, :], MUL, ADD, p))
                banks.free[k] = w[-1]
            late = (i, layer_norm(P, x, n, ready[0], ready[1], w, ready[2])())
        then(*late)

    def rows(l, lo, n, *w):
        g, b = P.big[:, lo:lo + 1024], P.big[:, lo + 1024:lo + 2048]
        return g, b, [P.row_load(g, A["ln_g_2"][l, n], *w), P.row_load(b, A["ln_b_2"][l, n], *w)]

    tiles = [(meta[0:16, :], 16, 0)] + [(x2[:, t, :], 128, 16 + 128 * t) for t in range(4)]
    moe = Moe(P, 0, [(x2[:, t, :], 128) for t in range(4)] + [(meta[0:16, :], 16)], banks, at, keep, hD, yD, zr, rw[0], rw_t[0], rows)
    residual(z, z_t, tiles, x2, rows(0, at.a, 0, [px, py]), lambda i, tok: moe.enter((i + 4) % 5, tok))
    hT = P.big[:, at.a:at.a + 8 * 514].rearrange("p (a b) -> p a b", a=8)
    h_t = []

    def leave(t, tok):
        if t == 3:
            k, bank, free = banks.take()
            p = P.tr([(bank[:, 16 * c:16 * c + 16], meta[0:16, 128 * c:128 * c + 128]) for c in range(8)], h_t_meta[0], free)
            h_t.append(P.cp(hT[:, :, 0:2], three(bank[:, 0:128], 8)[:, :, 14:16], p))
            banks.free[k] = h_t[-1]
        h_t.extend(turn_tile(P, banks, hT, slice(2 + 128 * t, 130 + 128 * t), x2[:, t, :], 128, tok))

    h_t_meta = []
    w = moe.run([4, 0, 1, 2, 3], lambda t, tok: h_t_meta.append(tok) if t == 4 else leave(t, tok))
    RB, R = P.region(at.b, at.c), P.region(at.c, at.hi)
    z = three(RB.take(4096), 8)
    cg = Slots([R.take(514) for _ in range(2)])
    zz = Slots([R.take(514) for _ in range(2)])
    zc = Slots([R.take(512) for _ in range(2)])
    for s in (cg, zz, zc):
        s.free = [w] * 2
    w3 = P.vec("sc_conv_w_2", 0, 24)
    z_t = []
    N2 = 257
    for s in range(2):
        jc, jv, jb = P.loads.take(), P.loads.take(), P.loads.take()
        for mm_ in range(4):
            c = 4 * s + mm_
            kc, cgb, cfree = cg.take()
            kz, zzb, zfree = zz.take()
            ko, zcb, ofree = zc.take()
            parts = []
            for job in (jc, jv):
                for hf in range(2):
                    k, bank, free = banks.take()
                    p = P.mm([(bank[:, 0:N2], job.ap[:, i, 128 * mm_:128 * mm_ + 128], hT[:, i, N2 * hf:N2 * hf + N2], i == 0, i == 7)
                              for i in range(8)], free, h_t, job.tok)
                    parts.append((k, bank, p))
                job.release = [p]
            zt = []
            for hf in range(2):
                k, bank, p = parts[hf]
                a = P.acp(cgb[:, N2 * hf:N2 * hf + N2], bank[:, 0:N2], p, cfree)
                banks.free[k] = a
                k, bank, p = parts[2 + hf]
                zt.append(P.tt(zzb[:, N2 * hf:N2 * hf + N2], cgb[:, N2 * hf:N2 * hf + N2], bank[:, 0:N2], MUL, a, p, zfree))
                banks.free[k] = zt[-1]
            cg.free[kc] = zt
            a = P.ts(zcb, zzb[:, 0:512], w3[:, c:c + 1], None, MUL, None, zt, ofree)
            for j in (1, 2):
                a = P.stt(zcb, zzb[:, j:j + 512], w3[:, 8 * j + c:8 * j + c + 1], zcb, MUL, ADD, a)
            zz.free[kz] = a
            k, bank, free = banks.take()
            p = P.mm([(bank[:, :], jb.ap[:, i, 128 * mm_:128 * mm_ + 128], hT[:, i, 2:514], i == 0, i == 7) for i in range(8)], free, jb.tok)
            v = P.tt(z[:, c, :], zcb, bank[:, :], MUL, a, p, w)
            jb.release = [p]
            banks.free[k] = zc.free[ko] = v
            z_t.append(v)
    tiles = [(x2[:, t, :], 128, 128 * t) for t in range(4)]
    moe = Moe(P, 1, [(x2[:, t, :], 128) for t in range(4)], banks, at, keep, hD, yD, zr, rw[1], rw_t[1], rows)
    residual(z, z_t, tiles, x2, rows(1, at.a, 0, p), moe.enter)
    s = DmaSem(P.sem("out"))

    def store(t, tok):
        s.add()
        P.ac.dma(lambda e: e.dma_start(P.out[0, 128 * t:128 * t + 128, :], x2[:, t, :]), s.sem, tok)

    w = moe.run([0, 1, 2, 3], store)
    P.ac.wait((s.sem, s.n))


class Moe:

    def __init__(self, P, l, tiles, banks, at, keep, hD, yD, zr, rw, rw_t, rows):
        self.P, self.l, self.tiles, self.banks, self.at, self.keep = P, l, tiles, banks, at, keep
        self.hD, self.yD, self.zr, self.rw, self.rw_t, self.rows = hD, yD, zr, rw, rw_t, rows
        nt = self.nt = len(tiles)
        R = P.region(at.c, at.hi - 2048)
        self.hT = R.take(8 * 528).rearrange("p (a b) -> p a b", a=8)
        self.buf_end = R.o
        self.lg = three(R.take(nt * 36), nt)
        self.temps = R
        self.hsem = DmaSem(P.sem("rows"))
        self.toks, self.lg_t, self.scaled = [], [], {}
        self.zl = self.turned = None

    def enter(self, t, tok):
        P, banks, hT = self.P, self.banks, self.hT
        x, n = self.tiles[t]
        self.toks.append(tok)
        if self.zl is None:
            self.zl = P.dv.op(lambda e: e.memset(self.lg, 0.0), tok)
        self.hw = self.hsem.add()
        P.ac.dma(lambda e: e.dma_start(self.hD[128 * t:128 * t + n, :], x), self.hsem.sem, tok)
        self.logits()
        self.turned = (t, n, turn_tile(P, banks, hT, slice(128 * t, 128 * t + n), x, n, tok))

    def logits(self):
        if self.turned is None:
            return
        P, banks, hT = self.P, self.banks, self.hT
        t, n, h_t = self.turned
        k, bank, free = banks.take()
        p = P.mm([(bank[0:n, 0:36], hT[:, c, 128 * t:128 * t + n], self.rw[:, c, :], c == 0, c == 7) for c in range(8)], h_t, self.rw_t, free)
        o, _ = RAT["moe_bias"]
        self.lg_t.append(P.tt(self.lg[0:n, t, :], bank[0:n, 0:36], P.row_sb[0:n, o + 36 * self.l:o + 36 * self.l + 36], ADD, p, self.zl))
        banks.free[k] = self.lg_t[-1]

    def route(self):
        P, banks, nt, R = self.P, self.banks, self.nt, self.temps
        idx, ovi, pos_i, gates = (self.keep[k] for k in ("idx", "ovi", "pos", "gates"))
        self.logits()
        n2 = 2 * nt
        sm = [R.take(n2) for _ in range(12)]
        small = [R.take(nt) for _ in range(6)]
        W4 = [three(R.take(nt * 4), nt) for _ in range(3)]
        elm, tmp, M = (three(R.take(nt * 32), nt) for _ in range(3))
        E = R.take((nt + 1) * 32)
        OH = R.take(n2 * 32)
        prod = R.take(n2 * 32)
        cb = three(R.take(nt * 32), nt)
        e32 = [R.take(32) for _ in range(5)]
        big = R.take(NOVF * 32)
        oh4 = OH.rearrange("p (t j e) -> p t j e", t=nt, j=2)
        oh3 = three(OH, n2)
        pr4, pr3 = prod.rearrange("p (t j e) -> p t j e", t=nt, j=2), three(prod, n2)
        gl, el = self.lg[:, :, 0:4], self.lg[:, :, 4:36]
        gid = P.cst("gid")[:, 0:4].unsqueeze(1).to_broadcast([128, nt, 4])
        eid = P.cst("eid").unsqueeze(1).to_broadcast([128, nt, 32])

        def bc(x, n):
            return x.unsqueeze(len(x.shape)).to_broadcast(list(x.shape) + [n])

        def first_max(v, val, ids, tmp, at_, hot, w):
            n = v.shape[2]
            a = P.red(val, v, MAX, w)
            a = P.tt(tmp, v, bc(val, n), ISEQ, a)
            a = P.tt(tmp, tmp, ids, MUL, a)
            a = P.red(at_, tmp, MIN, a)
            return P.tt(hot, ids, bc(at_, n), ISEQ, a)

        gmax, gat, v1, v2, den, ex = small
        ei2 = three(sm[0], nt)
        a = first_max(gl, gmax, gid, W4[0], gat, W4[1], self.lg_t)
        a = P.ts(W4[1], W4[1], 1.0, 1e30, SUB, MUL, a)
        a = P.tt(elm.rearrange("p t (g e) -> p t g e", g=4), el.rearrange("p t (g e) -> p t g e", g=4), bc(W4[1], 8), ADD, a)
        a = first_max(elm, v1, eid, tmp, ei2[:, :, 0], oh4[:, :, 0, :], a)
        a = P.stt(elm, oh4[:, :, 0, :], -2e30, elm, MUL, ADD, a)
        a = first_max(elm, v2, eid, tmp, ei2[:, :, 1], oh4[:, :, 1, :], a)
        m = P.tt(M, oh4[:, :, 0, :], oh4[:, :, 1, :], ADD, a)
        if nt == 5:
            m = P.tt(M[:, 4, :], M[:, 4, :], P.cst("first16"), MUL, m)
        E3 = three(E, nt + 1)
        e = P.dv.op(lambda en: en.memset(E3[:, 0, :], 0.0))
        for t in range(nt):
            e = P.tt(E3[:, t + 1, :], E3[:, t, :], M[:, t, :], ADD, m, e)
        k, bank, free = banks.take()
        strict, ones = P.cst("strict"), P.cst("ones")
        flat = M.rearrange("p t e -> p (t e)")
        p = P.mm([(bank[:, 0:32 * nt], strict, flat, True, False), (bank[:, 0:32 * nt], ones, E[:, 0:32 * nt], False, True),
                  (bank[:, 256:288], ones, E[:, 32 * nt:32 * nt + 32], True, True)], m, e, free)
        cnt, nb, inc, exc, fl = e32
        cn_t = P.cp(cnt, bank[:, 256:288], p)
        cb_t = P.cp(cb, three(bank[:, 0:32 * nt], nt), p)
        banks.free[k] = cb_t
        c8 = big[:, 0:256].rearrange("p (e q) -> p e q", q=8)
        a = P.tt(c8, bc(cnt, 8), P.cst("thr").unsqueeze(1).to_broadcast([128, 32, 8]), ISGT, cn_t)
        fl_t = P.cp(fl, c8[:, :, 0], a)
        nb_t = P.red(nb, c8[:, :, 1:8], ADD, a)
        b = P.dv.op(lambda en: en.tensor_tensor_scan(inc, nb, P.cst("zero")[:, 0:32], 0.0, ADD, ADD), nb_t)
        x_t = P.tt(exc, inc, nb, SUB, b)
        rank, ob, par, blk, pos, first, second, colm, p128, ad, rk = sm[1:12]
        a = P.tt(pr4, oh4, cb.unsqueeze(2).to_broadcast([128, nt, 2, 32]), MUL, cb_t)
        r_t = P.red(rank, pr3, ADD, a)
        a = P.tt(pr3, oh3, exc.unsqueeze(1).to_broadcast([128, n2, 32]), MUL, x_t, r_t)
        o_t = P.red(ob, pr3, ADD, a)
        ei = sm[0]
        a = P.ts(ei, ei, 100.0, None, ADD, None, r_t)
        p_t = P.ts(par, ei, 16.0, None, ISGE, None, a)
        r8 = three(big[:, 256:256 + 8 * n2], n2)
        b = P.tt(r8, bc(rank, 8), P.cst("thr").unsqueeze(1).to_broadcast([128, n2, 8]), ISGE, r_t)
        b = P.red(blk, r8, ADD, b)
        pos_t = P.stt(pos, blk, -64.0, rank, MUL, ADD, b)
        f_t = P.ts(first, blk, 0.0, None, ISEQ, None, b)
        s_t = P.ts(second, blk, 1.0, None, ISEQ, None, b)
        a = P.stt(ad, blk, 46.0, ob, ADD, ADD, b, o_t)
        a = P.stt(colm, ei, 16.0, ad, ADD, SUB, a)
        a = P.tt(colm, colm, second, MUL, a, s_t)
        blk_t = P.tt(ad, ad, colm, ADD, a)
        a = P.stt(colm, par, -16.0, ei, MUL, ADD, p_t, blk_t)
        a = P.tt(colm, colm, ad, SUB, a)
        a = P.tt(colm, colm, first, MUL, a, f_t)
        col_t = P.tt(colm, colm, ad, ADD, a)
        a = P.tt(p128, par, first, MUL, p_t, f_t)
        p_t = P.stt(p128, p128, 64.0, pos, MUL, ADD, a, pos_t)
        RP = P.region(self.at.a, self.at.c)
        ph = three(RP.take(n2 * 128), n2)
        ch = three(RP.take(n2 * 64), n2)
        iota = P.cst("iota")
        free_z = self.toks
        a = P.tt(ch, iota[:, 0:64].unsqueeze(1).to_broadcast([128, n2, 64]), bc(colm, 64), ISEQ, col_t, free_z)
        tk = P.cst("tok")[:, 0:nt].unsqueeze(2).unsqueeze(3).to_broadcast([128, nt, 2, 64])
        c4 = ch.rearrange("p (t j) c -> p t j c", j=2)
        c_t = P.tt(c4, c4, tk, MUL, a)
        ph_t = P.tt(ph, iota.unsqueeze(1).to_broadcast([128, n2, 128]), bc(p128, 128), ISEQ, p_t, free_z)
        k, bank, free = banks.take()
        p = P.mm([(bank[:, 0:64], ph[:, q, :], ch[:, q, :], q == 0, q == n2 - 1) for q in range(n2)], ph_t, c_t, free)
        self.idx_t = P.ts(idx, bank[:, 0:64], float(T + 16), None, ADD, None, p)
        banks.free[k] = self.idx_t
        a = P.tt(fl, fl, P.cst("bit"), MUL, fl_t)
        a = P.red(e32[0][:, 0:2], fl.rearrange("p (a b) -> p a b", a=2), ADD, a)
        self.flag_t = P.cp(ovi[:, 17:19], e32[0][:, 0:2], a)
        o3 = three(big, NOVF)
        d = P.tt(o3, inc.unsqueeze(1).to_broadcast([128, NOVF, 32]), iota[:, 0:NOVF].unsqueeze(2).to_broadcast([128, NOVF, 32]), ALU.is_le, b, r_t, pos_t)
        d = P.red(e32[1][:, 0:NOVF], o3, ADD, d)
        d = P.ts(ovi[:, 0:NOVF], e32[1][:, 0:NOVF], 31.0, None, MIN, None, d)
        self.ov_t = P.cp(ovi[:, 16:17], inc[:, 31:32], d)
        a = P.ts(ad, ad, 16.0, None, ADD, None, col_t)
        b = P.tt(colm, ei, ad, SUB, a, c_t)
        b = P.tt(colm, colm, first, MUL, b)
        b = P.tt(colm, colm, ad, ADD, b)
        self.pos_t = P.stt(pos_i[:, 0:n2], colm, 64.0, pos, MUL, ADD, b)
        b = P.tt(W4[2], gl, bc(gmax, 4), SUB)
        b = P.act(W4[2], W4[2], ACT.Exp, b)
        d = P.tt(ex, v2, v1, SUB)
        d = P.act(ex, ex, ACT.Exp, d)
        b = P.red(den, W4[2], ADD, b)
        b = P.stt(den, ex, 1.0, den, ADD, MUL, b, d)
        g3 = gates[:, 0:n2].rearrange("p (t j) -> p t j", j=2)
        b = P.recip(g3[:, :, 0], den, b)
        self.g_t = P.tt(g3[:, :, 1], g3[:, :, 0], ex, MUL, b)
        for t, (x, n) in enumerate(self.tiles):
            self.scaled[t] = P.ts(x, x, ALPHA, None, MUL, None, self.hw)

    def run(self, last, then):
        P, banks, l, at = self.P, self.banks, self.l, self.at
        A, yD, hD = P.A, self.yD, self.hD
        self.route()
        idx, ovi, pos_i, gates = (self.keep[k] for k in ("idx", "ovi", "pos", "gates"))
        R = P.region(at.a, self.buf_end)
        xg = Slots([R.take(1024) for _ in range(2)])
        xT = Slots([three(R.take(1024), 8) for _ in range(2)])
        hs = Slots([[R.take(256) for _ in range(3)] for _ in range(4)])
        yb = Slots([R.take(512) for _ in range(3)])
        xg2 = Slots([R.take(1024) for _ in range(2)])
        xT2 = Slots([three(R.take(512), 8)])
        routed = [self.idx_t, self.lg_t]
        for s in (hs, yb, xT, xT2):
            s.free = [routed] * len(s.items)
        ln2 = self.rows(l, at.hi - 2048, 1, routed)
        P.ac.wait(self.zr)
        P.po.wait(self.hw, self.zr, routed)
        flags = {}
        for name, q in (("pe", P.pe), ("ac", P.ac), ("dv", P.dv), ("po", P.po)):
            q.items.append(("tok", self.flag_t))
            flags[name] = [{}, {}]
            for k in range(2):
                q.items.append(("count", flags[name][k], ovi[0:1, 17 + k:18 + k], 65535))
        mains = (("pe", P.pe), ("ac", P.ac), ("dv", P.dv))

        def second(name, e):
            regs = flags[name][e // 16]
            return lambda en: regs["v"] & (1 << (e % 16))

        gsem, gcount, ysem, ycount = P.gsem, P.gcount, P.ysem, P.ycount

        def gather(buf, n, col, sem, *w):
            P.po.dma(lambda e: e.indirect_dma_start(out=buf[0:n, :], out_offset=None, in_=hD,
                                                    in_offset=bass.IndirectOffsetOnAxis(ap=idx[0:n, col:col + 1], axis=0),
                                                    bounds_check=T + 15, oob_is_err=False), sem, *w)

        def turn(xb, xt, n, w, wx):
            out = []
            for g in range(2):
                k, bank, free = banks.take()
                p = P.tr([(bank[:, n * c:n * c + n], xb[0:n, 512 * g + 128 * c:512 * g + 128 * c + 128]) for c in range(4)], w, free)
                dst, src = xt[:, 4 * g:4 * g + 4, 0:n], three(bank[:, 0:4 * n], 4)
                out.append(P.acp(dst, src, p, wx) if g else P.cp(dst, src, p, wx))
                banks.free[k] = out[-1]
            return out, p

        def up(gu, xt, x0, w):
            k, bank, free = banks.take()
            grp = []
            for c in range(8):
                for hf in range(2):
                    grp.append((bank[64 * hf:64 * hf + 64, :], xt[:, c, x0:x0 + 64], gu[:, :, 512 * c + 256 * hf:512 * c + 256 * hf + 256], c == 0, c == 7))
            p = P.mm(grp, free, w)
            kh, (s, h, ht), hfree = hs.take()
            a = P.act(s, bank[:, 0:256], ACT.Silu, p, hfree)
            b = P.tt(h, s, bank[:, 256:512], MUL, a)
            banks.free[k] = b
            return p, kh, h, ht, b

        def down(kh, h, ht, b, dw, w):
            k, bank, free = banks.take()
            p = P.tr([(bank[:, 128 * j:128 * j + 128], h[:, 128 * j:128 * j + 128]) for j in range(2)], b, free)
            e = P.cp(ht, bank[:, 0:256], p)
            banks.free[k] = e
            k, bank, free = banks.take()
            grp = []
            for c in range(4):
                lhs = ht[:, 128 * (c % 2) + 64 * (c // 2):128 * (c % 2) + 64 * (c // 2) + 64]
                for hf in range(2):
                    grp.append((bank[64 * hf:64 * hf + 64, :], lhs, dw[:, c, 512 * hf:512 * hf + 512], c == 0, c == 3))
            q = P.mm(grp, e, free, w)
            hs.free[kh] = q
            ky, y, yfree = yb.take()
            a = P.acp(y, bank[:, :], q, yfree)
            banks.free[k] = a
            return q, a, ky, y

        def store(blk, a, ky, y, sem):
            for hf in range(2):
                P.ac.dma((lambda hf: lambda en: en.dma_start(yD[64 * blk:64 * blk + 64, 512 * hf:512 * hf + 512], y[64 * hf:64 * hf + 64, :]))(hf), sem, a)

        def stored(blk, a, ky, y):
            store(blk, a, ky, y, ysem[ky])
            ycount[ky] += 32
            yb.free[ky] = (ysem[ky], ycount[ky])

        gath, gath2 = {}, {}

        def start(c):
            k, xb, free = xg.take()
            gather(xb, 128, c, gsem[k], free)
            gcount[k] += 16
            gath[c] = (k, xb, (gsem[k], gcount[k]))

        def start2(i):
            e = order(i)
            k, xb, free = xg2.take()
            sem = P.sem("second")
            P.po.open()
            gather(xb, 64, 16 + e, sem, free)
            gath2[i] = (k, xb, P.po.said((sem, 16)))
            P.po.close(second("po", e))

        def finish(i, jd, r, r2):
            e = order(i)
            q, a, ky, y = down(*r[1:], jd.ap, jd.tok)
            stored(e, a, ky, y)
            for _, qu in mains:
                qu.open()
            q2, a, ky, y = down(*r2[1:], jd.ap, jd.tok)
            stored(NEXP + e, a, ky, y)
            for name, qu in mains:
                qu.close(second(name, e), [(ysem[ky], 32)] if name == "ac" else [])
            jd.release = [q, q2]

        start(0)
        start(1)
        start2(0)
        start2(1)
        pend = None
        for i in range(NEXP):
            e = order(i)
            if i % 2 == 0:
                k, xb, gtok = gath[i // 2]
                kx, xt, xfree = xT.take()
                x_t, xg.free[k] = turn(xb, xt, 128, gtok, xfree)
                if i // 2 + 2 < 16:
                    start(i // 2 + 2)
            jg, ju, jd = P.loads.take(), P.loads.take(), P.loads.take()
            s0 = P.ring.index(jg.slot)
            gu = P.big[:, SLOT * s0:SLOT * s0 + 2 * SLOT].rearrange("p (s n) -> p s n", s=2)
            r = up(gu, xt, 64 * (i % 2), [x_t, jg.tok, ju.tok])
            xT.free[kx] = r[0]
            for _, qu in mains:
                qu.open()
            k, xb, gtok = gath2[i]
            kx2, xt2, xfree = xT2.take()
            x2_t, xg2.free[k] = turn(xb, xt2, 64, gtok, xfree)
            r2 = up(gu, xt2, 0, [x2_t, jg.tok, ju.tok])
            xT2.free[kx2] = r2[0]
            for name, qu in mains:
                qu.close(second(name, e))
            if i + 2 < NEXP:
                start2(i + 2)
            jg.release = ju.release = [r[0], r2[0]]
            if pend is not None:
                finish(*pend)
            pend = (i, jd, r, r2)
        finish(*pend)
        ydone = [(ysem[k], ycount[k]) for k in range(3)]
        main_done = [x.last() for x in (P.pe, P.ac, P.dv, P.po)]

        real = (P.pe, P.ac, P.dv, P.po)
        P.pe, P.ac, P.dv, P.po = (Queue(P.sem("ovf")) for _ in range(4))
        osp = Queue(P.sem("ovf"))
        queues = {"pe": (real[0], P.pe), "ac": (real[1], P.ac), "dv": (real[2], P.dv), "po": (real[3], P.po), "sp": (None, osp)}
        marks = {n: [0] for n in queues}
        for s in (banks, hs, yb, xT):
            s.free = [main_done] * len(s.items)
        yb.free = [ydone] * len(yb.items)
        wsem = [P.sem("ow") for _ in range(2)]
        gs, ys = [P.sem("ogather") for _ in range(2)], P.sem("oystore")
        gu = P.big[:, 0:2 * SLOT].rearrange("p (s n) -> p s n", s=2)
        dw = three(P.big[:, 2 * SLOT:3 * SLOT], 4)
        gu_free = dw_free = [job.release for job in P.loads.jobs[P.loads.at - 6:P.loads.at - 3]]
        yn = 0
        for i in range(NOVF):
            regs = {}
            osp.items.append(("read", regs, ovi[0:1, i:i + 1], NEXP - 1))
            for s, name in enumerate(("moe_w_gate_2", "moe_w_up_2")):
                osp.dma((lambda s, w, regs: lambda e: e.dma_start(three(gu[:, s, :], 8), w[l, bass.ds(regs["v"], 1)].rearrange("o (c p) n -> p (o c) n", p=128)))(s, A[name], regs),
                        wsem[0], gu_free)
            osp.dma((lambda w, regs: lambda e: e.dma_start(dw, w[l, bass.ds(regs["v"], 1)].rearrange("o (c p) n -> p (o c) n", p=128)))(A["moe_w_down_2"], regs),
                    wsem[1], dw_free)
            k, xb, free = xg.take()
            gather(xb, 64, 48 + i, gs[k], free)
            kx, xt, xfree = xT.take()
            x_t, xg.free[k] = turn(xb, xt, 64, (gs[k], 16 * (i // 2 + 1)), xfree)
            r = up(gu, xt, 0, [x_t, (wsem[0], 32 * (i + 1))])
            xT.free[kx] = gu_free = [r[0]]
            q, a, ky, y = down(*r[1:], dw, (wsem[1], 16 * (i + 1)))
            dw_free = [q]
            store(2 * NEXP + i, a, ky, y, ys)
            yn += 32
            P.ac.wait((ys, yn))
            yb.free[ky] = (ys, yn)
            for n, (_, q) in queues.items():
                marks[n].append(len(q.items))
        P.pe, P.ac, P.dv, P.po = real
        sp_sec = None
        for n, (main, q) in queues.items():
            count = {}
            sec = [("tok", self.ov_t), ("count", count, ovi[0:1, 16:17], NOVF)]
            for i in range(NOVF):
                sec.append(("when", (lambda count, i: lambda e: count["v"] > i)(count, i), q.items[marks[n][i]:marks[n][i + 1]]))
            if main is None:
                P.sp_sections.append(sec)
            else:
                main.items += sec
                main.seen = {}
        done = P.act(P.last_cell, P.last_cell, ACT.Copy, main_done, ydone)
        for q in (P.pe, P.dv, P.po):
            q.wait(done)
        banks.free = [done] * 8

        Rt = P.region(at.b, at.hi - 2048)
        rows_in = {}
        for t in last:
            n = self.tiles[t][1]
            for j in range(2):
                buf = Rt.take(1024)
                s = P.bsem[len(rows_in)]
                tok = s.add()
                P.po.dma((lambda buf, n, j, t: lambda e: e.indirect_dma_start(
                    out=buf[0:n, :], out_offset=None, in_=yD, in_offset=bass.IndirectOffsetOnAxis(ap=pos_i[0:n, 2 * t + j:2 * t + j + 1], axis=0),
                    bounds_check=64 * NBLK - 1, oob_is_err=False))(buf, n, j, t), s.sem, done, self.pos_t)
                rows_in[t, j] = (buf, tok)
        P.sp_ends.append(("wait", *tok))
        out = []
        started, ready = [], []
        for t in last + [None, None]:
            if t is not None:
                x, n = self.tiles[t]
                w = self.scaled[t]
                for j in range(2):
                    buf, tok = rows_in[t, j]
                    w = P.stt(x, buf[0:n, :], gates[0:n, 2 * t + j:2 * t + j + 1], x, MUL, ADD, w, tok, self.g_t)
                started.append((t, layer_norm(P, x, n, ln2[0], ln2[1], w, ln2[2])))
            if ready:
                then(*ready.pop())
            if started and (t is None or len(started) > 1):
                t0, rest = started.pop(0)
                ready.append((t0, rest()))
                out.append(ready[-1][1])
        if ready:
            then(*ready.pop())
        return out


def columns(a, n):
    return np.ascontiguousarray(a).reshape(-1, 128).T


def laid_out(inputs):
    x = {k: np.ascontiguousarray(v) for k, v in inputs.items()}
    vecs = np.concatenate([columns(x[k], n) for k, n in VECS], 1)
    x["moe_bias"] = np.concatenate([x["moe_b_group_2"], x["moe_b_expert_2"].reshape(2, NEXP)], 1)
    rows = np.concatenate([x[k].reshape(-1) for k, _ in ROWS])
    tables, _ = shape_tables()
    wa = np.zeros((2, 128, 8, 128), np.float32)
    for i, k in enumerate(("lru_w_a_2", "lru_w_i_2")):
        for h in range(16):
            wa[i, 64 * (h % 2):64 * (h % 2) + 64, h // 2, 64 * (h % 2):64 * (h % 2) + 64] = x[k][0, h]
    router = np.concatenate([x["moe_w_group_2"], x["moe_w_expert_2"]], 2)
    keep = ["x", "w_in", "rwkv_w_up", "rwkv_a_up", "rwkv_g_up", "w_branch", "w_out", "norm_mix_post", "norm_ffn_post",
            "ffn_w_gate", "ffn_w_up", "ffn_w_down", "meta_tokens_2", "lru_w_in_2", "lru_w_out_2", "sc_w_in_2", "sc_w_out_2",
            "moe_w_gate_2", "moe_w_up_2", "moe_w_down_2", "ln_g_2", "ln_b_2"]
    arrays = {k: x[k] for k in keep}
    arrays.update(vecs=np.ascontiguousarray(vecs), rows=np.ascontiguousarray(rows), tables=tables, lru_gates=wa,
                  router=np.ascontiguousarray(router))
    return arrays


def kernel(**inputs):
    import concourse.bacc as bacc
    from concourse.bass_utils import run_bass_kernel_spmd

    arrays = laid_out(inputs)
    _, cat = shape_tables()
    nc = bacc.Bacc("TRN2", target_bir_lowering=False, num_devices=1)
    aps = {k: nc.dram_tensor("in_" + k, a.shape, mybir.dt.from_np(a.dtype), kind="ExternalInput").ap() for k, a in arrays.items()}
    out = nc.dram_tensor("out_x", (1, T, D), F32, kind="ExternalOutput").ap()
    program(nc, aps, out, cat, arrays["tables"].shape[1])
    r = run_bass_kernel_spmd(nc, [{"in_" + k: a for k, a in arrays.items()}], core_ids=[0])
    return r.results[0]["out_x"]
```
